# Optimizing a Trainium2 kernel written in Bass

```python
import math
import jax, jax.numpy as jnp
from jax import lax
import numpy as np

D_MODEL = 1024
BATCH = 1
SEQ = 256
DEPTH = 1

MEM_LEN = 256
HEAD_DIM = 128
ATTN_HEADS = 6
ATTN_KV_HEADS = 2
ATTN_GROUP = ATTN_HEADS // ATTN_KV_HEADS
WINDOW = 128
BLOCK = 128
ROPE_DIM = HEAD_DIM // 4
ROPE_THETA = 500000.0
LRU_WIDTH = 768
LRU_BLOCKS = 6
LRU_BLOCK_W = LRU_WIDTH // LRU_BLOCKS
CONV_WIDTH = 4
CONV_LEFT = CONV_WIDTH // 2
LRU_C = 8.0
MEM_HEADS = 4
N_BRANCH = 3
PEER_HEADS = 8
PEER_KEYS = 128
PEER_EXPERTS = PEER_KEYS * PEER_KEYS
PEER_QDIM = 256
PEER_HALF = PEER_QDIM // 2
PEER_TOPK = 16
PEER_CHUNK = 128
EPS = 1e-6
NEG_INF = -1e30

ATTN_Q_W = ATTN_HEADS * HEAD_DIM
ATTN_KV_W = ATTN_KV_HEADS * HEAD_DIM
MEM_Q_W = MEM_HEADS * HEAD_DIM
GATE_W = N_BRANCH * D_MODEL
IN_W = ATTN_Q_W + 2 * ATTN_KV_W + 2 * LRU_WIDTH + MEM_Q_W + GATE_W


def rmsnorm(x, g):
    xf = x.astype(jnp.float32)
    y = xf * lax.rsqrt(jnp.mean(xf * xf, axis=-1, keepdims=True) + EPS) * g.astype(jnp.float32)
    return y.astype(x.dtype)

def partial_rope(t, positions):
    half = ROPE_DIM // 2
    inv_freq = ROPE_THETA ** (-jnp.arange(0, ROPE_DIM, 2, dtype=jnp.float32) / ROPE_DIM)
    ang = positions.astype(jnp.float32)[..., None] * inv_freq
    cos = jnp.cos(ang)[:, :, None, :]
    sin = jnp.sin(ang)[:, :, None, :]
    tr = t[..., :ROPE_DIM].astype(jnp.float32)
    t1, t2 = tr[..., :half], tr[..., half:]
    rot = jnp.concatenate([t1 * cos - t2 * sin, t2 * cos + t1 * sin], axis=-1)
    return jnp.concatenate([rot.astype(t.dtype), t[..., ROPE_DIM:]], axis=-1)

def band_blocks(t, nb):
    b = t.shape[0]
    tp = jnp.pad(t, ((0, 0), (BLOCK, BLOCK), (0, 0), (0, 0)))
    tp = tp.reshape(b, nb + 2, BLOCK, t.shape[2], t.shape[3])
    return jnp.concatenate([tp[:, :-2], tp[:, 1:-1], tp[:, 2:]], axis=2)

def windowed_gqa(q, k, v, sink):
    b, s = q.shape[0], q.shape[1]
    nb = s // BLOCK
    qb = q.reshape(b, nb, BLOCK, ATTN_KV_HEADS, ATTN_GROUP, HEAD_DIM)
    kb = band_blocks(k, nb)
    vb = band_blocks(v, nb)
    scores = jnp.einsum('bnqkgd,bnskd->bnkgqs', qb, kb).astype(jnp.float32) * (HEAD_DIM ** -0.5)
    blk = jnp.arange(nb, dtype=jnp.int32)[:, None]
    q_pos = blk * BLOCK + jnp.arange(BLOCK, dtype=jnp.int32)[None, :]
    k_pos = blk * BLOCK - BLOCK + jnp.arange(3 * BLOCK, dtype=jnp.int32)[None, :]
    valid = ((k_pos[:, None, :] >= 0) & (k_pos[:, None, :] < s)
             & (jnp.abs(k_pos[:, None, :] - q_pos[:, :, None]) <= WINDOW))
    scores = jnp.where(valid[None, :, None, None], scores, NEG_INF)
    sink_b = jnp.broadcast_to(sink.astype(jnp.float32).reshape(ATTN_KV_HEADS, ATTN_GROUP)[None, None, :, :, None, None],
                              scores.shape[:-1] + (1,))
    p = jax.nn.softmax(jnp.concatenate([scores, sink_b], axis=-1), axis=-1)[..., :-1]
    out = jnp.einsum('bnkgqs,bnskd->bnqkgd', p.astype(v.dtype), vb)
    return out.reshape(b, s, ATTN_Q_W)

def centred_depthwise_conv(t, w, bias):
    s = t.shape[1]
    tp = jnp.pad(t, ((0, 0), (CONV_LEFT, CONV_WIDTH - 1 - CONV_LEFT), (0, 0)))
    y = bias[None, None, :]
    for j in range(CONV_WIDTH):
        y = y + w[j][None, None, :] * tp[:, j:j + s]
    return y

def _lin_comb(c1, c2):
    a1, b1 = c1
    a2, b2 = c2
    return a1 * a2, a2 * b1 + b2

def bidir_rglru(xc, w_r, b_r, w_i, b_i, lam):
    b, s = xc.shape[0], xc.shape[1]
    xf = xc.astype(jnp.float32)
    xblk = xf.reshape(b, s, LRU_BLOCKS, LRU_BLOCK_W)
    r = jax.nn.sigmoid(jnp.einsum('bshc,dhce->dbshe', xblk, w_r.astype(jnp.float32)).reshape(2, b, s, LRU_WIDTH)
                       + b_r.astype(jnp.float32)[:, None, None, :])
    i = jax.nn.sigmoid(jnp.einsum('bshc,dhce->dbshe', xblk, w_i.astype(jnp.float32)).reshape(2, b, s, LRU_WIDTH)
                       + b_i.astype(jnp.float32)[:, None, None, :])
    log_a = -LRU_C * r * jax.nn.softplus(-lam.astype(jnp.float32))[:, None, None, :]
    a = jnp.exp(log_a)
    bx = jnp.sqrt(-jnp.expm1(2.0 * log_a)) * (i * xf[None])
    _, h_fwd = lax.associative_scan(_lin_comb, (a[0], bx[0]), axis=1)
    _, h_bwd = lax.associative_scan(_lin_comb, (a[1], bx[1]), axis=1, reverse=True)
    return (h_fwd + h_bwd).astype(xc.dtype)

def memory_cross_attention(q, k, v):
    scores = jnp.einsum('bshd,bmhd->bhsm', q, k).astype(jnp.float32) * (HEAD_DIM ** -0.5)
    p = jax.nn.softmax(scores, axis=-1)
    out = jnp.einsum('bhsm,bmhd->bshd', p.astype(v.dtype), v)
    return out.reshape(q.shape[0], q.shape[1], MEM_Q_W)

def peer_ffn(h, w_q, sub_keys, u_tab, v_tab):
    b, s, d = h.shape
    q = (h @ w_q).reshape(b, s, PEER_HEADS, 2, PEER_HALF)
    sc = jnp.einsum('bshpc,hpkc->bshpk', q, sub_keys).astype(jnp.float32)
    top_v, top_i = lax.top_k(sc, PEER_TOPK)
    cand_v = (top_v[..., 0, :, None] + top_v[..., 1, None, :]).reshape(b, s, PEER_HEADS, PEER_TOPK * PEER_TOPK)
    cand_i = (top_i[..., 0, :, None] * PEER_KEYS + top_i[..., 1, None, :]).reshape(b, s, PEER_HEADS, PEER_TOPK * PEER_TOPK)
    best_v, best_pos = lax.top_k(cand_v, PEER_TOPK)
    idx = jnp.take_along_axis(cand_i, best_pos, axis=-1)
    gate = jax.nn.softmax(best_v, axis=-1)
    n_tok = b * s
    n_chunk = n_tok // PEER_CHUNK
    hc = h.reshape(n_chunk, PEER_CHUNK, d)
    ic = idx.reshape(n_chunk, PEER_CHUNK, PEER_HEADS, PEER_TOPK)
    gc = gate.reshape(n_chunk, PEER_CHUNK, PEER_HEADS, PEER_TOPK)

    def expert_chunk(args):
        hx, ix, gx = args
        u = u_tab[ix]
        act = jax.nn.gelu(jnp.einsum('chkd,cd->chk', u, hx).astype(jnp.float32))
        vv = v_tab[ix]
        return jnp.einsum('chk,chkd->cd', (gx * act).astype(vv.dtype), vv)

    out = lax.map(expert_chunk, (hc, ic, gc))
    return out.reshape(b, s, d)

def first_inputs(seed: int = 0) -> dict:
    key = jax.random.key(seed)
    ks = jax.random.split(key, 32)
    f32 = jnp.float32
    nrm = lambda k, shape, scale: jax.random.normal(k, shape, f32) * scale
    u = jax.random.uniform(ks[12], (DEPTH, 2, LRU_WIDTH), f32, 0.9, 0.999)
    a0 = u ** (1.0 / LRU_C)
    lam = jnp.log(a0) - jnp.log1p(-a0)
    return {
        "x": nrm(ks[0], (BATCH, SEQ, D_MODEL), 1.0),
        "mem": nrm(ks[1], (BATCH, MEM_LEN, D_MODEL), 1.0),
        "positions": jnp.broadcast_to(jnp.arange(SEQ, dtype=jnp.int32)[None, :], (BATCH, SEQ)),
        "g_mix": 1.0 + nrm(ks[2], (DEPTH, D_MODEL), 0.02),
        "g_mem": 1.0 + nrm(ks[3], (DEPTH, D_MODEL), 0.02),
        "w_in": nrm(ks[4], (DEPTH, D_MODEL, IN_W), D_MODEL ** -0.5),
        "gate_b": nrm(ks[5], (DEPTH, GATE_W), 0.02),
        "attn_sink": nrm(ks[6], (DEPTH, ATTN_HEADS), 0.5),
        "conv_w": nrm(ks[7], (DEPTH, CONV_WIDTH, LRU_WIDTH), CONV_WIDTH ** -0.5),
        "conv_b": nrm(ks[8], (DEPTH, LRU_WIDTH), 0.02),
        "lru_wr": nrm(ks[9], (DEPTH, 2, LRU_BLOCKS, LRU_BLOCK_W, LRU_BLOCK_W), LRU_BLOCK_W ** -0.5),
        "lru_br": nrm(ks[10], (DEPTH, 2, LRU_WIDTH), 0.02),
        "lru_wi": nrm(ks[11], (DEPTH, 2, LRU_BLOCKS, LRU_BLOCK_W, LRU_BLOCK_W), LRU_BLOCK_W ** -0.5),
        "lru_bi": nrm(ks[13], (DEPTH, 2, LRU_WIDTH), 0.02),
        "lru_lambda": lam,
        "w_mem_kv": nrm(ks[14], (DEPTH, D_MODEL, 2 * MEM_Q_W), D_MODEL ** -0.5),
        "p_attn": nrm(ks[15], (DEPTH, ATTN_Q_W, D_MODEL), ATTN_Q_W ** -0.5),
        "p_lru": nrm(ks[16], (DEPTH, LRU_WIDTH, D_MODEL), LRU_WIDTH ** -0.5),
        "p_mem": nrm(ks[17], (DEPTH, MEM_Q_W, D_MODEL), MEM_Q_W ** -0.5),
        "w_out": nrm(ks[18], (DEPTH, D_MODEL, D_MODEL), D_MODEL ** -0.5),
        "g_ffn": 1.0 + nrm(ks[19], (DEPTH, D_MODEL), 0.02),
        "w_peer_q": nrm(ks[20], (DEPTH, D_MODEL, PEER_HEADS * PEER_QDIM), D_MODEL ** -0.5),
        "peer_sub_keys": nrm(ks[21], (DEPTH, PEER_HEADS, 2, PEER_KEYS, PEER_HALF), PEER_HALF ** -0.5),
        "peer_u": nrm(ks[22], (DEPTH, PEER_EXPERTS, D_MODEL), D_MODEL ** -0.5),
        "peer_v": nrm(ks[23], (DEPTH, PEER_EXPERTS, D_MODEL), 0.25),
        "g_final": 1.0 + nrm(ks[24], (D_MODEL,), 0.02),
    }

def first_block(x, mem, positions, g_mix, g_mem, w_in, gate_b, attn_sink, conv_w, conv_b,
              lru_wr, lru_br, lru_wi, lru_bi, lru_lambda, w_mem_kv, p_attn, p_lru, p_mem,
              w_out, g_ffn, w_peer_q, peer_sub_keys, peer_u, peer_v, g_final):
    b, s, d = x.shape
    offs = [int(o) for o in np.cumsum([ATTN_Q_W, ATTN_KV_W, ATTN_KV_W, LRU_WIDTH, LRU_WIDTH, MEM_Q_W])]
    for l in range(DEPTH):
        h = rmsnorm(x, g_mix[l])
        proj = h @ w_in[l]
        q_a, k_a, v_a, x_l, gate_l, q_m, gates = jnp.split(proj, offs, axis=-1)
        q_a = partial_rope(q_a.reshape(b, s, ATTN_HEADS, HEAD_DIM), positions)
        k_a = partial_rope(k_a.reshape(b, s, ATTN_KV_HEADS, HEAD_DIM), positions)
        v_a = v_a.reshape(b, s, ATTN_KV_HEADS, HEAD_DIM)
        attn_out = windowed_gqa(q_a, k_a, v_a, attn_sink[l])
        xc = centred_depthwise_conv(x_l, conv_w[l], conv_b[l])
        lru_out = bidir_rglru(xc, lru_wr[l], lru_br[l], lru_wi[l], lru_bi[l], lru_lambda[l]) * jax.nn.gelu(gate_l)
        kv_m = rmsnorm(mem, g_mem[l]) @ w_mem_kv[l]
        k_m = kv_m[..., :MEM_Q_W].reshape(b, MEM_LEN, MEM_HEADS, HEAD_DIM)
        v_m = kv_m[..., MEM_Q_W:].reshape(b, MEM_LEN, MEM_HEADS, HEAD_DIM)
        mem_out = memory_cross_attention(q_m.reshape(b, s, MEM_HEADS, HEAD_DIM), k_m, v_m)
        g = jax.nn.sigmoid(gates + gate_b[l]).reshape(b, s, N_BRANCH, d)
        merged = (g[:, :, 0] * (attn_out @ p_attn[l])
                  + g[:, :, 1] * (lru_out @ p_lru[l])
                  + g[:, :, 2] * (mem_out @ p_mem[l]))
        x = x + merged @ w_out[l]
        h2 = rmsnorm(x, g_ffn[l])
        x = x + peer_ffn(h2, w_peer_q[l], peer_sub_keys[l], peer_u[l], peer_v[l])
    return rmsnorm(x, g_final)


DEPTH_2 = 2

MIX_WIDTH = 512
N_BRANCH_2 = 4
RET_HEADS = 4
RET_DK = MIX_WIDTH // RET_HEADS
RET_DV = MIX_WIDTH // RET_HEADS
RET_CHUNK = 128
ROPE_BASE = 10000.0
CONV_CH = MIX_WIDTH
CONV_WIDTH_2 = 31
GMLP_CH = MIX_WIDTH
GMLP_GROUPS = 4
GMLP_GROUP_CH = GMLP_CH // GMLP_GROUPS
GMLP_CHUNK = 128
SWA_HEADS = 8
SWA_KV_HEADS = 2
SWA_GROUP = SWA_HEADS // SWA_KV_HEADS
SWA_HEAD_DIM = MIX_WIDTH // SWA_HEADS
SWA_WINDOW = 128
SWA_BLOCK = 128
REL_BUCKETS = 32
REL_MAX_DIST = 128
D_FF = ((8 * D_MODEL + 3 * 256 - 1) // (3 * 256)) * 256
RET_COLS = 4 * MIX_WIDTH
CONV_COLS = 2 * CONV_CH
GMLP_COLS = 2 * GMLP_CH
SWA_COLS = (SWA_HEADS + 2 * SWA_KV_HEADS) * SWA_HEAD_DIM
GATE_COLS = N_BRANCH_2 * D_MODEL
IN_COLS = RET_COLS + CONV_COLS + GMLP_COLS + SWA_COLS + GATE_COLS
IN_SPLITS = [RET_COLS, RET_COLS + CONV_COLS, RET_COLS + CONV_COLS + GMLP_COLS,
             RET_COLS + CONV_COLS + GMLP_COLS + SWA_COLS]


def rms_norm(x, g):
    xf = x.astype(jnp.float32)
    y = xf * lax.rsqrt(jnp.mean(xf * xf, axis=-1, keepdims=True) + EPS)
    return (y * g.astype(jnp.float32)).astype(x.dtype)

def layer_norm(x, g, b):
    xf = x.astype(jnp.float32)
    mu = jnp.mean(xf, axis=-1, keepdims=True)
    var = jnp.mean(jnp.square(xf - mu), axis=-1, keepdims=True)
    return (xf - mu) * lax.rsqrt(var + EPS) * g.astype(jnp.float32) + b.astype(jnp.float32)

def rotary(x, pos):
    half = x.shape[-1] // 2
    inv = ROPE_BASE ** (-jnp.arange(half, dtype=jnp.float32) / half)
    ang = pos.astype(jnp.float32)[:, None] * inv[None, :]
    cos = jnp.cos(ang)[None, :, None, :]
    sin = jnp.sin(ang)[None, :, None, :]
    x1, x2 = x[..., :half], x[..., half:]
    return jnp.concatenate([x1 * cos - x2 * sin, x1 * sin + x2 * cos], axis=-1)

def retention(za, gn_g):
    B, S, _ = za.shape
    C = RET_CHUNK
    N = S // C
    H = RET_HEADS
    qa, ka, va, ga = jnp.split(za, 4, axis=-1)
    pos = jnp.arange(S)
    q = rotary(qa.astype(jnp.float32).reshape(B, S, H, RET_DK), pos)
    k = rotary(ka.astype(jnp.float32).reshape(B, S, H, RET_DK), pos) * (RET_DK ** -0.5)
    v = va.astype(jnp.float32).reshape(B, S, H, RET_DV)
    gamma = 1.0 - 2.0 ** (-5.0 - jnp.arange(H, dtype=jnp.float32))
    log_g = jnp.log(gamma)
    idx = jnp.arange(C, dtype=jnp.float32)
    diff = idx[:, None] - idx[None, :]
    decay = jnp.where(diff >= 0, jnp.exp(log_g[:, None, None] * jnp.maximum(diff, 0.0)), 0.0)
    xi = jnp.exp(log_g[None, :] * (idx[:, None] + 1.0))
    zeta = jnp.exp(log_g[None, :] * (C - 1.0 - idx[:, None]))
    chunk_decay = jnp.exp(log_g * C)
    qc = q.reshape(B, N, C, H, RET_DK)
    kc = k.reshape(B, N, C, H, RET_DK)
    vc = v.reshape(B, N, C, H, RET_DV)
    scores = jnp.einsum('bnthd,bnshd->bnhts', qc, kc) * decay[None, None]
    y_inner = jnp.einsum('bnhts,bnshv->bnthv', scores, vc)
    kv = jnp.einsum('bnshd,bnshv->bnhdv', kc * zeta[None, None, :, :, None], vc)

    def step(state, kv_n):
        return chunk_decay[None, :, None, None] * state + kv_n, state

    state0 = jnp.zeros((B, H, RET_DK, RET_DV), jnp.float32)
    _, state_prev = lax.scan(step, state0, jnp.moveaxis(kv, 1, 0))
    state_prev = jnp.moveaxis(state_prev, 0, 1)
    y_cross = jnp.einsum('bnthd,bnhdv->bnthv', qc * xi[None, None, :, :, None], state_prev)
    y = (y_inner + y_cross).reshape(B, S, H, RET_DV)
    mu = jnp.mean(y, axis=-1, keepdims=True)
    var = jnp.mean(jnp.square(y - mu), axis=-1, keepdims=True)
    y = ((y - mu) * lax.rsqrt(var + EPS)).reshape(B, S, H * RET_DV) * gn_g.astype(jnp.float32)
    return jax.nn.silu(ga.astype(jnp.float32)) * y

def conformer_conv(zb, conv_w, conv_b, ln_g, ln_b):
    a, gate = jnp.split(zb, 2, axis=-1)
    u = (a * jax.nn.sigmoid(gate)).astype(conv_w.dtype)
    u = lax.conv_general_dilated(u, conv_w, window_strides=(1,), padding=[(CONV_WIDTH_2 - 1, 0)],
                                 dimension_numbers=('NWC', 'WIO', 'NWC'),
                                 feature_group_count=CONV_CH)
    u = u + conv_b
    return jax.nn.silu(layer_norm(u, ln_g, ln_b))

def spatial_gating(zc, ln_g, ln_b, w_s, b_s):
    B, S, _ = zc.shape
    N = S // GMLP_CHUNK
    hc = jax.nn.gelu(zc.astype(jnp.float32))
    u, v = jnp.split(hc, 2, axis=-1)
    v = layer_norm(v, ln_g, ln_b).reshape(B, N, GMLP_CHUNK, GMLP_GROUPS, GMLP_GROUP_CH)
    mask = jnp.tril(jnp.ones((GMLP_CHUNK, GMLP_CHUNK), jnp.float32))
    ws = w_s.astype(jnp.float32) * mask[None]
    s = jnp.einsum('gts,bnsgc->bntgc', ws, v) + b_s.astype(jnp.float32).T[None, None, :, :, None]
    return u * s.reshape(B, S, GMLP_CH)

def t5_bucket(dist):
    max_exact = REL_BUCKETS // 2
    d = jnp.maximum(dist, 1).astype(jnp.float32)
    large = max_exact + (jnp.log(d / max_exact) / math.log(REL_MAX_DIST / max_exact)
                         * (REL_BUCKETS - max_exact)).astype(jnp.int32)
    large = jnp.minimum(large, REL_BUCKETS - 1)
    return jnp.where(dist < max_exact, dist, large)

def swa_attention(zd, q_g, k_g, sinks, rel_bias):
    B, S, _ = zd.shape
    Bk = SWA_BLOCK
    N = S // Bk
    d = SWA_HEAD_DIM
    qd, kd, vd = jnp.split(zd, [SWA_HEADS * d, (SWA_HEADS + SWA_KV_HEADS) * d], axis=-1)
    q = rms_norm(qd.reshape(B, S, SWA_HEADS, d), q_g).astype(jnp.float32)
    k = rms_norm(kd.reshape(B, S, SWA_KV_HEADS, d), k_g).astype(jnp.float32)
    v = vd.reshape(B, S, SWA_KV_HEADS, d).astype(jnp.float32)
    qb = q.reshape(B, N, Bk, SWA_KV_HEADS, SWA_GROUP, d)

    def band(t):
        tb = t.reshape(B, N, Bk, SWA_KV_HEADS, d)
        prev = jnp.pad(tb[:, :-1], ((0, 0), (1, 0), (0, 0), (0, 0), (0, 0)))
        return jnp.concatenate([prev, tb], axis=2)

    kb, vb = band(k), band(v)
    s = jnp.einsum('bnqhgd,bnkhd->bnhgqk', qb, kb) * (d ** -0.5)
    qi = jnp.arange(Bk)[:, None] + Bk
    kj = jnp.arange(2 * Bk)[None, :]
    dist = qi - kj
    in_win = (dist >= 0) & (dist < SWA_WINDOW)
    bias = rel_bias.astype(jnp.float32)[t5_bucket(jnp.maximum(dist, 0))]
    bias = bias.transpose(2, 0, 1).reshape(SWA_KV_HEADS, SWA_GROUP, Bk, 2 * Bk)
    valid = in_win[None] & ((jnp.arange(N)[:, None, None] > 0) | (kj[None] >= Bk))
    s = jnp.where(valid[None, :, None, None], s + bias[None, None], -jnp.inf)
    sink = sinks.astype(jnp.float32).reshape(SWA_KV_HEADS, SWA_GROUP)[None, None, :, :, None, None]
    m = jnp.maximum(jnp.max(s, axis=-1, keepdims=True), sink)
    p = jnp.exp(s - m)
    denom = jnp.sum(p, axis=-1, keepdims=True) + jnp.exp(sink - m)
    o = jnp.einsum('bnhgqk,bnkhd->bnqhgd', p / denom, vb)
    return o.reshape(B, S, SWA_HEADS * d)

def hybrid_layer(x, rel_bias, norm1_g, w_in, ret_gn_g, conv_w, conv_b, conv_ln_g, conv_ln_b,
                 gmlp_ln_g, gmlp_ln_b, gmlp_ws, gmlp_bs, swa_q_g, swa_k_g, swa_sinks,
                 w_branch, w_out, norm2_g, w_ffn_in, w_ffn_out):
    B, S, _ = x.shape
    h = rms_norm(x, norm1_g)
    z = h @ w_in
    za, zb, zc, zd, zg = jnp.split(z, IN_SPLITS, axis=-1)
    ya = retention(za, ret_gn_g)
    yb = conformer_conv(zb, conv_w, conv_b, conv_ln_g, conv_ln_b)
    yc = spatial_gating(zc, gmlp_ln_g, gmlp_ln_b, gmlp_ws, gmlp_bs)
    yd = swa_attention(zd, swa_q_g, swa_k_g, swa_sinks, rel_bias)
    ys = jnp.stack([ya, yb, yc, yd], axis=2).astype(w_branch.dtype)
    branches = jnp.einsum('bsnc,ncd->bsnd', ys, w_branch)
    gates = jax.nn.sigmoid(zg.reshape(B, S, N_BRANCH_2, D_MODEL))
    mix = jnp.sum(gates * branches, axis=2)
    x = x + (mix @ w_out).astype(x.dtype)
    h = rms_norm(x, norm2_g)
    gt, up = jnp.split(h @ w_ffn_in, 2, axis=-1)
    return x + ((jax.nn.silu(gt) * up) @ w_ffn_out).astype(x.dtype)

def second_inputs(seed: int = 0) -> dict:
    key = jax.random.key(seed)
    ks = jax.random.split(key, 24)
    f32 = jnp.float32
    nrm = lambda k, shape, s: jax.random.normal(k, shape, f32) * s
    L = DEPTH_2
    return {
        'x': nrm(ks[0], (BATCH, SEQ, D_MODEL), 1.0),
        'rel_bias': nrm(ks[1], (REL_BUCKETS, SWA_HEADS), 0.5),
        'norm1_g': 1.0 + nrm(ks[2], (L, D_MODEL), 0.02),
        'w_in': nrm(ks[3], (L, D_MODEL, IN_COLS), D_MODEL ** -0.5),
        'ret_gn_g': 1.0 + nrm(ks[4], (L, MIX_WIDTH), 0.02),
        'conv_w': nrm(ks[5], (L, CONV_WIDTH_2, 1, CONV_CH), CONV_WIDTH_2 ** -0.5),
        'conv_b': nrm(ks[6], (L, CONV_CH), 0.02),
        'conv_ln_g': 1.0 + nrm(ks[7], (L, CONV_CH), 0.02),
        'conv_ln_b': nrm(ks[8], (L, CONV_CH), 0.02),
        'gmlp_ln_g': 1.0 + nrm(ks[9], (L, GMLP_CH), 0.02),
        'gmlp_ln_b': nrm(ks[10], (L, GMLP_CH), 0.02),
        'gmlp_ws': nrm(ks[11], (L, GMLP_GROUPS, GMLP_CHUNK, GMLP_CHUNK), 0.5 * GMLP_CHUNK ** -0.5),
        'gmlp_bs': 1.0 + nrm(ks[12], (L, GMLP_GROUPS, GMLP_CHUNK), 0.02),
        'swa_q_g': 1.0 + nrm(ks[13], (L, SWA_HEAD_DIM), 0.02),
        'swa_k_g': 1.0 + nrm(ks[14], (L, SWA_HEAD_DIM), 0.02),
        'swa_sinks': nrm(ks[15], (L, SWA_HEADS), 0.5),
        'w_branch': nrm(ks[16], (L, N_BRANCH_2, MIX_WIDTH, D_MODEL), MIX_WIDTH ** -0.5),
        'w_out': nrm(ks[17], (L, D_MODEL, D_MODEL), 0.5 * D_MODEL ** -0.5),
        'norm2_g': 1.0 + nrm(ks[18], (L, D_MODEL), 0.02),
        'w_ffn_in': nrm(ks[19], (L, D_MODEL, 2 * D_FF), D_MODEL ** -0.5),
        'w_ffn_out': nrm(ks[20], (L, D_FF, D_MODEL), 0.5 * D_FF ** -0.5),
    }

def second_block(x, rel_bias, norm1_g, w_in, ret_gn_g, conv_w, conv_b, conv_ln_g, conv_ln_b,
              gmlp_ln_g, gmlp_ln_b, gmlp_ws, gmlp_bs, swa_q_g, swa_k_g, swa_sinks,
              w_branch, w_out, norm2_g, w_ffn_in, w_ffn_out):
    for l in range(DEPTH_2):
        x = hybrid_layer(x, rel_bias, norm1_g[l], w_in[l], ret_gn_g[l], conv_w[l], conv_b[l],
                         conv_ln_g[l], conv_ln_b[l], gmlp_ln_g[l], gmlp_ln_b[l], gmlp_ws[l],
                         gmlp_bs[l], swa_q_g[l], swa_k_g[l], swa_sinks[l], w_branch[l],
                         w_out[l], norm2_g[l], w_ffn_in[l], w_ffn_out[l])
    return x


_first_inputs = second_inputs


def second_inputs(seed=0):
    import zlib

    import numpy as np

    out = dict(_first_inputs(seed))
    spreads = {}
    factors = {'norm1_g': 4.284,
     'ret_gn_g': 8.0,
     'conv_b': 5.477,
     'conv_ln_g': 8.0,
     'conv_ln_b': 8.0,
     'gmlp_ln_g': 8.0,
     'gmlp_ln_b': 8.0,
     'gmlp_bs': 8.0,
     'swa_q_g': 8.0,
     'swa_k_g': 8.0,
     'swa_sinks': 8.0,
     'norm2_g': 5.074}
    for name, (base, spread) in spreads.items():
        noise = np.random.default_rng([zlib.crc32(name.encode()), seed]).standard_normal(out[name].shape)
        drawn = base * np.exp(spread * noise) if base else spread * noise
        out[name] = __import__('jax').numpy.asarray(drawn.astype(out[name].dtype))
    for name, factor in factors.items():
        out[name] = (out[name] * factor).astype(out[name].dtype)
    return out


_narrow_inputs = second_inputs


def second_inputs(seed=0):

    out = dict(_narrow_inputs(seed))
    wider = {'rel_bias': 5.02,
     'conv_b': 3.74,
     'conv_ln_g': 9.51,
     'conv_ln_b': 9.82,
     'gmlp_ln_g': 6.58,
     'gmlp_ln_b': 6.82,
     'swa_sinks': 12.0}
    for name, times in wider.items():
        mean = out[name].mean()
        out[name] = (mean + times * (out[name] - mean)).astype(out[name].dtype)
    return out


def setup_inputs(seed=0):
    out = dict(first_inputs(seed))
    for name, value in second_inputs(seed + 1).items():
        if name != "x":
            out[name + "_2"] = value
    return out


def reference(
    x, mem, positions, g_mix, g_mem, w_in, gate_b, attn_sink, conv_w, conv_b, lru_wr, lru_br,
    lru_wi, lru_bi, lru_lambda, w_mem_kv, p_attn, p_lru, p_mem, w_out, g_ffn, w_peer_q,
    peer_sub_keys, peer_u, peer_v, g_final, rel_bias_2, norm1_g_2, w_in_2, ret_gn_g_2, conv_w_2,
    conv_b_2, conv_ln_g_2, conv_ln_b_2, gmlp_ln_g_2, gmlp_ln_b_2, gmlp_ws_2, gmlp_bs_2,
    swa_q_g_2, swa_k_g_2, swa_sinks_2, w_branch_2, w_out_2, norm2_g_2, w_ffn_in_2, w_ffn_out_2,
):
    x = first_block(
        x, mem, positions, g_mix, g_mem, w_in, gate_b, attn_sink, conv_w, conv_b, lru_wr,
        lru_br, lru_wi, lru_bi, lru_lambda, w_mem_kv, p_attn, p_lru, p_mem, w_out, g_ffn,
        w_peer_q, peer_sub_keys, peer_u, peer_v, g_final,
    )
    return second_block(
        x, rel_bias_2, norm1_g_2, w_in_2, ret_gn_g_2, conv_w_2, conv_b_2, conv_ln_g_2,
        conv_ln_b_2, gmlp_ln_g_2, gmlp_ln_b_2, gmlp_ws_2, gmlp_bs_2, swa_q_g_2, swa_k_g_2,
        swa_sinks_2, w_branch_2, w_out_2, norm2_g_2, w_ffn_in_2, w_ffn_out_2,
    )


_drawn_inputs = setup_inputs


def setup_inputs(seed=0):
    import zlib

    import numpy as np

    out = dict(_drawn_inputs(seed))
    spreads = {}
    factors = {'attn_sink': 8.0, 'lru_br': 2.734, 'swa_sinks_2': 2.986, 'g_mem': 2.724, 'lru_bi': 2.96}
    for name, (base, spread) in spreads.items():
        noise = np.random.default_rng([zlib.crc32(name.encode()), seed]).standard_normal(out[name].shape)
        drawn = base * np.exp(spread * noise) if base else spread * noise
        out[name] = __import__('jax').numpy.asarray(drawn.astype(out[name].dtype))
    for name, factor in factors.items():
        out[name] = (out[name] * factor).astype(out[name].dtype)
    return out
```

```python
import numpy as np

import concourse.bass as bass
from concourse import mybir

ALU = mybir.AluOpType
ACT = mybir.ActivationFunctionType
AXIS_X = mybir.AxisListType.X
F32 = mybir.dt.float32
F32R = mybir.dt.float32r
U32 = mybir.dt.uint32
I32 = mybir.dt.int32

P = 128
TOKENS, D = 256, 1024
TILES = TOKENS // P
KD = D // P
EPS = 1e-6
MASKED = -1e30
HEAD = 128
Q_HEADS, KV_HEADS, MEM_HEADS = 6, 2, 4
LRU_BLOCKS, CONV_TAPS, CONV_LEFT = 6, 4, 2
LRU_BATCH = 2
BRANCHES = 3
ROPE_DIM, ROPE_THETA = 32, 500000.0
WINDOW = 128
PEER_HEADS, KEYS, TOPK = 8, 128, 16
SLOTS = PEER_HEADS * TOPK
LRU_C = 8.0
LAYERS = 2
MIX = 512
KM = MIX // P
RET_HEADS = 4
TAPS2 = 31
SWA_HEADS, SWA_DIM, SWA_WINDOW = 8, 64, 128
BUCKETS = 32
BRANCHES2 = 4
D_FF = 2816
KF = D_FF // P
SKEW = 384



def fm_units(w):
    k, n = w.shape
    return np.ascontiguousarray(
        w.reshape(k // P, P, n // P, P).transpose(2, 1, 0, 3).reshape(n // P, P, (k // P) * P))


def tm_units(w, chunks, width):
    k, n = w.shape
    a = w.reshape(k // P // chunks, chunks, P, n // width, width).transpose(3, 0, 2, 1, 4)
    return np.ascontiguousarray(a.reshape(-1, P, chunks * width))


def columns(v):
    v = np.asarray(v)
    return v.reshape(-1, P).T


SWA_ORDER = [h for c in range(4) for h in (c, c + 4)]


def swa_q_columns(w):
    return w.reshape(w.shape[0], SWA_HEADS, SWA_DIM)[:, SWA_ORDER].reshape(w.shape[0], -1)


COLS = {}
COLS_N = 0


def _col(name, n):
    global COLS_N
    COLS[name] = (COLS_N, n)
    COLS_N += n


for _n, _w in (("g_mix", KD), ("g_mem", KD), ("gate_b", 24), ("conv_w", 24), ("conv_b", 6), ("lru_br", 12),
               ("lru_bi", 12), ("lam", 12), ("g_ffn", KD), ("sink", Q_HEADS)):
    _col(_n, _w)
for _l in range(LAYERS):
    for _n, _w in (("norm1", KD), ("gn", KM), ("conv_w2", TAPS2 * KM), ("conv_b2", KM), ("cln_g", KM),
                   ("cln_b", KM), ("q_g", 1), ("k_g", 1), ("norm2", KD), ("sinks2", SWA_HEADS)):
        _col(f"{_n}.{_l}", _w)


def bucket_of(dist):
    d = np.maximum(dist, 1).astype(np.float32)
    large = 16 + (np.log(d / np.float32(16)) / np.float32(np.log(8.0)) * np.float32(16)).astype(np.int32)
    return np.where(dist < 16, dist, np.minimum(large, BUCKETS - 1))


def shape_constants():
    f = np.float32
    p = np.arange(P)
    c = {}
    c["ident"] = np.eye(P, dtype=f)
    c["iota"] = np.broadcast_to(p.astype(f), (P, P)).copy()
    half = ROPE_DIM // 2
    inv = (f(ROPE_THETA) ** (-np.arange(0, ROPE_DIM, 2, dtype=f) / f(ROPE_DIM))).astype(f)
    c["inv_freq"] = np.concatenate([inv, inv, np.zeros(P - ROPE_DIM, f)])[:, None].copy()
    swap = np.zeros((P, P), f)
    for m in range(half):
        swap[m + half, m] = -1
        swap[m, m + half] = 1
    c["swap1"] = swap
    q = np.arange(TOKENS)
    ok = np.abs(q[None, :] - q[:, None]) <= WINDOW
    m = np.where(ok, 0, MASKED).astype(f)
    c["mask1"] = m.reshape(TILES, P, TOKENS).transpose(1, 0, 2).reshape(P, -1).copy()
    hh = P // 2
    inv2 = f(10000.0) ** (-np.arange(hh, dtype=f) / f(hh))
    ang = np.arange(TOKENS).astype(f)[:, None] * inv2[None, :]
    c["ret_cos"] = np.tile(np.cos(ang).T, (2, 1)).astype(f)
    c["ret_sin"] = np.tile(np.sin(ang).T, (2, 1)).astype(f)
    swap = np.zeros((P, P), f)
    for m_ in range(hh):
        swap[m_ + hh, m_] = -1
        swap[m_, m_ + hh] = 1
    c["swap2"] = swap
    gamma = 1.0 - 2.0 ** (-5.0 - np.arange(RET_HEADS, dtype=np.float64))
    diff = np.arange(TOKENS)[None, :] - p[:, None]
    dec = [np.where(diff >= 0, g ** np.maximum(diff, 0), 0) * P ** -0.5 for g in gamma]
    c["decay"] = np.stack(dec, 1).astype(f).reshape(P, -1)
    c["tril"] = (p[None, :] >= p[:, None]).astype(f)
    c["half_ones"] = np.kron(np.eye(2), np.ones((SWA_DIM, SWA_DIM))).astype(f)
    dist = 2 * P - 1 - np.arange(SKEW)
    inside = (dist >= 0) & (dist < SWA_WINDOW)
    one = np.zeros((P, SKEW), f)
    one[bucket_of(np.maximum(dist, 0))[inside], np.arange(SKEW)[inside]] = 1
    c["bucket"] = one
    c["outside"] = np.broadcast_to(np.where(inside, 0, MASKED).astype(f), (P, SKEW)).copy()
    return c


BASE_CONSTS = ("ident", "iota", "inv_freq")
MIX_CONSTS = ("swap1", "mask1")
LAYER_CONSTS = ("ret_cos", "ret_sin", "swap2", "decay", "tril", "half_ones")
BIAS_CONSTS = ("bucket", "outside")


def pack(c, names):
    return np.concatenate([c[n] for n in names], axis=1)




class Queue:

    def __init__(self, nc, engine, name):
        self.e, self.sem, self.count, self.seen = engine, nc.alloc_semaphore(name), 0, {}

    def did(self, instruction):
        self.count += 1
        instruction.then_inc(self.sem, 1)
        return (self.sem, self.count)

    def wait(self, *marks):
        need = {}
        for m in marks:
            if m is None:
                continue
            if isinstance(m, list):
                for x in m:
                    if x is not None:
                        need[x[0].name] = max(need.get(x[0].name, (0, None)), (x[1], x[0]), key=lambda t: t[0])
            else:
                need[m[0].name] = max(need.get(m[0].name, (0, None)), (m[1], m[0]), key=lambda t: t[0])
        for name, (value, sem) in need.items():
            if self.seen.get(name, 0) < value:
                self.e.wait_ge(sem, value)
                self.seen[name] = value

    def then(self, instruction):
        m = self.did(instruction)
        self.wait(m)
        return m


class Pair:

    def __init__(self, hi, lo, marks=None):
        self.hi, self.lo, self.marks = hi, lo, marks
        self.chunk_marks = None

    def at(self, f):
        return Pair(f(self.hi), f(self.lo), self.marks)


class Bank:

    def __init__(self, nc, name):
        self.t = nc.alloc_psum_tensor(name, [P, 512], F32)
        self.free = []

    def v(self, n=512, **kw):
        return self.t[:, 0:n]


def wide(ap, n):
    return ap.unsqueeze(2).to_broadcast([ap.shape[0], ap.shape[1], n])


class Program:
    def __init__(self, nc, dram, out):
        self.nc, self.dram, self.out = nc, dram, out
        self.pe = Queue(nc, nc.tensor, "pe_done")
        self.act = Queue(nc, nc.scalar, "act_done")
        self.dve = Queue(nc, nc.vector, "dve_done")
        self.pool = Queue(nc, nc.gpsimd, "pool_done")
        self.sp = Queue(nc, nc.sync, "sp_unused")
        self.dma_sems = {}
        self.names = 0
        self.address = {}
        self.base = (nc.sbuf_base + 63) // 64 * 64
        self.top = self.base
        self.end = nc.sbuf_usable_end
        self.stream_banks = [Bank(nc, f"stream_bank{i}") for i in range(3)]
        self.side_banks = [Bank(nc, f"side_bank{i}") for i in range(5)]
        self.next_stream_bank = 0
        self.writes_out = []

    def place(self, name, shape, dtype=F32, at=None):
        size = 4 * int(np.prod(shape[1:]))
        size = (size + 31) // 32 * 32
        if at is None:
            at = self.top
            self.top += size
        assert at + size <= self.end, (name, at + size - self.end)
        self.names += 1
        t = self.nc.alloc_sbuf_tensor_at(f"{name}_{self.names}", list(shape), dtype, offset=at)
        self.address[t.name] = at
        return t

    def addr(self, t):
        return self.address[t.name]

    def pair(self, name, shape, at=None):
        size = 4 * int(np.prod(shape[1:]))
        hi = self.place(name + "_hi", shape, F32R, at)
        lo = self.place(name + "_lo", shape, F32R, None if at is None else at + size)
        return Pair(hi, lo, [])

    def dma(self, name, out, in_, *marks, queue=None):
        q = queue or self.sp
        sem, n = self.dma_sems.get(name, (None, 0))
        if sem is None:
            sem = self.nc.alloc_semaphore("dma_" + name)
        q.wait(*marks)
        q.e.dma_start(out, in_).then_inc(sem, 16)
        self.dma_sems[name] = (sem, n + 16)
        return (sem, n + 16)

    def start_stream(self, plan, raw_slots=3, split_slots=4):
        self.plan = plan
        self.R, self.H = raw_slots, split_slots
        self.raw = [self.place(f"raw{i}", [P, 1024]) for i in range(raw_slots)]
        self.hi = [self.place(f"unit_hi{i}", [P, 1024], F32R) for i in range(split_slots)]
        self.lo = [self.place(f"unit_lo{i}", [P, 1024], F32R) for i in range(split_slots)]
        self.loaded, self.split_marks, self.used = {}, {}, {}
        self.taken = 0
        for n in range(raw_slots):
            self.load_unit(n)
        for n in range(split_slots - 1):
            self.split_unit(n)

    def load_unit(self, n):
        if n >= len(self.plan):
            return
        _, src = self.plan[n]
        width = src.shape[-1]
        before = self.split_marks.get(n - self.R)
        self.loaded[n] = self.dma(f"raw{n % self.R}", self.raw[n % self.R][:, 0:width], src, before)

    def split_unit(self, n):
        if n >= len(self.plan):
            return
        width = self.plan[n][1].shape[-1]
        raw, hi, lo = (t[n % k][:, 0:width] for t, k in ((self.raw, self.R), (self.hi, self.H), (self.lo, self.H)))
        self.act.wait(self.loaded[n], self.used.get(n - self.H))
        h = self.act.did(self.nc.scalar.activation(hi, raw, ACT.Copy))
        q = self.pool if n % 2 else self.dve
        q.wait(self.loaded[n], self.used.get(n - self.H), h)
        l = q.did(q.e.tensor_tensor(lo, raw, hi, ALU.subtract))
        self.split_marks[n] = [h, l]
        self.load_unit(n + self.R)

    def take(self, key):
        n = self.taken
        self.taken += 1
        assert self.plan[n][0] == key, (self.plan[n][0], key)
        self.split_unit(n + self.H - 1)
        self.pe.wait(self.split_marks[n])
        return n, Pair(self.hi[n % self.H], self.lo[n % self.H])

    def mm3(self, out, l, r, start, stop, skip=False):
        mm = self.nc.tensor.matmul
        kw = dict(skip_group_check=True) if skip else {}
        mm(out, l.hi, r.hi, start=start, stop=False, **kw)
        mm(out, l.hi, r.lo, start=False, stop=False, **kw)
        return mm(out, l.lo, r.hi, start=False, stop=stop, **kw)

    def stream_bank(self):
        b = self.stream_banks[self.next_stream_bank % len(self.stream_banks)]
        self.next_stream_bank += 1
        self.pe.wait(b.free)
        return b

    def fm_unit(self, key, rhs, chunks, *marks):
        n, w = self.take(key)
        b = self.stream_bank()
        self.pe.wait(None if rhs.chunk_marks else rhs.marks, *marks)
        out = b.t[:, 0:TOKENS]
        for k in range(chunks):
            if rhs.chunk_marks:
                self.pe.wait(rhs.chunk_marks[k])
            last = self.mm3(out, w.at(lambda t: t[:, k * P:(k + 1) * P]), rhs.at(lambda t: t[:, k, :]),
                            k == 0, k == chunks - 1)
        m = self.pe.did(last)
        self.used[n] = m
        return b, out, m

    def tm_unit(self, key, lhs, first_chunk, chunks, width, banks, start, stop, *marks):
        n, w = self.take(key)
        self.pe.wait(lhs.marks, *marks)
        for k in range(chunks):
            for t in range(TILES):
                for h, bank in enumerate(banks[t]):
                    wd = min(width, 512)
                    last = self.mm3(bank[:, 0:wd], lhs.at(lambda a: a[:, first_chunk + k, t * P:(t + 1) * P]),
                                    w.at(lambda a: a[:, k * width + h * wd:k * width + (h + 1) * wd]),
                                    start and k == 0, stop and k == chunks - 1)
        m = self.pe.did(last)
        self.used[n] = m
        return m

    def split(self, pair, src, bank, *marks, scale=None):
        self.act.wait(*marks)
        h = self.act.did(self.nc.scalar.activation(pair.hi, src, ACT.Copy if scale is None or isinstance(scale, float)
                                                   else ACT.Identity, scale=1.0 if scale is None else scale))
        self.dve.wait(h, *marks)
        if scale is None:
            i = self.nc.vector.tensor_tensor(pair.lo, src, pair.hi, ALU.subtract)
        else:
            i = self.nc.vector.scalar_tensor_tensor(pair.lo, src, scale, pair.hi, ALU.mult, ALU.subtract)
        l = self.dve.did(i)
        if bank is not None:
            bank.free = [l]
        return [h, l]

    def col(self, name, i=0, n=1):
        a, w = COLS[name]
        assert i + n <= w
        return self.cols[:, a + i:a + i + n]

    def rstd_tm(self, x, pieces, name):
        nc = self.nc
        sq, r = self.small(name + "_sq", 2 * TILES), self.small(name + "_r", TILES)
        self.act.wait(self.base_ready)
        self.act.did(nc.scalar.activation(self.small(name + "_t", 1), self.ones[:, 0:1], ACT.Sqrt))
        for (t, h), m in pieces:
            self.act.wait(m)
            cols = slice(h * 512, (h + 1) * 512)
            m = self.act.did(nc.scalar.activation(self.junk[:, t, cols], x[:, t, cols], ACT.Square,
                                                  accum_out=sq[:, h * TILES + t:h * TILES + t + 1]))
        self.dve.wait(m)
        m = self.dve.then(nc.vector.scalar_tensor_tensor(r, sq[:, 0:TILES], EPS * D, sq[:, TILES:], ALU.add, ALU.add))
        self.act.wait(m)
        m = self.act.did(nc.scalar.activation(r, r, ACT.Sqrt, scale=1.0 / D))
        self.dve.wait(m)
        m = self.dve.then(nc.vector.reciprocal(r, r))
        return r, m

    def small(self, name, n):
        a = self.small_at
        self.small_at += n
        assert self.small_at <= self.smalls.shape[1], name
        return self.smalls[:, a:a + n]

    def norm_to_fm(self, x, pieces, gcol, out, name):
        for _ in self.norm_steps(x, pieces, gcol, out, name):
            pass

    def norm_steps(self, x, pieces, gcol, out, name):
        nc = self.nc
        r, m = self.rstd_tm(x, pieces, name)
        self.dve.wait(self.diag_free)
        for t in range(TILES):
            diag_ready = self.dve.did(nc.vector.tensor_scalar(self.diag[:, t, :], self.ident, r[:, t:t + 1], None,
                                                              ALU.mult))
        out.chunk_marks = [None] * KD
        yield
        for k2 in range(KD // 2):
            b = self.side_banks[k2 % 4]
            self.pe.wait(b.free, diag_ready)
            for j in range(2):
                for t in range(TILES):
                    k = 2 * k2 + j
                    last = nc.tensor.matmul(b.t[:, j * TOKENS + t * P:j * TOKENS + (t + 1) * P],
                                            x[:, t, k * P:(k + 1) * P], self.diag[:, t, :], start=True, stop=True)
            turned = self.diag_free = self.pe.did(last)
            self.act.wait(turned)
            for j in range(2):
                k = 2 * k2 + j
                h = self.act.did(nc.scalar.activation(out.hi[:, k, :], b.t[:, j * TOKENS:(j + 1) * TOKENS],
                                                      ACT.Identity, scale=self.col(gcol, k)))
            self.dve.wait(h, turned)
            for j in range(2):
                k = 2 * k2 + j
                l = self.dve.did(nc.vector.scalar_tensor_tensor(
                    out.lo[:, k, :], b.t[:, j * TOKENS:(j + 1) * TOKENS], self.col(gcol, k), out.hi[:, k, :],
                    ALU.mult, ALU.subtract))
                out.chunk_marks[k] = [h, l]
            b.free = [l]
            yield
        out.marks = [h, l]

    def barrier(self):
        qs = (self.pe, self.act, self.dve, self.pool)
        nc = self.nc
        marks = []
        for q in qs:
            if q.count:
                marks.append((q.sem, q.count))
        for q in qs + (self.sp,):
            q.wait(marks)

    def run(self, steps, side=()):
        side = list(side)
        for _ in steps:
            for s in list(side):
                if next(s, "end") == "end":
                    side.remove(s)
        for s in side:
            for _ in s:
                pass




def softmax_head(g, name, state):
    nc = g.nc
    s = state
    bank = g.side_banks[s["bank"]]
    q = s["queries"]
    g.pe.wait(bank.free, s["marks"])
    at, where = 0, []
    for (t, k0, kn) in s["segments"]:
        last = nc.tensor.matmul(bank.t[:, at:at + kn], s["q"](t), s["k"](k0, kn), start=True, stop=True)
        where.append((at, kn))
        at += kn
    scored = g.pe.did(last)
    yield
    S, mx, den = s["S"], s["mx"], s["den"]
    g.dve.wait(scored, s["S_free"][0], g.base_ready, s["bias_ready"])
    if s["bias"] is not None:
        for i, (a, kn) in enumerate(where):
            m = g.dve.did(nc.vector.scalar_tensor_tensor(S[:, a:a + kn], bank.t[:, a:a + kn], s["scale"],
                                                         s["bias"](i), ALU.mult, ALU.add))
        bank.free = [m]
        g.dve.wait(m)
        src, scale = S, 1.0
    else:
        src, scale = bank.t, s["scale"]
    for i, (a, kn) in enumerate(where):
        m = g.dve.did(nc.vector.tensor_reduce(mx[:, i:i + 1], src[:, a:a + kn], AXIS_X, ALU.max))
    g.dve.wait(m)
    if s["sink"] is not None:
        m = g.dve.did(nc.vector.tensor_scalar(mx, mx, s["sink"], -1.0, ALU.max, ALU.mult))
    else:
        m = g.dve.did(nc.vector.tensor_scalar(mx, mx, -scale, None, ALU.mult))
    g.act.wait(m)
    for i, (a, kn) in enumerate(where):
        m = g.act.did(nc.scalar.activation(S[:, a:a + kn], src[:, a:a + kn], ACT.Exp, bias=mx[:, i:i + 1],
                                           scale=scale, accum_out=den[:, i:i + 1]))
    if s["bias"] is None:
        bank.free = [m]
    if s["sink"] is not None:
        m = g.act.did(nc.scalar.activation(s["es"], mx, ACT.Exp, bias=s["sink"]))
    g.dve.wait(m)
    if s["sink"] is not None:
        g.dve.then(nc.vector.tensor_tensor(den, den, s["es"], ALU.add))
    g.dve.then(nc.vector.reciprocal(den, den))
    for i, (a, kn) in enumerate(where):
        m = g.dve.did(nc.vector.tensor_scalar(S[:, a:a + kn], S[:, a:a + kn], den[:, i:i + 1], None, ALU.mult))
    yield
    tb = g.side_banks[s["turn_bank"]]
    g.pe.wait(tb.free, m)
    blocks = {}
    for (t, k0, kn), (a, _) in zip(s["segments"], where):
        for j in range(kn // P):
            kt = k0 // P + j
            dst = tb.t[:, kt * q + t * P:kt * q + (t + 1) * P]
            last = nc.tensor.transpose(dst, S[:, a + j * P:a + (j + 1) * P], g.ident)
            blocks.setdefault(kt, []).append(t)
    turned = g.pe.did(last)
    s["S_free"][0] = turned
    PT = s["PT"]
    g.act.wait(turned, s["PT_free"][0])
    for kt, ts in blocks.items():
        a, n = kt * q + min(ts) * P, len(ts) * P
        m = g.act.did(nc.scalar.activation(PT[:, a:a + n], tb.t[:, a:a + n], ACT.Copy))
    tb.free = [m]
    yield
    ob = g.side_banks[s["out_bank"]]
    g.pe.wait(ob.free, m, s["v_marks"])
    order = sorted(blocks, key=lambda kt: -len(blocks[kt]))
    assert len(blocks[order[0]]) == TILES
    for i, kt in enumerate(order):
        ts = blocks[kt]
        a, n = min(ts) * P, len(ts) * P
        last = nc.tensor.matmul(ob.t[:, a:a + n], s["v"](kt), PT[:, kt * q + a:kt * q + a + n],
                                start=(i == 0), stop=(i == len(order) - 1), skip_group_check=True)
    out = g.pe.did(last)
    s["PT_free"][0] = out
    s["done"](ob, ob.t[:, 0:q], out)
    yield


def pipeline(generators, distance=1):
    waiting, live = list(generators), []
    while waiting or live:
        if waiting:
            live.append(waiting.pop(0))
        for x in list(live):
            if next(x, "end") == "end":
                live.remove(x)
        yield




def mixer(g, phase):
    nc, a = g.nc, g.dram
    V, S = nc.vector, nc.scalar
    g.top = phase
    consts = g.place("mix_consts", [P, P + TILES * TOKENS])
    swap, mask = consts[:, 0:P], consts[:, P:]
    mix_consts = g.dma("mix_consts", consts[:, :], a["mix_consts"])
    hT = g.pair("hT", [P, KD, TOKENS])
    branch = g.pair("branch", [P, 16, TOKENS])
    branch.marks = []
    memT_at = g.top - 2 * 16 * 4 * TOKENS
    memT = g.pair("memT", [P, KD, TOKENS], at=memT_at)
    qk = g.place("qk", [P, 8, TOKENS])
    v_a = g.place("v_a", [P, TILES, 256])
    xl_w = TOKENS + CONV_TAPS - 1
    xl = g.place("xl", [P, LRU_BLOCKS, xl_w])
    xc = g.place("xc", [P, LRU_BLOCKS, TOKENS])
    gl = g.place("gelu_gate", [P, LRU_BLOCKS, TOKENS])
    qm = g.place("qm", [P, MEM_HEADS, TOKENS])
    gates_at = g.top
    gates = g.place("gates", [P, 24, TOKENS])
    x_in = g.place("x_in", [P, TILES, D], at=gates_at)
    m_in = g.place("m_in", [P, TILES, D], at=gates_at + 8192)
    g.junk = g.place("squares", [P, TILES, D], at=gates_at + 16384)
    km = g.place("km", [P, MEM_HEADS, TOKENS])
    vm = g.place("vm", [P, TILES, MIX])
    lru_a = g.place("lru_a", [P, LRU_BATCH, 2, TOKENS])
    lru_b = g.place("lru_b", [P, LRU_BATCH, 2, TOKENS])
    lru_i = g.place("lru_i", [P, LRU_BATCH, 2, TOKENS])
    lru_w = g.place("lru_w", [P, 24, P])
    Sbuf = [g.place(f"S{i}", [P, 512]) for i in range(2)]
    PT = g.place("PT", [P, 512])
    t1 = g.place("t1", [P, 2, TOKENS])
    rope_c, rope_s = g.place("rope_c", [P, TOKENS]), g.place("rope_s", [P, TOKENS])
    pos_i = g.place("pos_i", [P, TOKENS], I32, at=g.addr(lru_b))
    ang, kk = (g.place(n, [P, TOKENS], at=g.addr(lru_i) + 1024 * i) for i, n in enumerate(("ang", "kk")))

    g.rope_tmp = g.place("rope_tmp", [P, TOKENS])[:, :]
    x_ready = g.dma("x_in", x_in[:, :, :], a["x"])
    m_ready = g.dma("m_in", m_in[:, :, :], a["mem"])
    pos_ready = g.dma("pos", pos_i[:, :], a["positions"])
    w_ready = g.dma("lru_w", lru_w[:, :, :], a["lru_w"].rearrange("p (a e) -> p a e", a=24))

    g.norm_to_fm(m_in, [((t, h), m_ready) for t in range(TILES) for h in range(2)], "g_mem", memT, "nm")
    g.act.wait((g.act.sem, g.act.count))
    g.norm_to_fm(x_in, [((t, h), x_ready) for t in range(TILES) for h in range(2)], "g_mix", hT, "nx")
    inputs_read = [(g.pe.sem, g.pe.count), (g.act.sem, g.act.count), (g.dve.sem, g.dve.count)]

    two_pi = 2 * np.pi
    c1 = 6.28125
    c2 = float(np.float32(two_pi - c1).view(np.uint32) & 0xFFFFF000)
    c2 = float(np.array([int(c2)], np.uint32).view(np.float32)[0])
    c3 = two_pi - c1 - c2
    magic = 12582912.0
    g.dve.wait(pos_ready, g.base_ready)
    g.dve.then(V.tensor_copy(ang[:, :], pos_i[:, :]))
    g.dve.then(V.tensor_scalar(ang[:, :], ang[:, :], g.inv_freq, None, ALU.mult))
    g.dve.then(V.tensor_scalar(kk[:, :], ang[:, :], 1 / two_pi, magic, ALU.mult, ALU.add))
    g.dve.then(V.tensor_scalar(kk[:, :], kk[:, :], magic, None, ALU.subtract))
    for c in (c1, c2, c3):
        g.dve.then(V.scalar_tensor_tensor(ang[:, :], kk[:, :], -c, ang[:, :], ALU.mult, ALU.add))
    g.dve.then(V.tensor_scalar(ang[:, :], ang[:, :], 3.1415925, -3.1415925, ALU.min, ALU.max))
    m = g.dve.then(V.scalar_tensor_tensor(kk[:, :], ang[:, :], -1.0, ang[:, :], ALU.mult, ALU.max))
    m = g.dve.then(V.tensor_scalar(kk[:, :], kk[:, :], -1.0, float(np.pi / 2), ALU.mult, ALU.add))
    g.dve.did(V.memset(rope_s[:, :], 0.0))
    m = g.dve.did(V.memset(rope_c[:, :], 1.0))
    g.act.wait(m)
    g.act.did(S.activation(rope_s[0:ROPE_DIM, :], ang[0:ROPE_DIM, :], ACT.Sin))
    rope_ready = g.act.did(S.activation(rope_c[0:ROPE_DIM, :], kk[0:ROPE_DIM, :], ACT.Sin))

    lam = g.col("lam", 0, 12)
    ya, yb, c8, hb = g.small("ya", 12), g.small("yb", 12), g.small("c8", 12), g.small("hb", 24)
    g.dve.then(V.scalar_tensor_tensor(ya, lam, -1.0, lam, ALU.mult, ALU.max))
    m = g.dve.then(V.tensor_scalar(yb, lam, -1.0, 0.0, ALU.mult, ALU.max))
    g.act.wait(m)
    m = g.act.did(S.activation(ya, ya, ACT.Exp, scale=-1.0))
    g.dve.wait(m)
    z, z2 = g.small("z", 12), g.small("z2", 12)
    g.dve.then(V.tensor_scalar(z, ya, 2.0, None, ALU.add))
    g.dve.then(V.reciprocal(z, z))
    g.dve.then(V.tensor_tensor(z, ya, z, ALU.mult))
    g.dve.then(V.tensor_tensor(z2, z, z, ALU.mult))
    terms = 9
    g.dve.then(V.tensor_scalar(c8, z2, 1.0 / (2 * terms + 1), 1.0 / (2 * terms - 1), ALU.mult, ALU.add))
    for i in range(terms - 2, -1, -1):
        g.dve.then(V.tensor_tensor(c8, c8, z2, ALU.mult))
        g.dve.then(V.tensor_scalar(c8, c8, 1.0 / (2 * i + 1), None, ALU.add))
    g.dve.then(V.tensor_tensor(c8, c8, z, ALU.mult))
    g.dve.then(V.scalar_tensor_tensor(c8, c8, 2.0, yb, ALU.mult, ALU.add))
    g.dve.then(V.tensor_scalar(c8, c8, -LRU_C / 2, None, ALU.mult))
    g.dve.did(V.tensor_scalar(hb, g.cols[:, COLS["lru_br"][0]:COLS["lru_br"][0] + 24], 0.5, None, ALU.mult))
    hgb = g.small("hgb", 24)
    smalls_ready = g.dve.did(V.tensor_scalar(hgb, g.col("gate_b", 0, 24), 0.5, None, ALU.mult))
    pads_zero = g.dve.did(V.memset(xl[:, :, 0:CONV_LEFT], 0.0))
    pads_zero = g.dve.did(V.memset(xl[:, :, CONV_LEFT + TOKENS:xl_w], 0.0))

    marks = {}

    def to_sbuf(key, i, dst, chunks=KD, rhs=hT, func=ACT.Copy, **kw):
        b, out, m = g.fm_unit((key, i), rhs, chunks)
        g.act.wait(m, kw.pop("after", None))
        m = g.act.did(S.activation(dst, out, func, **kw))
        b.free = [m]
        marks[key, i] = m

    def tm_to_sbuf(key, dst, units, chunks, width, lhs):
        banks = [g.side_banks[0], g.side_banks[1]]
        for b in banks:
            g.pe.wait(b.free)
        for u in range(units):
            m = g.tm_unit((key, u), lhs, u * chunks, chunks, width, [[b.t] for b in banks], u == 0, u == units - 1)
            yield
        g.act.wait(m)
        for t, b in enumerate(banks):
            e = g.act.did(S.activation(dst[:, t, :], b.t[:, 0:width], ACT.Copy))
            b.free = [e]
        marks[key] = e

    def main():
        for i in range(MEM_HEADS):
            to_sbuf("km", i, km[:, i, :], rhs=memT)
            yield
        yield from tm_to_sbuf("vm", vm, 4, 2, 512, memT)
        marks["memT"] = (g.pe.sem, g.pe.count)
        yield from tm_to_sbuf("va", v_a, 2, 4, 256, hT)
        for i in range(LRU_BLOCKS):
            to_sbuf("xl", i, xl[:, i, CONV_LEFT:CONV_LEFT + TOKENS], after=pads_zero)
            yield
        for i in range(MEM_HEADS):
            to_sbuf("qm", i, qm[:, i, :])
            yield
        for i in range(8):
            to_sbuf("qk", i, qk[:, i, :])
            yield
        for i in range(LRU_BLOCKS):
            to_sbuf("gl", i, gl[:, i, :])
            yield
        g.act.wait(inputs_read)
        for i in range(24):
            to_sbuf("gate", i, gates[:, i, :], func=ACT.Tanh, scale=0.5, bias=hgb[:, i:i + 1],
                    after=[smalls_ready])
            yield

    def conv():
        for i in range(LRU_BLOCKS):
            while ("xl", i) not in marks:
                yield
            g.dve.wait(marks["xl", i], g.base_ready)
            w = lambda j: g.col("conv_w", j * LRU_BLOCKS + i)
            g.dve.then(V.tensor_scalar(xc[:, i, :], xl[:, i, 0:TOKENS], w(0), g.col("conv_b", i), ALU.mult, ALU.add))
            for j in range(1, CONV_TAPS):
                m = g.dve.then(V.scalar_tensor_tensor(xc[:, i, :], xl[:, i, j:j + TOKENS], w(j), xc[:, i, :],
                                                      ALU.mult, ALU.add))
            marks["xc", i] = m
            yield

    lru_free = [None, None]

    def lru_gates(i):
        bank = g.side_banks[4]
        j = i % LRU_BATCH
        for kind in range(2):
            g.pe.wait(bank.free, marks["xc", i], w_ready)
            for d in range(2):
                last = nc.tensor.matmul(bank.t[:, d * TOKENS:(d + 1) * TOKENS], lru_w[:, (kind * 2 + d) * 6 + i, :],
                                        xc[:, i, :], start=True, stop=True)
            m = g.pe.did(last)
            dst = lru_a if kind == 0 else lru_i
            g.act.wait(m, smalls_ready, lru_free)
            for d in range(2):
                m = g.act.did(S.activation(dst[:, j, d, :], bank.t[:, d * TOKENS:(d + 1) * TOKENS], ACT.Tanh,
                                           scale=0.5, bias=hb[:, kind * 12 + d * 6 + i:kind * 12 + d * 6 + i + 1]))
            bank.free = [m]
            if kind == 0:
                g.act.wait(m)
                for d in range(2):
                    c = c8[:, d * 6 + i:d * 6 + i + 1]
                    m = g.act.did(S.activation(lru_b[:, j, d, :], lru_a[:, j, d, :], ACT.Tanh, scale=c, bias=c))
                g.act.wait(m)
                for d in range(2):
                    c = c8[:, d * 6 + i:d * 6 + i + 1]
                    m = g.act.did(S.activation(lru_a[:, j, d, :], lru_a[:, j, d, :], ACT.Exp, scale=c, bias=c))
                th = m
            yield
        g.dve.wait(m, th)
        g.dve.then(V.tensor_scalar(t1[:, :, :], lru_b[:, j, :, :], -1.0, 1.0, ALU.mult, ALU.add))
        g.dve.then(V.reciprocal(t1[:, :, :], t1[:, :, :]))
        m = g.dve.then(V.tensor_tensor(lru_b[:, j, :, :], lru_b[:, j, :, :], t1[:, :, :], ALU.mult))
        for d in range(2):
            m2 = g.dve.did(V.scalar_tensor_tensor(lru_i[:, j, d, :], lru_i[:, j, d, :], 1.0, xc[:, i, :],
                                                  ALU.add, ALU.mult))
        marks["lru_q", i] = [m, m2]
        yield

    def lru_scan(i):
        j = i % LRU_BATCH
        g.dve.wait(marks["lru_sqrt", i // LRU_BATCH])
        m = g.dve.then(V.tensor_tensor(lru_b[:, j, :, :], lru_b[:, j, :, :], lru_i[:, j, :, :], ALU.mult))
        g.dve.then(V.tensor_tensor_scan(t1[:, 0, :], lru_a[:, j, 0, :], lru_b[:, j, 0, :], 0.0, ALU.mult, ALU.add))
        g.dve.then(V.tensor_tensor_scan(t1[:, 1, ::-1], lru_a[:, j, 1, ::-1], lru_b[:, j, 1, ::-1], 0.0,
                                        ALU.mult, ALU.add))
        yield
        g.dve.then(V.tensor_tensor(t1[:, 0, :], t1[:, 0, :], t1[:, 1, :], ALU.add))
        g.dve.wait(marks["gelu"])
        m = g.dve.then(V.scalar_tensor_tensor(t1[:, 0, :], t1[:, 0, :], 0.5, gl[:, i, :], ALU.mult, ALU.mult))
        bp = branch.at(lambda t: t[:, 6 + i, :])
        branch.marks = g.split(bp, t1[:, 0, :], None, m, marks["memT"])
        g.dve.wait(branch.marks)
        yield

    def gelu_gate():
        while ("gl", LRU_BLOCKS - 1) not in marks:
            yield
        c = float(np.sqrt(2 / np.pi))
        for i in range(LRU_BLOCKS):
            u = t1[:, 0, :]
            m = g.dve.wait(marks["gl", i])
            g.dve.then(V.tensor_tensor(u, gl[:, i, :], gl[:, i, :], ALU.mult))
            g.dve.then(V.tensor_scalar(u, u, 0.044715, 1.0, ALU.mult, ALU.add))
            m = g.dve.then(V.tensor_tensor(u, u, gl[:, i, :], ALU.mult))
            g.act.wait(m)
            m = g.act.did(S.activation(u, u, ACT.Tanh, scale=c))
            g.dve.wait(m)
            m = g.dve.then(V.scalar_tensor_tensor(gl[:, i, :], u, 1.0, gl[:, i, :], ALU.add, ALU.mult))
            yield
        marks["gelu"] = m

    def lru():
        yield from conv()
        for half in range(LRU_BLOCKS // LRU_BATCH):
            blocks = range(LRU_BATCH * half, LRU_BATCH * (half + 1))
            for i in blocks:
                yield from lru_gates(i)
            m = sum((marks["lru_q", i] for i in blocks), [])
            g.act.wait(m)
            marks["lru_sqrt", half] = g.act.did(S.activation(lru_b[:, :, :, :], lru_b[:, :, :, :], ACT.Sqrt, scale=-0.5))
            if half == 0:
                yield from gelu_gate()
            for i in blocks:
                yield from lru_scan(i)
            lru_free[:] = [(g.dve.sem, g.dve.count)]

    S_free, PT_free = [[None], [None]], [None]
    n_head = [0]

    def rope():
        for c in list(range(6, 8)) + list(range(6)):
            while ("qk", c) not in marks:
                yield
            bank = g.side_banks[3]
            g.pe.wait(bank.free, marks["qk", c], mix_consts)
            m = g.pe.did(nc.tensor.matmul(bank.t[:, 0:TOKENS], swap, qk[:, c, :], start=True, stop=True))
            g.pool.wait(marks["qk", c], rope_ready, m)
            m2 = g.pool.did(nc.gpsimd.tensor_tensor(qk[:, c, :], qk[:, c, :], rope_c[:, :], ALU.mult))
            g.dve.wait(m, rope_ready)
            u = g.rope_tmp
            m3 = g.dve.then(V.tensor_tensor(u, bank.t[:, 0:TOKENS], rope_s[:, :], ALU.mult))
            bank.free = [m3]
            g.dve.wait(m2)
            marks["rope", c] = g.dve.then(V.tensor_tensor(qk[:, c, :], qk[:, c, :], u, ALU.add))
            yield

    def head(kind, h):
        i = n_head[0]
        n_head[0] += 1
        st = dict(bank=i % 2, turn_bank=2, out_bank=3, queries=TOKENS, scale=HEAD ** -0.5,
                  segments=[(t, 0, TOKENS) for t in range(TILES)], S=Sbuf[i % 2], S_free=S_free[i % 2], PT=PT,
                  PT_free=PT_free, mx=g.small(f"mx{i}", 2), den=g.small(f"den{i}", 2), es=g.small(f"es{i}", 2))
        if kind == "attn":
            kv = h // 3
            st.update(marks=[marks["rope", h], marks["rope", 6 + kv]], q=lambda t: qk[:, h, t * P:(t + 1) * P],
                      k=lambda k0, kn: qk[:, 6 + kv, k0:k0 + kn], v=lambda kt: v_a[:, kt, kv * P:(kv + 1) * P],
                      v_marks=marks["va"], bias=lambda i: mask[:, i * TOKENS:(i + 1) * TOKENS],
                      bias_ready=mix_consts, sink=g.col("sink", h))
            chunk = h
        else:
            st.update(marks=[marks["qm", h], marks["km", h]], q=lambda t: qm[:, h, t * P:(t + 1) * P],
                      k=lambda k0, kn: km[:, h, k0:k0 + kn], v=lambda kt: vm[:, kt, h * P:(h + 1) * P],
                      v_marks=marks["vm"], bias=None, bias_ready=None, sink=None)
            chunk = 12 + h

        def done(bank, out, m):
            branch.marks = g.split(branch.at(lambda t: t[:, chunk, :]), out, bank, m, marks["memT"])

        st["done"] = done
        yield from softmax_head(g, f"{kind}{h}", st)

    def attention():
        while ("qm", MEM_HEADS - 1) not in marks or "va" not in marks:
            yield
        yield from pipeline([head("mem", h) for h in range(MEM_HEADS)])
        yield from rope()
        yield from pipeline([head("attn", h) for h in range(Q_HEADS)])

    g.run(main(), [lru(), attention()])
    hT_free = (g.pe.sem, g.pe.count)
    all_branches = [(g.act.sem, g.act.count), (g.dve.sem, g.dve.count)]
    branch.marks = all_branches

    merged = Pair(hT.hi, hT.lo, [])

    acc, tmp = g.place("acc", [P, 2, TOKENS], at=g.addr(lru_a)), g.place("tmp", [P, 2, TOKENS], at=g.addr(lru_b))
    spans = (("p_attn", 0, 6), ("p_lru", 6, 6), ("p_mem", 12, 4))
    acc_free = [None, None]
    xr = g.place("x_res", [P, TILES, D], at=g.addr(qk))
    g.sp.wait(all_branches, hT_free)
    xr_ready = g.dma("x_res", xr[:, :, :], a["x"])
    g.dve.wait(all_branches)
    merged_marks = []
    for m_ in range(KD):
        A = acc[:, m_ % 2, :]
        for n, (key, first, chunks) in enumerate(spans):
            b, out, mk = g.fm_unit((key, m_), branch.at(lambda t: t[:, first:first + chunks, :]), chunks)
            gate = gates[:, n * KD + m_, :]
            g.dve.wait(mk, acc_free[m_ % 2] if n == 0 else None)
            dst = A if n == 0 else tmp[:, n % 2, :]
            m = g.dve.then(V.scalar_tensor_tensor(dst, gate, 1.0, out, ALU.add, ALU.mult))
            b.free = [m]
            if n:
                m = g.dve.then(V.tensor_tensor(A, A, dst, ALU.add))
        g.act.wait(hT_free)
        ms = g.split(merged.at(lambda t: t[:, m_, :]), A, None, m, scale=0.5)
        acc_free[m_ % 2] = ms[0]
        merged_marks = ms
    merged.marks = merged_marks
    project_out(g, "w_out", merged, xr, [xr_ready])


def project_out(g, key, lhs, res, res_marks):
    nc = g.nc
    marks = []
    for h in range(2):
        banks = [g.side_banks[2 * h + t] for t in range(TILES)]
        for b in banks:
            g.pe.wait(b.free)
        for u in range(4):
            m = g.tm_unit((key, h * 4 + u), lhs, 2 * u, 2, 512, [[b.t] for b in banks], u == 0, u == 3)
        g.dve.wait(m, *res_marks)
        for t, b in enumerate(banks):
            mk = g.dve.did(nc.vector.tensor_tensor(g.X[:, t, h * 512:(h + 1) * 512], b.t[:, :],
                                                   res[:, t, h * 512:(h + 1) * 512], ALU.add))
            b.free = [mk]
            marks.append(mk)
    g.X_marks = marks
    g.X_pieces = [((t, h), marks[h * TILES + t]) for h in range(2) for t in range(TILES)]




def peer(g, phase):
    nc, a = g.nc, g.dram
    V, S = nc.vector, nc.scalar
    g.top = phase
    experts = g.place("experts", [P, KEYS, TOKENS])
    h2T = g.pair("h2T", [P, KD, TOKENS])
    slot_T = g.place("slot_T", [P, 3, TOKENS])
    G = 4
    hot_at = g.addr(h2T.hi)
    HOTS = 3
    first_hot = [g.place(f"first_hot{i}", [P, G, P], at=hot_at + 2048 * i) for i in range(HOTS)]
    second_hot = [g.place(f"second_hot{i}", [P, G, P], at=hot_at + 2048 * (HOTS + i)) for i in range(HOTS)]
    ex = g.addr(experts)
    g.junk = g.place("squares2", [P, TILES, D], at=ex)
    late = ex + 70 * 1024
    g_late = [late]

    def in_late(name, shape, dtype=F32):
        t = g.place(name, shape, dtype, at=g_late[0])
        g_late[0] += 4 * int(np.prod(shape[1:]))
        assert g_late[0] <= ex + 128 * 1024
        return t

    HP = 2 * PEER_HEADS
    queries = in_late("queries", [P, HP, TOKENS])
    keys = in_late("sub_keys", [P, HP, KEYS])
    scores = in_late("key_scores", [P, HP, KEYS])
    top_v = in_late("top_v", [P, HP, TOPK])
    top_i = in_late("top_i", [P, HP, TOPK], U32)
    top_f = in_late("top_f", [P, HP, TOPK])
    pairs = in_late("pair_sums", [P, PEER_HEADS, TOPK, TOPK])
    hot = in_late("hot", [P, PEER_HEADS, TOPK, TOPK])
    best_v = in_late("best_v", [P, PEER_HEADS, TOPK])
    best_p = in_late("best_p", [P, PEER_HEADS, TOPK], U32)
    part_u = in_late("part_u", [P, PEER_HEADS, TOPK], U32)
    part_f = in_late("part_f", [P, PEER_HEADS, TOPK])
    picked = in_late("picked", [P, 3, PEER_HEADS, TOPK])
    sums = in_late("gate_sums", [P, PEER_HEADS])
    late_j = (late - ex) // 1024

    g.norm_to_fm(g.X, g.X_pieces, "g_ffn", h2T, "nf")
    norm_done = [(g.pe.sem, g.pe.count), (g.act.sem, g.act.count)]
    keys_ready = g.dma("keys", keys[:, :, :], a["sub_keys"].rearrange("p (a k) -> p a k", a=HP), norm_done)
    q_marks = []
    for i in range(HP):
        b, out, m = g.fm_unit(("peer_q", i), h2T, KD)
        g.act.wait(m)
        m = g.act.did(S.activation(queries[:, i, :], out, ACT.Copy))
        b.free = [m]
        q_marks = [m]
    topk_done = []

    def topk():
        for t in range(TILES):
            for b4 in range(4):
                b = g.side_banks[b4]
                g.pe.wait(b.free, q_marks, keys_ready)
                for j in range(4):
                    i = 4 * b4 + j
                    last = nc.tensor.matmul(b.t[:, j * P:(j + 1) * P], queries[:, i, t * P:(t + 1) * P],
                                            keys[:, i, :], start=True, stop=True)
                m = g.pe.did(last)
                g.act.wait(m, (g.dve.sem, g.dve.count) if t else None)
                m = g.act.did(S.activation(scores[:, 4 * b4:4 * b4 + 4, :],
                                           b.t[:, :].rearrange("p (a k) -> p a k", a=4), ACT.Copy))
                b.free = [m]
            g.dve.wait(m)
            yield
            for i in range(HP):
                top16(scores[:, i, :], top_v[:, i, :], top_i[:, i, :])
                yield
            g.dve.then(V.tensor_copy(top_f[:, :, :], top_i[:, :, :]))
            v4 = top_v[:, :, :].rearrange("p (h two) k -> p h two k", two=2)
            g.dve.then(V.tensor_tensor(pairs[:, :, :, :], v4[:, :, 0, :].unsqueeze(3).to_broadcast(list(pairs.shape)),
                                       v4[:, :, 1, :].unsqueeze(2).to_broadcast(list(pairs.shape)), ALU.add))
            for h in range(PEER_HEADS):
                top16(pairs[:, h, :, :].rearrange("p a b -> p (a b)"), best_v[:, h, :], best_p[:, h, :])
                yield
            f4 = top_f[:, :, :].rearrange("p (h two) k -> p h two k", two=2)
            for part in range(2):
                if part == 0:
                    g.dve.then(V.tensor_single_scalar(part_u[:, :, :], best_p[:, :, :], 4, ALU.logical_shift_right))
                else:
                    g.dve.then(V.tensor_single_scalar(part_u[:, :, :], best_p[:, :, :], 15, ALU.bitwise_and))
                g.dve.then(V.tensor_copy(part_f[:, :, :], part_u[:, :, :]))
                shape = list(hot.shape)
                g.dve.then(V.tensor_tensor(
                    hot[:, :, :, :], part_f[:, :, :].unsqueeze(3).to_broadcast(shape),
                    g.iota[:, 0:TOPK].unsqueeze(1).unsqueeze(1).to_broadcast(shape), ALU.is_equal))
                yield
                g.dve.then(V.tensor_tensor(hot[:, :, :, :], hot[:, :, :, :],
                                           f4[:, :, part, :].unsqueeze(2).to_broadcast(shape), ALU.mult))
                g.dve.then(V.tensor_reduce(picked[:, part, :, :], hot[:, :, :, :], AXIS_X, ALU.add))
                yield
            gate = picked[:, 2, :, :]
            m = g.dve.then(V.tensor_tensor(gate, best_v[:, :, :], best_v[:, :, 0:1].to_broadcast(list(best_v.shape)),
                                           ALU.subtract))
            g.act.wait(m)
            m = g.act.did(S.activation(gate, gate, ACT.Exp))
            g.dve.wait(m)
            g.dve.then(V.tensor_reduce(sums[:, :], gate, AXIS_X, ALU.add))
            g.dve.then(V.reciprocal(sums[:, :], sums[:, :]))
            m = g.dve.then(V.tensor_tensor(gate, gate, sums[:, :].unsqueeze(2).to_broadcast(list(best_v.shape)),
                                           ALU.mult))
            b = g.side_banks[4]
            g.pe.wait(b.free, m)
            for k in range(3):
                last = nc.tensor.transpose(b.t[:, k * P:(k + 1) * P], picked[:, k, :, :].rearrange("p a b -> p (a b)"),
                                           g.ident)
            m = g.pe.did(last)
            g.act.wait(m)
            m = g.act.did(S.activation(slot_T[:, :, t * P:(t + 1) * P],
                                       b.t[:, 0:3 * P].rearrange("p (a k) -> p a k", a=3), ACT.Copy))
            b.free = [m]
            g.dve.wait(m)
            yield
        topk_done.extend([m, (g.pe.sem, g.pe.count), (g.dve.sem, g.dve.count)])

    def top16(src, values, places):
        g.dve.then(V.max(values[:, 0:8], src))
        g.dve.then(V.max_index(places[:, 0:8], values[:, 0:8], src))
        g.dve.then(V.match_replace(src, values[:, 0:8], src, -3.0e38))
        g.dve.then(V.max(values[:, 8:16], src))
        g.dve.then(V.max_index(places[:, 8:16], values[:, 8:16], src))

    def activations():
        g.act.wait(norm_done)
        for j in range(KEYS):
            if j == late_j:
                while not topk_done:
                    yield
            b, out, m = g.fm_unit(("peer_u", j), h2T, KD)
            g.act.wait(m, list(topk_done) if j >= late_j else None)
            m = g.act.did(S.activation(experts[:, j, :], out, ACT.Gelu_apprx_tanh))
            b.free = [m]
            yield
        activations.mark = m

    g.run(activations(), [topk()])
    h2T_free = (g.pe.sem, g.pe.count)

    hot_free = [h2T_free] * HOTS
    g.dve.wait(activations.mark, topk_done)
    g.pool.wait(topk_done, g.base_ready)
    minus_key = g.place("minus_key", [P, TOKENS], at=hot_at + 4096 * HOTS)
    g.act.wait(topk_done, h2T_free)
    g.act.then(S.activation(minus_key[:, :], slot_T[:, 1, :], ACT.Copy, scale=-1.0))
    for n in range(TOKENS // G):
        fh, sh = first_hot[n % HOTS], second_hot[n % HOTS]
        g.pool.wait(hot_free[n % HOTS])
        t = n * G + G - 1
        g.pool.did(nc.gpsimd.tensor_scalar(fh[:, G - 1, :], g.iota, slot_T[:, 0, t:t + 1], slot_T[:, 2, t:t + 1],
                                           ALU.is_equal, ALU.mult))
        m2 = g.pool.did(nc.gpsimd.tensor_scalar(sh[:, G - 1, :], g.iota, slot_T[:, 1, t:t + 1], None, ALU.is_equal))
        g.act.wait(hot_free[n % HOTS])
        for k in range(G - 1):
            t = n * G + k
            m3 = g.act.did(S.activation(sh[:, k, :], g.iota, ACT.Abs, bias=minus_key[:, t:t + 1]))
        g.act.wait(m3)
        m3 = g.act.did(S.activation(sh[:, 0:G - 1, :], sh[:, 0:G - 1, :], ACT.Relu, scale=-1.0, bias=1.0))
        g.dve.wait(hot_free[n % HOTS])
        for k in range(G - 1):
            t = n * G + k
            m1 = g.dve.did(V.tensor_scalar(fh[:, k, :], g.iota, slot_T[:, 0, t:t + 1], slot_T[:, 2, t:t + 1],
                                           ALU.is_equal, ALU.mult))
        b = g.side_banks[n % 4]
        g.pe.wait(b.free, m1, m2, m3)
        for k in range(G):
            last = nc.tensor.matmul(b.t[:, k * P:(k + 1) * P], fh[:, k, :], sh[:, k, :], start=True, stop=True)
        m = g.pe.did(last)
        hot_free[n % HOTS] = m
        if n:
            apply_gates(g, experts, n - 1, G, gate_mark)
        gate_mark = m
    apply_gates(g, experts, TOKENS // G - 1, G, gate_mark)
    gated = (g.dve.sem, g.dve.count)

    epair = [g.pair(f"expert_pair{i}", [P, TOKENS], at=g.addr(h2T.hi) + i * 2048).at(lambda t: t[:, :]) for i in range(3)]
    banks = [[g.side_banks[2 * t + h] for h in range(2)] for t in range(TILES)]
    free = [(g.pe.sem, g.pe.count)] * 3
    g.act.wait(gated)

    def split_expert(j):
        ep = epair[j % 3]
        ep.marks = g.split(ep, experts[:, j, :], None, free[j % 3], gated)

    split_expert(0)
    split_expert(1)
    for bb in banks:
        for b in bb:
            g.pe.wait(b.free)
    for j in range(KEYS):
        if j + 2 < KEYS:
            split_expert(j + 2)
        ep = epair[j % 3]
        n, w = g.take(("peer_v", j))
        g.pe.wait(ep.marks)
        for t in range(TILES):
            for h in range(2):
                last = g.mm3(banks[t][h].t[:, :], ep.at(lambda x: x[:, t * P:(t + 1) * P]),
                             w.at(lambda x: x[:, h * 512:(h + 1) * 512]), j == 0, j == KEYS - 1)
        m = g.pe.did(last)
        g.used[n] = m
        free[j % 3] = m
    g.dve.wait(m, g.X_marks)
    marks = []
    for t in range(TILES):
        for h in range(2):
            mk = g.dve.did(V.tensor_tensor(g.X[:, t, h * 512:(h + 1) * 512], banks[t][h].t[:, :],
                                           g.X[:, t, h * 512:(h + 1) * 512], ALU.add))
            banks[t][h].free = [mk]
            marks.append(mk)
    g.X_marks = marks
    g.X_pieces = [((t, h), marks[t * 2 + h]) for t in range(TILES) for h in range(2)]

    gf = g.place("g_final", [P, D], at=g.addr(h2T.hi) + 8192)
    gf_ready = g.dma("g_final", gf[:, :], a["g_final"], m)
    g.junk = g.place("squares3", [P, TILES, D], at=ex)
    r, rm = g.rstd_tm(g.X, g.X_pieces, "nl")
    g.dve.wait(gf_ready)
    marks = []
    g.X_pieces = []
    for t in range(TILES):
        for h in range(2):
            cols = slice(h * 512, (h + 1) * 512)
            marks.append(g.dve.did(V.scalar_tensor_tensor(g.X[:, t, cols], g.X[:, t, cols], r[:, t:t + 1],
                                                          gf[:, cols], ALU.mult, ALU.mult)))
            g.X_pieces.append(((t, h), marks[-1]))
    g.X_marks = marks


def apply_gates(g, experts, n, G, mark):
    b = g.side_banks[n % 4]
    view = experts[:, :, n * G:(n + 1) * G]
    g.dve.wait(mark)
    m = g.dve.did(g.nc.vector.tensor_tensor(view, view, b.t[:, :].rearrange("p (t j) -> p j t", t=G), ALU.mult))
    b.free = [m]




def bias_tables(g, bias, at):
    nc, a = g.nc, g.dram
    consts = g.place("bias_consts", [P, 2 * SKEW], at=at)
    rb = g.place("rel_bias", [P, SWA_HEADS], at=at + 8 * SKEW)
    rbw = g.place("rel_bias_wide", [P, SWA_HEADS, P], at=at + 8 * SKEW + 32)
    row = g.place("bias_rows", [P, SWA_HEADS, SKEW], at=at + 8 * SKEW + 32 + 4096)
    m1 = g.dma("bias_consts", consts[:, :], a["bias_consts"], (g.pe.sem, g.pe.count), (g.act.sem, g.act.count), (g.dve.sem, g.dve.count))
    m2 = g.dma("rel_bias", rb[0:BUCKETS, :], a["rel_bias"])
    g.dve.wait(m2)
    m = g.dve.did(nc.vector.tensor_copy(rbw[0:BUCKETS, :, :], wide(rb[0:BUCKETS, :], P)))
    for h in range(SWA_HEADS):
        b = g.side_banks[h % 4]
        g.pe.wait(m, m1, b.free)
        mm = g.pe.did(nc.tensor.matmul(b.t[:, 0:SKEW], rbw[0:BUCKETS, h, :], consts[0:BUCKETS, 0:SKEW],
                                       start=True, stop=True))
        g.dve.wait(mm, m1)
        r = g.dve.did(nc.vector.tensor_tensor(row[:, h, :], b.t[:, 0:SKEW], consts[:, SKEW:], ALU.add))
        b.free = [r]
    scratch = nc.dram_tensor("bias_scratch", [SWA_HEADS * P * SKEW], F32, kind="Internal").ap()
    w = g.dma("bias_out", scratch.rearrange("(h p m) -> p h m", h=SWA_HEADS, p=P), row[:, :, :], r)
    for h in range(SWA_HEADS):
        start = h * P * SKEW + P - 1
        src = scratch[start:start + P * (SKEW - 1)].rearrange("(p m) -> p m", m=SKEW - 1)[:, 0:2 * P]
        ready = g.dma("bias_in", bias[:, h, :], src, w)
    return ready


def layer(g, l, places, rets):
    nc, a = g.nc, g.dram
    V, S = nc.vector, nc.scalar
    (hT, ys, qk, v_r, ga, cu, cv, gu, gv, sq, sk, sv, gates, Sbuf, PT, t1, t2, y_tm, ws, lnb) = places["all"]
    cos, sin, swap, decay, tril, half_ones, bias = places["consts"]
    c_ready, bias_ready = places["ready"]
    name = lambda s: f"{s}.{l}"
    before = [(g.pe.sem, g.pe.count), (g.act.sem, g.act.count), (g.dve.sem, g.dve.count), (g.pool.sem, g.pool.count)]
    ws_ready = g.dma("ws", ws[:, :], a["gmlp_ws"][l], before)
    lnb_ready = g.dma("lnb", lnb[:, :], a["gmlp_ln"][l], before)
    bs_ready = g.dma("bs", places["bs"][0:1, :], a["gmlp_bs"][l:l + 1, :], before)
    bs = places["bs"]
    g.junk = places["junk"]
    g.norm_to_fm(g.X, g.X_pieces, name("norm1"), hT, name("n1"))
    g.pool.wait(ws_ready, c_ready, before)
    for i in range(4):
        ws_masked = g.pool.did(nc.gpsimd.tensor_tensor(ws[:, i * P:(i + 1) * P], ws[:, i * P:(i + 1) * P], tril, ALU.mult))
    g.dve.wait(before)
    pads = g.dve.did(V.memset(cu[:, :, 0:TAPS2 - 1], 0.0))
    marks = {}

    def to_sbuf(key, i, dst, rhs=hT, func=ACT.Copy, after=None, **kw):
        b, out, m = g.fm_unit((name(key), i), rhs, KD)
        g.act.wait(m, after)
        m = g.act.did(S.activation(dst, out, func, **kw))
        b.free = [m]
        marks[key, i] = m

    def tm_to_sbuf(key, dst, units, chunks, width, tag=None):
        banks = [g.side_banks[0], g.side_banks[1]]
        for b in banks:
            g.pe.wait(b.free)
        for u in range(units):
            m = g.tm_unit((name(key), u), hT, u * chunks, chunks, width, [[b.t] for b in banks], u == 0, u == units - 1)
            if u < units - 1:
                yield
        g.act.wait(m)
        for t, b in enumerate(banks):
            e = g.act.did(S.activation(dst[:, t, :], b.t[:, 0:width], ACT.Copy))
            b.free = [e]
        marks[key] = e
        yield

    def main():
        for i in range(KM):
            to_sbuf("cg", i, cv[:, i, :], func=ACT.Tanh, scale=0.5)
            yield
        for i in range(KM):
            b, out, m = g.fm_unit((name("ca"), i), hT, KD)
            g.dve.wait(m, marks["cg", i], pads)
            m = g.dve.then(V.scalar_tensor_tensor(cu[:, i, TAPS2 - 1:], cv[:, i, :], 1.0, out, ALU.add, ALU.mult))
            b.free = [m]
            marks["cu", i] = g.dve.did(V.tensor_scalar(cu[:, i, TAPS2 - 1:], cu[:, i, TAPS2 - 1:], 0.5, None, ALU.mult))
            yield
        yield from tm_to_sbuf("gv", gv, 4, 2, 512)
        yield from tm_to_sbuf("rv", v_r, 4, 2, 512)
        yield from tm_to_sbuf("sv", sv, 1, 8, 128)
        for i in range(8):
            to_sbuf("rqk", i, qk[:, i, :])
            yield
        to_sbuf("sk", 0, sk[:, :])
        yield
        for i in range(4):
            to_sbuf("sq", i, sq[:, i, :])
            yield
        for i in range(4):
            to_sbuf("ga", i, ga[:, i, :])
            yield
        for i in range(4):
            to_sbuf("gu", i, gu[:, i, :])
            yield
        for i in range(32):
            to_sbuf("gate", i, gates[:, i, :], func=ACT.Tanh, scale=0.5)
            yield

    side_ready = {}

    def take_bank(i):
        b = g.side_banks[i]
        g.pe.wait(b.free)
        return b

    def gelu2(dst, tmp, marks_):
        g.dve.wait(marks_)
        g.dve.then(V.tensor_tensor(tmp, dst, dst, ALU.mult))
        g.dve.then(V.tensor_scalar(tmp, tmp, 0.044715, 1.0, ALU.mult, ALU.add))
        m = g.dve.then(V.tensor_tensor(tmp, tmp, dst, ALU.mult))
        g.act.wait(m)
        m = g.act.did(S.activation(tmp, tmp, ACT.Tanh, scale=float(np.sqrt(2 / np.pi))))
        g.dve.wait(m)
        return g.dve.then(V.scalar_tensor_tensor(dst, tmp, 1.0, dst, ALU.add, ALU.mult))

    def convolution():
        for i in range(KM):
            while ("cu", i) not in marks:
                yield
            g.dve.wait(marks["cu", i])
            w = lambda j: g.col(name("conv_w2"), j * KM + i)
            g.dve.then(V.tensor_scalar(cv[:, i, :], cu[:, i, 0:TOKENS], w(0), g.col(name("conv_b2"), i),
                                       ALU.mult, ALU.add))
            for j in range(1, TAPS2):
                m = g.dve.then(V.scalar_tensor_tensor(cv[:, i, :], cu[:, i, j:j + TOKENS], w(j), cv[:, i, :],
                                                      ALU.mult, ALU.add))
                if j % 4 == 0:
                    yield
            yield
        b = take_bank(4)
        g.pe.wait(m)
        for i in range(KM):
            last = nc.tensor.matmul(b.t[:, 0:TOKENS], g.ones, cv[:, i, :], start=(i == 0), stop=(i == KM - 1))
        mm = g.pe.did(last)
        g.dve.wait(mm)
        mean = t2[:, 0, :]
        g.dve.then(V.tensor_scalar(mean, b.t[:, 0:TOKENS], 1.0 / MIX, None, ALU.mult))
        for i in range(KM):
            m = g.dve.did(V.tensor_tensor(cv[:, i, :], cv[:, i, :], mean, ALU.subtract))
        g.act.wait(m)
        sqs = cu[:, :, 0:TOKENS]
        m = g.act.did(S.activation(sqs, cv[:, :, :], ACT.Square))
        yield
        g.pe.wait(m)
        for i in range(KM):
            last = nc.tensor.matmul(b.t[:, TOKENS:2 * TOKENS], g.ones, cu[:, i, 0:TOKENS], start=(i == 0),
                                    stop=(i == KM - 1))
        mm = g.pe.did(last)
        g.dve.wait(mm)
        var = t2[:, 1, :]
        m = g.dve.then(V.tensor_scalar(var, b.t[:, TOKENS:2 * TOKENS], 1.0 / MIX, EPS, ALU.mult, ALU.add))
        b.free = [m]
        g.act.wait(m)
        m = g.act.did(S.activation(var, var, ACT.Sqrt))
        g.dve.wait(m)
        g.dve.then(V.reciprocal(var, var))
        yield
        for i in range(KM):
            u, sg = cv[:, i, :], t2[:, 0, :]
            g.dve.then(V.tensor_tensor(u, u, var, ALU.mult))
            m = g.dve.then(V.tensor_scalar(u, u, g.col(name("cln_g"), i), g.col(name("cln_b"), i), ALU.mult, ALU.add))
            g.act.wait(m)
            m = g.act.did(S.activation(sg, u, ACT.Tanh, scale=0.5))
            g.dve.wait(m)
            m = g.dve.then(V.scalar_tensor_tensor(u, sg, 1.0, u, ALU.add, ALU.mult))
            ys.marks = g.split(ys.at(lambda t: t[:, 4 + i, :]), u, None, m, scale=0.5)
            yield

    def gating():
        while "gv" not in marks:
            yield
        for t in range(TILES):
            v, tmp = gv[:, t, :], y_tm[:, 0, :]
            m = gelu2(v, tmp, marks["gv"])
            yield
            st, ag = g.small(name(f"gst{t}"), 6), g.small(name(f"gag{t}"), 2)
            g.dve.then(V.bn_stats(st, v))
            g.dve.then(V.bn_aggr(ag, st))
            m = g.dve.then(V.tensor_scalar(ag[:, 1:2], ag[:, 1:2], 0.25, EPS, ALU.mult, ALU.add))
            g.act.wait(m)
            m = g.act.did(S.activation(ag[:, 1:2], ag[:, 1:2], ACT.Sqrt, scale=4.0))
            g.dve.wait(m)
            g.dve.then(V.reciprocal(ag[:, 1:2], ag[:, 1:2]))
            g.dve.then(V.tensor_scalar(v, v, ag[:, 0:1], ag[:, 1:2], ALU.subtract, ALU.mult))
            g.dve.wait(lnb_ready)
            g.dve.then(V.tensor_tensor(v, v, lnb[:, 0:MIX], ALU.mult))
            m = g.dve.then(V.tensor_tensor(v, v, lnb[:, MIX:], ALU.add))
            marks["gvn", t] = m
            yield
        while ("gu", KM - 1) not in marks:
            yield
        for i in range(KM):
            b = take_bank(4)
            g.pe.wait(marks["gvn", 1], ws_masked, bs_ready, g.base_ready)
            for t in range(TILES):
                out = b.t[:, t * P:(t + 1) * P]
                nc.tensor.matmul(out, gv[:, t, i * P:(i + 1) * P], ws[:, i * P:(i + 1) * P], start=True, stop=False)
                last = nc.tensor.matmul(out, g.ones[0:1, :], bs[0:1, i * P:(i + 1) * P], start=False, stop=True)
            mm = g.pe.did(last)
            u = gu[:, i, :]
            m = gelu2(u, t1[:, 0, :], marks["gu", i])
            g.dve.wait(mm)
            m = g.dve.then(V.tensor_tensor(u, b.t[:, 0:TOKENS], u, ALU.mult))
            b.free = [m]
            ys.marks = g.split(ys.at(lambda t: t[:, 8 + i, :]), u, None, m, scale=0.5)
            yield

    def retention():
        for c in range(8):
            while ("rqk", c) not in marks:
                yield
            b = take_bank(3)
            g.pe.wait(marks["rqk", c], c_ready)
            m = g.pe.did(nc.tensor.matmul(b.t[:, 0:TOKENS], swap, qk[:, c, :], start=True, stop=True))
            g.pool.wait(m, c_ready)
            m2 = g.pool.did(nc.gpsimd.tensor_tensor(qk[:, c, :], qk[:, c, :], cos, ALU.mult))
            g.dve.wait(m, c_ready)
            m3 = g.dve.then(V.tensor_tensor(g.rope_tmp, b.t[:, 0:TOKENS], sin, ALU.mult))
            b.free = [m3]
            g.dve.wait(m2)
            marks["rot", c] = g.dve.then(V.tensor_tensor(qk[:, c, :], qk[:, c, :], g.rope_tmp, ALU.add))
            yield
        for h in range(RET_HEADS):
            b = take_bank(2)
            g.pe.wait(marks["rot", h], marks["rot", 4 + h])
            nc.tensor.matmul(b.t[:, 0:TOKENS], qk[:, 4 + h, 0:P], qk[:, h, :], start=True, stop=True)
            last = nc.tensor.matmul(b.t[:, TOKENS:TOKENS + P], qk[:, 4 + h, P:], qk[:, h, P:], start=True, stop=True)
            mm = g.pe.did(last)
            g.dve.wait(mm, marks.get("ret_y"))
            g.dve.did(V.tensor_tensor(PT[:, 0:TOKENS], b.t[:, 0:TOKENS], decay[:, h, :], ALU.mult))
            m = g.dve.did(V.tensor_tensor(PT[:, TOKENS:TOKENS + P], b.t[:, TOKENS:TOKENS + P], decay[:, h, 0:P],
                                          ALU.mult))
            b.free = [m]
            yield
            b = take_bank(3)
            g.pe.wait(m, marks["rv"])
            v = lambda t: v_r[:, t, h * P:(h + 1) * P]
            nc.tensor.matmul(b.t[:, 0:P], PT[:, 0:P], v(0), start=True, stop=True)
            nc.tensor.matmul(b.t[:, P:2 * P], PT[:, P:2 * P], v(0), start=True, stop=False)
            last = nc.tensor.matmul(b.t[:, P:2 * P], PT[:, 2 * P:3 * P], v(1), start=False, stop=True)
            mm = g.pe.did(last)
            marks["ret_y"] = mm
            g.dve.wait(mm)
            for t in range(TILES):
                y = t1[:, t, 0:P]
                st, ag = g.small(name(f"rst{h}{t}"), 6), g.small(name(f"rag{h}{t}"), 2)
                g.dve.then(V.bn_stats(st, b.t[:, t * P:(t + 1) * P]))
                g.dve.then(V.bn_aggr(ag, st))
                m = g.dve.then(V.tensor_scalar(ag[:, 1:2], ag[:, 1:2], EPS, None, ALU.add))
                g.act.wait(m)
                m = g.act.did(S.activation(ag[:, 1:2], ag[:, 1:2], ACT.Sqrt))
                g.dve.wait(m, marks.get(("yT", t)))
                g.dve.then(V.reciprocal(ag[:, 1:2], ag[:, 1:2]))
                m = g.dve.then(V.tensor_scalar(y_tm[:, t, 0:P] if False else g.ret_n[:, t, :], b.t[:, t * P:(t + 1) * P],
                                               ag[:, 0:1], ag[:, 1:2], ALU.subtract, ALU.mult))
            b.free = [m]
            yield
            b = take_bank(2)
            g.pe.wait(m)
            for t in range(TILES):
                last = nc.tensor.transpose(b.t[:, t * P:(t + 1) * P], g.ret_n[:, t, :], g.ident)
            mm = g.pe.did(last)
            marks["yT", 0] = marks["yT", 1] = mm
            while ("ga", h) not in marks:
                yield
            g.act.wait(marks["ga", h])
            sg = g.ret_s
            g.act.wait(marks.get("ret_out"))
            m = g.act.did(S.activation(sg, ga[:, h, :], ACT.Tanh, scale=0.5))
            g.dve.wait(m, mm)
            g.dve.then(V.scalar_tensor_tensor(ga[:, h, :], sg, 1.0, ga[:, h, :], ALU.add, ALU.mult))
            m = g.dve.then(V.scalar_tensor_tensor(ga[:, h, :], b.t[:, 0:TOKENS], g.col(name("gn"), h), ga[:, h, :],
                                                  ALU.mult, ALU.mult))
            marks["ret_out"] = m
            b.free = [m]
            ys.marks = g.split(ys.at(lambda t: t[:, h, :]), ga[:, h, :], None, m, scale=0.5)
            yield

    def swa_norm(x, mark, gain, extra):
        g.act.wait(mark)
        sqv = g.swa_t[:, 0, :]
        g.act.wait((g.pe.sem, g.pe.count))
        m = g.act.did(S.activation(sqv, x, ACT.Square))
        b = take_bank(1)
        g.pe.wait(m, c_ready)
        m = g.pe.did(nc.tensor.matmul(b.t[:, 0:TOKENS], half_ones, sqv, start=True, stop=True))
        g.dve.wait(m)
        r = g.swa_t[:, 1, :]
        m = g.dve.then(V.tensor_scalar(r, b.t[:, 0:TOKENS], 1.0 / SWA_DIM, EPS, ALU.mult, ALU.add))
        b.free = [m]
        g.act.wait(m)
        m = g.act.did(S.activation(r, r, ACT.Sqrt))
        g.dve.wait(m)
        g.dve.then(V.reciprocal(r, r))
        return g.dve.then(V.scalar_tensor_tensor(x, x, gain, r, ALU.mult, ALU.mult))

    S_free, PT_free = [[None], [None]], [None]

    def swa_head(i, c, half):
        h = c + 4 * half
        rows = slice(half * SWA_DIM, (half + 1) * SWA_DIM)
        segments = [(0, 0, P), (1, 0, TOKENS)]
        st = dict(bank=i % 2, turn_bank=2, out_bank=3, queries=TOKENS, scale=SWA_DIM ** -0.5, segments=segments,
                  S=Sbuf[i % 2], S_free=S_free[i % 2], PT=PT, PT_free=PT_free, mx=g.small(name(f"smx{i}"), 2),
                  den=g.small(name(f"sden{i}"), 2), es=g.small(name(f"ses{i}"), 2),
                  marks=[marks["sqn", c], marks["skn"]], q=lambda t: sq[rows, c, t * P:(t + 1) * P],
                  k=lambda k0, kn: sk[rows, k0:k0 + kn], v=lambda kt: sv[:, kt, :], v_marks=marks["sv"],
                  bias=lambda s: bias[:, h, P:2 * P] if s == 0 else bias[:, h, :], bias_ready=bias_ready,
                  sink=g.col(name("sinks2"), h))

        def done(bank, out, m):
            part = ys.at(lambda t: t[rows, 12 + c, :])
            ys.marks = g.split(part, out[rows, :], bank, m)

        st["done"] = done
        yield from softmax_head(g, f"swa{h}", st)

    def swa():
        while ("sk", 0) not in marks or ("gvn", 1) not in marks:
            yield
        g.act.wait(marks["gvn", 1], marks["ret_out"])
        marks["skn"] = swa_norm(sk[:, :], marks["sk", 0], g.col(name("k_g")), 1.0)
        yield
        for c in range(4):
            while ("sq", c) not in marks:
                yield
            marks["sqn", c] = swa_norm(sq[:, c, :], marks["sq", c], g.col(name("q_g")), 1.0)
            yield
        yield from pipeline([swa_head(2 * c + half, c, half) for c in range(4) for half in range(2)])

    def sides():
        yield from retention()
        yield from swa()

    g.run(main(), [convolution(), gating(), sides()])
    done = [(g.pe.sem, g.pe.count), (g.act.sem, g.act.count), (g.dve.sem, g.dve.count)]
    ys.marks = done

    mix = Pair(hT.hi, hT.lo, [])
    acc, tmp = t1, t2
    acc_free = [None, None]
    g.dve.wait(done)
    g.act.wait(done)
    for i in range(KD):
        A = acc[:, i % 2, :]
        for n in range(BRANCHES2):
            b, out, mk = g.fm_unit((name("branch"), i * BRANCHES2 + n), ys.at(lambda t: t[:, 4 * n:4 * n + 4, :]), KM)
            g.dve.wait(mk, acc_free[i % 2] if n == 0 else None)
            dst = A if n == 0 else tmp[:, n % 2, :]
            m = g.dve.then(V.scalar_tensor_tensor(dst, gates[:, n * KD + i, :], 1.0, out, ALU.add, ALU.mult))
            b.free = [m]
            if n:
                m = g.dve.then(V.tensor_tensor(A, A, dst, ALU.add))
        ms = g.split(mix.at(lambda t: t[:, i, :]), A, None, m, scale=0.5)
        acc_free[i % 2] = ms[0]
    mix.marks = ms
    project_out(g, name("w_out"), mix, g.X, [])

    g.norm_to_fm(g.X, g.X_pieces, name("norm2"), hT, name("n2"))
    hidden = places["hidden"]
    g.act.wait(g.X_marks)
    g.stream_banks += g.side_banks[:4]
    for i in range(KF):
        b, out, m = g.fm_unit((name("gt"), i), hT, KD)
        g.act.wait(m, acc_free[i % 2])
        sg = t1[:, i % 2, :]
        m = g.act.did(S.activation(sg, out, ACT.Tanh, scale=0.5))
        g.dve.wait(m)
        u = t2[:, i % 2, :]
        m = g.dve.then(V.scalar_tensor_tensor(u, sg, 1.0, out, ALU.add, ALU.mult))
        b.free = [m]
        b, out, m = g.fm_unit((name("up"), i), hT, KD)
        g.dve.wait(m)
        m = g.dve.then(V.tensor_tensor(u, u, out, ALU.mult))
        b.free = [m]
        ms = g.split(hidden.at(lambda t: t[:, i, :]), u, None, m, scale=0.5)
        acc_free[i % 2] = ms[1]
    hidden.marks = ms
    g.stream_banks = g.stream_banks[:3]
    banks = [[g.side_banks[2 * t + h] for h in range(2)] for t in range(TILES)]
    for bb in banks:
        for b in bb:
            g.pe.wait(b.free)
    for i in range(KF):
        m = g.tm_unit((name("ffn_out"), i), hidden, i, 1, 1024, [[b.t for b in bb] for bb in banks], i == 0, i == KF - 1)
    g.dve.wait(m)
    mk = []
    for t in range(TILES):
        for h in range(2):
            x = g.dve.did(V.tensor_tensor(g.X[:, t, h * 512:(h + 1) * 512], banks[t][h].t[:, :],
                                          g.X[:, t, h * 512:(h + 1) * 512], ALU.add))
            banks[t][h].free = [x]
            mk.append(x)
    g.X_marks = mk
    g.X_pieces = [((t, h), mk[t * 2 + h]) for t in range(TILES) for h in range(2)]


def layers(g, phase):
    nc, a = g.nc, g.dram
    g.top = phase
    n_consts = a["layer_consts"].shape[-1]
    lc = g.place("layer_consts", [P, n_consts])
    widths = {"ret_cos": TOKENS, "ret_sin": TOKENS, "swap2": P, "decay": RET_HEADS * TOKENS, "tril": P, "half_ones": P}
    at, c = 0, {}
    for n in LAYER_CONSTS:
        c[n] = lc[:, at:at + widths[n]]
        at += widths[n]
    bias = g.place("bias", [P, SWA_HEADS, 2 * P])
    hT = g.pair("hT2", [P, KD, TOKENS])
    t1, t2 = g.place("t1b", [P, 2, TOKENS]), g.place("t2b", [P, 2, TOKENS])
    overlay = g.top
    ys = g.pair("ys", [P, 16, TOKENS])
    qk = g.place("ret_qk", [P, 8, TOKENS])
    junk = g.place("squares4", [P, TILES, D], at=g.addr(qk))
    v_r = g.place("ret_v", [P, TILES, MIX])
    ga = g.place("ret_gate", [P, KM, TOKENS])
    cu = g.place("conv_in", [P, KM, TAPS2 - 1 + TOKENS])
    cv = g.place("conv_out", [P, KM, TOKENS])
    gu = g.place("gmlp_u", [P, KM, TOKENS])
    gv = g.place("gmlp_v", [P, TILES, MIX])
    sq = g.place("swa_q", [P, KM, TOKENS])
    sk = g.place("swa_k", [P, TOKENS])
    sv = g.place("swa_v", [P, TILES, P])
    gates = g.place("gates2", [P, 32, TOKENS])
    Sbuf = [g.place(f"S2{i}", [P, 384]) for i in range(2)]
    PT = g.place("PT2", [P, 512])
    g.rope_tmp = g.place("rope_tmp2", [P, TOKENS])[:, :]
    g.swa_t = g.place("swa_t", [P, 2, TOKENS])
    g.ret_n = g.place("ret_n", [P, TILES, P], at=g.addr(g.swa_t))
    g.ret_s = g.place("ret_s", [P, TOKENS], at=g.addr(g.swa_t) + 1024)[:, :]
    y_tm = g.place("gelu_tmp", [P, 1, MIX], at=g.addr(ys.lo) + 14 * 1024)
    lnb = g.place("gmlp_ln", [P, 2 * MIX], at=g.addr(ys.hi) + 12 * 1024)
    ws = g.place("gmlp_ws", [P, 4 * P])
    bs = g.place("gmlp_bs", [P, 4 * P])
    hidden = g.pair("hidden", [P, KF, TOKENS], at=overlay)
    assert overlay + 2 * 4 * KF * TOKENS <= g.addr(gates), "hidden must not reach"
    c_ready = g.dma("layer_consts", lc[:, :], a["layer_consts"])
    bias_ready = bias_tables(g, bias, g.addr(gates))
    places = {"all": (hT, ys, qk, v_r, ga, cu, cv, gu, gv, sq, sk, sv, gates, Sbuf, PT, t1, t2, y_tm, ws, lnb),
              "consts": (c["ret_cos"], c["ret_sin"], c["swap2"],
                         c["decay"].rearrange("p (h t) -> p h t", h=RET_HEADS), c["tril"], c["half_ones"], bias),
              "ready": (c_ready, bias_ready), "bs": bs, "junk": junk, "hidden": hidden}
    g.act.wait(bias_ready)
    small = g.small_at
    for l in range(LAYERS):
        layer(g, l, places, None)
        g.small_at = small



SOURCES = (
    ("km", "w_km", 4), ("vm", "w_vm", 4), ("va", "w_va", 2), ("xl", "w_xl", 6), ("qm", "w_qm", 4),
    ("qk", "w_qk", 8), ("gl", "w_gl", 6), ("gate", "w_gate", 24))


def stream_plan(a):
    plan = []

    def add(key, array, n=None):
        src = a[array]
        for i in range(src.shape[0]):
            plan.append(((key, i), src[i]))

    for key, array, n in SOURCES:
        add(key, array)
    for i in range(KD):
        for n in ("p_attn", "p_lru", "p_mem"):
            plan.append(((n, i), a[n][i]))
    add("w_out", "w_out")
    add("peer_q", "peer_q")
    add("peer_u", "peer_u")
    add("peer_v", "peer_v")
    for l in range(LAYERS):
        for key in ("cg", "ca", "gv", "rv", "sv", "rqk", "sk", "sq", "ga", "gu", "gate"):
            add(f"{key}.{l}", f"{key}.{l}")
        for i in range(KD):
            for n in range(BRANCHES2):
                plan.append(((f"branch.{l}", i * BRANCHES2 + n), a[f"branch.{l}"][n * KD + i]))
        add(f"w_out.{l}", f"w_out.{l}")
        for i in range(KF):
            plan.append(((f"gt.{l}", i), a[f"gt.{l}"][i]))
            plan.append(((f"up.{l}", i), a[f"up.{l}"][i]))
        add(f"ffn_out.{l}", f"ffn_out.{l}")
    return plan


def build(nc, a, out):
    g = Program(nc, a, out)
    cols = g.place("cols", [P, COLS_N])
    g.cols = cols
    base = g.place("base_consts", [P, 2 * P + 1])
    g.ident, g.iota, g.inv_freq = base[:, 0:P], base[:, P:2 * P], base[:, 2 * P:2 * P + 1]
    ones = g.place("ones", [P, P])
    g.smalls = g.place("smalls", [P, 400])
    g.small_at = 0
    g.X = g.place("X", [P, TILES, D])
    g.diag, g.diag_free = g.place("diag_rms", [P, TILES, P]), None
    m = [g.dma("cols", cols[:, :], a["cols"]), g.dma("base_consts", base[:, :], a["base_consts"])]
    g.ones = ones[:, :]
    m.append(g.dve.did(nc.vector.memset(ones[:, :], 1.0)))
    g.base_ready = m
    for q in (g.pe, g.act, g.dve, g.pool):
        q.wait(m)
    g.start_stream(stream_plan(a))
    phase = (g.top + 31) // 32 * 32
    g.junk = None
    g.mix_phase = phase
    mixer(g, phase)
    g.barrier()
    peer(g, phase)
    g.barrier()
    layers(g, phase)
    g.writes_out.append(g.dma("out", out, g.X[:, :, :], g.X_marks))
    g.sp.wait(g.writes_out)




def lay_out(inp):
    n = {k: np.asarray(v) for k, v in inp.items()}
    d = {}
    c = shape_constants()
    d["base_consts"] = pack(c, BASE_CONSTS)
    d["mix_consts"] = pack(c, MIX_CONSTS)
    d["layer_consts"] = pack(c, LAYER_CONSTS)
    d["bias_consts"] = pack(c, BIAS_CONSTS)

    def tm(x):
        return np.ascontiguousarray(x[0].reshape(TILES, P, D).transpose(1, 0, 2))

    d["x"], d["mem"] = tm(n["x"]), tm(n["mem"])
    d["positions"] = np.ascontiguousarray(np.broadcast_to(n["positions"], (P, TOKENS)))
    w = n["w_in"][0]
    o = np.cumsum([0, 768, 256, 256, 768, 768, 512, 3072])
    cut = lambda i, j=None: w[:, o[i]:o[i + 1 if j is None else j]]
    d["w_qk"], d["w_va"], d["w_xl"], d["w_gl"] = fm_units(cut(0, 2)), tm_units(cut(2), 4, 256), fm_units(cut(3)), fm_units(cut(4))
    d["w_qm"], d["w_gate"] = fm_units(cut(5)), fm_units(cut(6))
    kv = n["w_mem_kv"][0]
    d["w_km"], d["w_vm"] = fm_units(kv[:, :512]), tm_units(kv[:, 512:], 2, 512)
    for k in ("p_attn", "p_lru", "p_mem"):
        d[k] = fm_units(n[k][0])
    d["w_out"] = tm_units(n["w_out"][0], 2, 512)
    lw = np.stack([n["lru_wr"][0], n["lru_wi"][0]])
    d["lru_w"] = np.ascontiguousarray(lw.reshape(24, P, P).transpose(1, 0, 2).reshape(P, -1))
    d["peer_q"] = fm_units(n["w_peer_q"][0])
    d["sub_keys"] = np.ascontiguousarray(n["peer_sub_keys"][0].reshape(16, KEYS, P).transpose(2, 0, 1).reshape(P, -1))
    d["peer_u"] = np.ascontiguousarray(
        n["peer_u"][0].reshape(KEYS, KEYS, KD, P).transpose(1, 3, 2, 0).reshape(KEYS, P, KD * KEYS))
    d["peer_v"] = np.ascontiguousarray(n["peer_v"][0].reshape(KEYS, KEYS, D).transpose(1, 0, 2))
    d["g_final"] = np.ascontiguousarray(np.broadcast_to(n["g_final"], (P, D)))
    d["rel_bias"] = n["rel_bias_2"]

    def rows(x):
        return np.broadcast_to(x, (P,) + x.shape)

    parts = {"g_mix": columns(n["g_mix"]), "g_mem": columns(n["g_mem"]), "gate_b": columns(n["gate_b"]),
             "conv_w": columns(n["conv_w"]), "conv_b": columns(n["conv_b"]), "lru_br": columns(n["lru_br"]),
             "lru_bi": columns(n["lru_bi"]), "lam": columns(n["lru_lambda"]), "g_ffn": columns(n["g_ffn"]),
             "sink": rows(n["attn_sink"][0])}
    w_in, wb, wf = n["w_in_2"], n["w_branch_2"], n["w_ffn_in_2"]
    for l in range(LAYERS):
        o = np.cumsum([0, 1024, 512, 512, 512, 512, 512, 512, 512, 128, 128, 4096])
        w = w_in[l]
        cut = lambda i: w[:, o[i]:o[i + 1]]
        d[f"rqk.{l}"], d[f"rv.{l}"], d[f"ga.{l}"] = fm_units(cut(0)), tm_units(cut(1), 2, 512), fm_units(cut(2))
        d[f"ca.{l}"], d[f"cg.{l}"] = fm_units(cut(3)), fm_units(cut(4))
        d[f"gu.{l}"], d[f"gv.{l}"] = fm_units(cut(5)), tm_units(cut(6), 2, 512)
        d[f"sq.{l}"], d[f"sk.{l}"], d[f"sv.{l}"] = fm_units(swa_q_columns(cut(7))), fm_units(cut(8)), tm_units(cut(9), 8, 128)
        d[f"gate.{l}"] = fm_units(cut(10))
        b = wb[l].copy()
        b[3] = b[3].reshape(SWA_HEADS, SWA_DIM, D)[SWA_ORDER].reshape(MIX, D)
        d[f"branch.{l}"] = np.concatenate([fm_units(b[i]) for i in range(BRANCHES2)])
        d[f"w_out.{l}"] = tm_units(n["w_out_2"][l], 2, 512)
        d[f"gt.{l}"], d[f"up.{l}"] = fm_units(wf[l][:, :D_FF]), fm_units(wf[l][:, D_FF:])
        d[f"ffn_out.{l}"] = np.ascontiguousarray(n["w_ffn_out_2"][l].reshape(KF, P, D))
        parts[f"norm1.{l}"], parts[f"norm2.{l}"] = columns(n["norm1_g_2"][l]), columns(n["norm2_g_2"][l])
        parts[f"gn.{l}"] = columns(n["ret_gn_g_2"][l])
        parts[f"conv_w2.{l}"] = columns(n["conv_w_2"][l, :, 0])
        parts[f"conv_b2.{l}"] = columns(n["conv_b_2"][l])
        parts[f"cln_g.{l}"], parts[f"cln_b.{l}"] = columns(n["conv_ln_g_2"][l]), columns(n["conv_ln_b_2"][l])
        parts[f"q_g.{l}"] = np.tile(n["swa_q_g_2"][l], 2)[:, None]
        parts[f"k_g.{l}"] = np.tile(n["swa_k_g_2"][l], 2)[:, None]
        parts[f"sinks2.{l}"] = rows(n["swa_sinks_2"][l])
    d["cols"] = np.ascontiguousarray(np.concatenate([parts[k] for k in COLS], axis=1))
    d["gmlp_ws"] = np.ascontiguousarray(n["gmlp_ws_2"].transpose(0, 3, 1, 2).reshape(LAYERS, P, -1))
    d["gmlp_bs"] = n["gmlp_bs_2"].reshape(LAYERS, -1)
    ln = np.concatenate([n["gmlp_ln_g_2"], n["gmlp_ln_b_2"]], axis=1)
    d["gmlp_ln"] = np.ascontiguousarray(np.broadcast_to(ln[:, None, :], (LAYERS, P, 2 * MIX)))
    return d


def kernel(**inputs):
    import concourse.bacc as _bacc
    from concourse.bass_utils import run_bass_kernel_spmd as _run

    nc = _bacc.Bacc("TRN2", target_bir_lowering=False, num_devices=1)
    arrays, args = {}, {}
    for name, x in lay_out(inputs).items():
        dram = "in_" + name.replace(".", "_") + "_dram"
        arrays[dram] = x
        args[name] = nc.dram_tensor(dram, x.shape, mybir.dt.from_np(x.dtype), kind="ExternalInput").ap()
    out = nc.dram_tensor("out_dram", (P, TILES, D), F32, kind="ExternalOutput").ap()
    build(nc, args, out)
    r = _run(nc, [arrays], core_ids=[0])
    got = r.results[0]["out_dram"]
    return np.ascontiguousarray(got.transpose(1, 0, 2)).reshape(1, TOKENS, D)
```

```python
import numpy as np

import concourse.bass as bass
from concourse import mybir

ALU = mybir.AluOpType
ACT = mybir.ActivationFunctionType
AXIS_X = mybir.AxisListType.X
F32 = mybir.dt.float32
F32R = mybir.dt.float32r
U32 = mybir.dt.uint32
I32 = mybir.dt.int32

P = 128
TOKENS, D = 256, 1024
TILES = TOKENS // P
KD = D // P
EPS = 1e-6
MASKED = -1e30
HEAD = 128
Q_HEADS, KV_HEADS, MEM_HEADS = 6, 2, 4
LRU_BLOCKS, CONV_TAPS, CONV_LEFT = 6, 4, 2
LRU_BATCH = 2
BRANCHES = 3
ROPE_DIM, ROPE_THETA = 32, 500000.0
WINDOW = 128
PEER_HEADS, KEYS, TOPK = 8, 128, 16
SLOTS = PEER_HEADS * TOPK
LRU_C = 8.0
LAYERS = 2
MIX = 512
KM = MIX // P
RET_HEADS = 4
TAPS2 = 31
SWA_HEADS, SWA_DIM, SWA_WINDOW = 8, 64, 128
BUCKETS = 32
BRANCHES2 = 4
BRANCH_ORDER = (0, 1, 3, 2)
CONV_STEPS_FIRST = 26
D_FF = 2816
KF = D_FF // P
KEEP_WARM = 8
DVE_EVERY_BESIDE_SIDE_WORK, DVE_EVERY_ALONE = 8, 1
SKEW = 384



def fm_units(w):
    k, n = w.shape
    return np.ascontiguousarray(
        w.reshape(k // P, P, n // P, P).transpose(2, 1, 0, 3).reshape(n // P, P, (k // P) * P))


def fm_unit_pairs(w):
    u = fm_units(w)
    return np.ascontiguousarray(u.reshape(len(u) // 2, 2, P, -1).transpose(0, 2, 1, 3).reshape(len(u) // 2, P, -1))


def tm_units(w, chunks, width):
    k, n = w.shape
    a = w.reshape(k // P // chunks, chunks, P, n // width, width).transpose(3, 0, 2, 1, 4)
    return np.ascontiguousarray(a.reshape(-1, P, chunks * width))


def columns(v):
    v = np.asarray(v)
    return v.reshape(-1, P).T


SWA_ORDER = [h for c in range(4) for h in (c, c + 4)]


def swa_q_columns(w):
    return w.reshape(w.shape[0], SWA_HEADS, SWA_DIM)[:, SWA_ORDER].reshape(w.shape[0], -1)


COLS = {}
COLS_N = 0


def _col(name, n):
    global COLS_N
    COLS[name] = (COLS_N, n)
    COLS_N += n


for _n, _w in (("g_mix", KD), ("g_mem", KD), ("gate_b", 24), ("conv_w", 24), ("conv_b", 6), ("lru_br", 12),
               ("lru_bi", 12), ("lam", 12), ("g_ffn", KD), ("sink", Q_HEADS)):
    _col(_n, _w)
for _l in range(LAYERS):
    for _n, _w in (("norm1", KD), ("gn", KM), ("conv_w2", TAPS2 * KM), ("conv_b2", KM), ("cln_g", KM),
                   ("cln_b", KM), ("q_g", 1), ("k_g", 1), ("norm2", KD), ("sinks2", SWA_HEADS)):
        _col(f"{_n}.{_l}", _w)


def bucket_of(dist):
    d = np.maximum(dist, 1).astype(np.float32)
    large = 16 + (np.log(d / np.float32(16)) / np.float32(np.log(8.0)) * np.float32(16)).astype(np.int32)
    return np.where(dist < 16, dist, np.minimum(large, BUCKETS - 1))


def shape_constants():
    f = np.float32
    p = np.arange(P)
    c = {}
    c["ident"] = np.eye(P, dtype=f)
    c["iota"] = np.broadcast_to(p.astype(f), (P, P)).copy()
    half = ROPE_DIM // 2
    inv = (f(ROPE_THETA) ** (-np.arange(0, ROPE_DIM, 2, dtype=f) / f(ROPE_DIM))).astype(f)
    c["inv_freq"] = np.concatenate([inv, inv, np.zeros(P - ROPE_DIM, f)])[:, None].copy()
    swap = np.zeros((P, P), f)
    for m in range(half):
        swap[m + half, m] = -1
        swap[m, m + half] = 1
    c["swap1"] = swap
    q = np.arange(TOKENS)
    ok = np.abs(q[None, :] - q[:, None]) <= WINDOW
    m = np.where(ok, 0, MASKED).astype(f)
    c["mask1"] = m.reshape(TILES, P, TOKENS).transpose(1, 0, 2).reshape(P, -1).copy()
    hh = P // 2
    inv2 = f(10000.0) ** (-np.arange(hh, dtype=f) / f(hh))
    ang = np.arange(TOKENS).astype(f)[:, None] * inv2[None, :]
    c["ret_cos"] = np.tile(np.cos(ang).T, (2, 1)).astype(f)
    c["ret_sin"] = np.tile(np.sin(ang).T, (2, 1)).astype(f)
    swap = np.zeros((P, P), f)
    for m_ in range(hh):
        swap[m_ + hh, m_] = -1
        swap[m_, m_ + hh] = 1
    c["swap2"] = swap
    gamma = 1.0 - 2.0 ** (-5.0 - np.arange(RET_HEADS, dtype=np.float64))
    diff = np.arange(TOKENS)[None, :] - p[:, None]
    dec = [np.where(diff >= 0, g ** np.maximum(diff, 0), 0) * P ** -0.5 for g in gamma]
    c["decay"] = np.stack(dec, 1).astype(f).reshape(P, -1)
    c["tril"] = (p[None, :] >= p[:, None]).astype(f)
    c["half_ones"] = np.kron(np.eye(2), np.ones((SWA_DIM, SWA_DIM))).astype(f)
    dist = 2 * P - 1 - np.arange(SKEW)
    inside = (dist >= 0) & (dist < SWA_WINDOW)
    one = np.zeros((P, SKEW), f)
    one[bucket_of(np.maximum(dist, 0))[inside], np.arange(SKEW)[inside]] = 1
    c["bucket"] = one
    c["outside"] = np.broadcast_to(np.where(inside, 0, MASKED).astype(f), (P, SKEW)).copy()
    return c


BASE_CONSTS = ("ident", "iota", "inv_freq")
MIX_CONSTS = ("swap1", "mask1")
LAYER_CONSTS = ("ret_cos", "ret_sin", "swap2", "decay", "tril", "half_ones")
BIAS_CONSTS = ("bucket", "outside")


def pack(c, names):
    return np.concatenate([c[n] for n in names], axis=1)




class Queue:

    def __init__(self, nc, engine, name):
        self.e, self.sem, self.count, self.seen = engine, nc.alloc_semaphore(name), 0, {}

    def did(self, instruction):
        self.count += 1
        instruction.then_inc(self.sem, 1)
        return (self.sem, self.count)

    def wait(self, *marks):
        need = {}
        for m in marks:
            if m is None:
                continue
            if isinstance(m, list):
                for x in m:
                    if x is not None:
                        need[x[0].name] = max(need.get(x[0].name, (0, None)), (x[1], x[0]), key=lambda t: t[0])
            else:
                need[m[0].name] = max(need.get(m[0].name, (0, None)), (m[1], m[0]), key=lambda t: t[0])
        for name, (value, sem) in need.items():
            if self.seen.get(name, 0) < value:
                self.e.wait_ge(sem, value)
                self.seen[name] = value

    def then(self, instruction):
        m = self.did(instruction)
        self.wait(m)
        return m


class Pair:

    def __init__(self, hi, lo, marks=None):
        self.hi, self.lo, self.marks = hi, lo, marks
        self.chunk_marks = None

    def at(self, f):
        return Pair(f(self.hi), f(self.lo), self.marks)


class Bank:

    def __init__(self, nc, name):
        self.t = nc.alloc_psum_tensor(name, [P, 512], F32)
        self.free = []


def wide(ap, n):
    return ap.unsqueeze(2).to_broadcast([ap.shape[0], ap.shape[1], n])


class Program:
    def __init__(self, nc, dram, out):
        self.nc, self.dram, self.out = nc, dram, out
        self.pe = Queue(nc, nc.tensor, "pe_done")
        self.act = Queue(nc, nc.scalar, "act_done")
        self.dve = Queue(nc, nc.vector, "dve_done")
        self.pool = Queue(nc, nc.gpsimd, "pool_done")
        self.sp = Queue(nc, nc.sync, "sp_unused")
        self.dma_sems = {}
        self.names = 0
        self.address = {}
        self.base = (nc.sbuf_base + 63) // 64 * 64
        self.top = self.base
        self.end = nc.sbuf_usable_end
        self.stream_banks = [Bank(nc, f"stream_bank{i}") for i in range(3)]
        self.side_banks = [Bank(nc, f"side_bank{i}") for i in range(5)]
        self.next_stream_bank = 0
        self.writes_out = []
        self.bank_marks = {}

    def place(self, name, shape, dtype=F32, at=None):
        size = 4 * int(np.prod(shape[1:]))
        size = (size + 31) // 32 * 32
        if at is None:
            at = self.top
            self.top += size
        assert at + size <= self.end, (name, at + size - self.end)
        self.names += 1
        t = self.nc.alloc_sbuf_tensor_at(f"{name}_{self.names}", list(shape), dtype, offset=at)
        self.address[t.name] = at
        return t

    def addr(self, t):
        return self.address[t.name]

    def pair(self, name, shape, at=None):
        size = 4 * int(np.prod(shape[1:]))
        hi = self.place(name + "_hi", shape, F32R, at)
        lo = self.place(name + "_lo", shape, F32R, None if at is None else at + size)
        return Pair(hi, lo, [])

    def dma(self, name, out, in_, *marks):
        q = self.sp
        sem, n = self.dma_sems.get(name, (None, 0))
        if sem is None:
            sem = self.nc.alloc_semaphore("dma_" + name)
        q.wait(*marks)
        q.e.dma_start(out, in_).then_inc(sem, 16)
        self.dma_sems[name] = (sem, n + 16)
        return (sem, n + 16)

    def start_stream(self, plan, raw_slots=3, split_slots=4):
        self.plan = plan
        self.R, self.H = raw_slots, split_slots
        self.raw = [self.place(f"raw{i}", [P, 1024]) for i in range(raw_slots)]
        self.hi = [self.place(f"unit_hi{i}", [P, 1024], F32R) for i in range(split_slots)]
        self.lo = [self.place(f"unit_lo{i}", [P, 1024], F32R) for i in range(split_slots)]
        self.loaded, self.split_marks, self.used = {}, {}, {}
        self.taken = 0
        self.dve_every = DVE_EVERY_BESIDE_SIDE_WORK

    def load_unit(self, n):
        if n >= len(self.plan):
            return
        _, src = self.plan[n]
        width = src.shape[-1]
        before = self.split_marks.get(n - self.R)
        self.loaded[n] = self.dma(f"raw{n % self.R}", self.raw[n % self.R][:, 0:width], src, before)

    def split_unit(self, n):
        if n >= len(self.plan):
            return
        width = self.plan[n][1].shape[-1]
        raw, hi, lo = (t[n % k][:, 0:width] for t, k in ((self.raw, self.R), (self.hi, self.H), (self.lo, self.H)))
        self.act.wait(self.loaded[n], self.used.get(n - self.H))
        h = self.act.did(self.nc.scalar.activation(hi, raw, ACT.Copy))
        q = self.pool if n % self.dve_every else self.dve
        q.wait(self.loaded[n], self.used.get(n - self.H), h)
        l = q.did(q.e.tensor_tensor(lo, raw, hi, ALU.subtract))
        self.split_marks[n] = [h, l]
        self.load_unit(n + self.R)

    def take(self, key):
        n = self.taken
        self.taken += 1
        assert self.plan[n][0] == key, (self.plan[n][0], key)
        self.split_unit(n + self.H - 1)
        self.pe.wait(self.split_marks[n])
        return n, Pair(self.hi[n % self.H], self.lo[n % self.H])

    def mm3(self, out, l, r, start, stop, skip=False):
        mm = self.nc.tensor.matmul
        kw = dict(skip_group_check=True) if skip else {}
        mm(out, l.hi, r.hi, start=start, stop=False, **kw)
        mm(out, l.hi, r.lo, start=False, stop=False, **kw)
        return mm(out, l.lo, r.hi, start=False, stop=stop, **kw)

    def stream_bank(self):
        b = self.stream_banks[self.next_stream_bank % len(self.stream_banks)]
        self.next_stream_bank += 1
        self.pe.wait(b.free)
        return b

    def fm_unit(self, key, rhs, chunks, *marks, outs=1):
        n, w = self.take(key)
        b = self.stream_bank()
        self.pe.wait(None if rhs.chunk_marks else rhs.marks, *marks)
        out = b.t[:, 0:outs * TOKENS]
        for j in range(outs):
            for k in range(chunks):
                if rhs.chunk_marks:
                    self.pe.wait(rhs.chunk_marks[k])
                c = (j * chunks + k) * P
                last = self.mm3(out[:, j * TOKENS:(j + 1) * TOKENS], w.at(lambda t: t[:, c:c + P]),
                                rhs.at(lambda t: t[:, k, :]), k == 0, k == chunks - 1)
        m = self.pe.did(last)
        self.used[n] = m
        return b, out, m

    def tm_unit(self, key, lhs, first_chunk, chunks, width, banks, start, stop, *marks):
        n, w = self.take(key)
        self.pe.wait(None if lhs.chunk_marks else lhs.marks, *marks)
        for k in range(chunks):
            if lhs.chunk_marks:
                self.pe.wait(lhs.chunk_marks[first_chunk + k])
            for t in range(TILES):
                for h, bank in enumerate(banks[t]):
                    wd = min(width, 512)
                    last = self.mm3(bank[:, 0:wd], lhs.at(lambda a: a[:, first_chunk + k, t * P:(t + 1) * P]),
                                    w.at(lambda a: a[:, k * width + h * wd:k * width + (h + 1) * wd]),
                                    start and k == 0, stop and k == chunks - 1)
                    if stop and k == chunks - 1:
                        self.bank_marks[t, h] = m = self.pe.did(last)
        if not stop:
            m = self.pe.did(last)
        self.used[n] = m
        return m

    def keep_warm(self, products=KEEP_WARM):
        b = self.side_banks[4]
        self.pe.wait(b.free, self.base_ready)
        for _ in range(products):
            last = self.nc.tensor.matmul(b.t[:, 0:TOKENS], self.ident, self.warm, start=True, stop=True)
        b.free = [self.pe.did(last)]

    def split(self, pair, src, bank, *marks, scale=None):
        self.act.wait(*marks)
        h = self.act.did(self.nc.scalar.activation(pair.hi, src, ACT.Copy if scale is None or isinstance(scale, float)
                                                   else ACT.Identity, scale=1.0 if scale is None else scale))
        self.dve.wait(h, *marks)
        if scale is None:
            i = self.nc.vector.tensor_tensor(pair.lo, src, pair.hi, ALU.subtract)
        else:
            i = self.nc.vector.scalar_tensor_tensor(pair.lo, src, scale, pair.hi, ALU.mult, ALU.subtract)
        l = self.dve.did(i)
        if bank is not None:
            bank.free = [l]
        return [h, l]

    def col(self, name, i=0, n=1):
        a, w = COLS[name]
        assert i + n <= w
        return self.cols[:, a + i:a + i + n]

    def rstd_tm(self, x, pieces, name):
        nc = self.nc
        sq, r = self.small(name + "_sq", 2 * TILES), self.small(name + "_r", TILES)
        self.act.wait(self.base_ready)
        self.act.did(nc.scalar.activation(self.small(name + "_t", 1), self.ones[:, 0:1], ACT.Sqrt))
        for (t, h), m in pieces:
            self.act.wait(m)
            cols = slice(h * 512, (h + 1) * 512)
            m = self.act.did(nc.scalar.activation(self.junk[:, t, cols], x[:, t, cols], ACT.Square,
                                                  accum_out=sq[:, h * TILES + t:h * TILES + t + 1]))
        self.dve.wait(m)
        m = self.dve.then(nc.vector.scalar_tensor_tensor(r, sq[:, 0:TILES], EPS * D, sq[:, TILES:], ALU.add, ALU.add))
        self.act.wait(m)
        m = self.act.did(nc.scalar.activation(r, r, ACT.Sqrt, scale=1.0 / D))
        self.dve.wait(m)
        self.dve.then(nc.vector.reciprocal(r, r))
        return r

    def small(self, name, n):
        a = self.small_at
        self.small_at += n
        assert self.small_at <= self.smalls.shape[1], name
        return self.smalls[:, a:a + n]

    def norm_to_fm(self, x, pieces, gcol, out, name):
        for _ in self.norm_steps(x, pieces, gcol, out, name):
            pass

    def norm_steps(self, x, pieces, gcol, out, name):
        nc = self.nc
        self.keep_warm()
        r = self.rstd_tm(x, pieces, name)
        self.dve.wait(self.diag_free)
        for t in range(TILES):
            diag_ready = self.dve.did(nc.vector.tensor_scalar(self.diag[:, t, :], self.ident, r[:, t:t + 1], None,
                                                              ALU.mult))
        out.chunk_marks = [None] * KD
        yield
        for k2 in range(KD // 2):
            b = self.side_banks[k2 % 4]
            self.pe.wait(b.free, diag_ready)
            for j in range(2):
                for t in range(TILES):
                    k = 2 * k2 + j
                    last = nc.tensor.matmul(b.t[:, j * TOKENS + t * P:j * TOKENS + (t + 1) * P],
                                            x[:, t, k * P:(k + 1) * P], self.diag[:, t, :], start=True, stop=True)
            turned = self.diag_free = self.pe.did(last)
            self.act.wait(turned)
            for j in range(2):
                k = 2 * k2 + j
                h = self.act.did(nc.scalar.activation(out.hi[:, k, :], b.t[:, j * TOKENS:(j + 1) * TOKENS],
                                                      ACT.Identity, scale=self.col(gcol, k)))
            self.dve.wait(h, turned)
            for j in range(2):
                k = 2 * k2 + j
                l = self.dve.did(nc.vector.scalar_tensor_tensor(
                    out.lo[:, k, :], b.t[:, j * TOKENS:(j + 1) * TOKENS], self.col(gcol, k), out.hi[:, k, :],
                    ALU.mult, ALU.subtract))
                out.chunk_marks[k] = [h, l]
            b.free = [l]
            yield
        out.marks = [h, l]

    def barrier(self):
        qs = (self.pe, self.act, self.dve, self.pool)
        marks = []
        for q in qs:
            if q.count:
                marks.append((q.sem, q.count))
        for q in qs + (self.sp,):
            q.wait(marks)

    def run(self, steps, side=()):
        side = list(side)
        for _ in steps:
            for s in list(side):
                if next(s, "end") == "end":
                    side.remove(s)
        for s in side:
            for _ in s:
                pass




def softmax_head(g, state):
    nc = g.nc
    s = state
    bank = g.side_banks[s["bank"]]
    q = s["queries"]
    g.pe.wait(bank.free, s["marks"])
    at, where = 0, []
    for (t, k0, kn) in s["segments"]:
        last = nc.tensor.matmul(bank.t[:, at:at + kn], s["q"](t), s["k"](k0, kn), start=True, stop=True)
        where.append((at, kn))
        at += kn
    scored = g.pe.did(last)
    yield
    S, mx, den = s["S"], s["mx"], s["den"]
    g.dve.wait(scored, s["S_free"][0], g.base_ready, s["bias_ready"])
    if s["bias"] is not None:
        for i, (a, kn) in enumerate(where):
            m = g.dve.did(nc.vector.scalar_tensor_tensor(S[:, a:a + kn], bank.t[:, a:a + kn], s["scale"],
                                                         s["bias"](i), ALU.mult, ALU.add))
        bank.free = [m]
        g.dve.wait(m)
        src, scale = S, 1.0
    else:
        src, scale = bank.t, s["scale"]
    for i, (a, kn) in enumerate(where):
        m = g.dve.did(nc.vector.tensor_reduce(mx[:, i:i + 1], src[:, a:a + kn], AXIS_X, ALU.max))
    g.dve.wait(m)
    if s["sink"] is not None:
        m = g.dve.did(nc.vector.tensor_scalar(mx, mx, s["sink"], -1.0, ALU.max, ALU.mult))
    else:
        m = g.dve.did(nc.vector.tensor_scalar(mx, mx, -scale, None, ALU.mult))
    yield
    g.act.wait(m)
    for i, (a, kn) in enumerate(where):
        m = g.act.did(nc.scalar.activation(S[:, a:a + kn], src[:, a:a + kn], ACT.Exp, bias=mx[:, i:i + 1],
                                           scale=scale, accum_out=den[:, i:i + 1]))
    if s["bias"] is None:
        bank.free = [m]
    if s["sink"] is not None:
        m = g.act.did(nc.scalar.activation(s["es"], mx, ACT.Exp, bias=s["sink"]))
    yield
    g.dve.wait(m)
    if s["sink"] is not None:
        g.dve.then(nc.vector.tensor_tensor(den, den, s["es"], ALU.add))
    g.dve.then(nc.vector.reciprocal(den, den))
    for i, (a, kn) in enumerate(where):
        m = g.dve.did(nc.vector.tensor_scalar(S[:, a:a + kn], S[:, a:a + kn], den[:, i:i + 1], None, ALU.mult))
    yield
    tb = g.side_banks[s["turn_bank"]]
    g.pe.wait(tb.free, m)
    blocks = {}
    for (t, k0, kn), (a, _) in zip(s["segments"], where):
        for j in range(kn // P):
            kt = k0 // P + j
            dst = tb.t[:, kt * q + t * P:kt * q + (t + 1) * P]
            last = nc.tensor.transpose(dst, S[:, a + j * P:a + (j + 1) * P], g.ident)
            blocks.setdefault(kt, []).append(t)
    turned = g.pe.did(last)
    s["S_free"][0] = turned
    PT = s["PT"]
    g.act.wait(turned, s["PT_free"][0])
    for kt, ts in blocks.items():
        a, n = kt * q + min(ts) * P, len(ts) * P
        m = g.act.did(nc.scalar.activation(PT[:, a:a + n], tb.t[:, a:a + n], ACT.Copy))
    tb.free = [m]
    yield
    ob = g.side_banks[s["out_bank"]]
    g.pe.wait(ob.free, m, s["v_marks"])
    order = sorted(blocks, key=lambda kt: -len(blocks[kt]))
    assert len(blocks[order[0]]) == TILES
    for i, kt in enumerate(order):
        ts = blocks[kt]
        a, n = min(ts) * P, len(ts) * P
        last = nc.tensor.matmul(ob.t[:, a:a + n], s["v"](kt), PT[:, kt * q + a:kt * q + a + n],
                                start=(i == 0), stop=(i == len(order) - 1), skip_group_check=True)
    out = g.pe.did(last)
    s["PT_free"][0] = out
    s["done"](ob, ob.t[:, 0:q], out)
    yield


def pipeline(generators, distance=2):
    waiting, live, rounds = list(generators), [], 0
    while waiting or live:
        if waiting and rounds % distance == 0:
            live.append(waiting.pop(0))
        for x in list(live):
            if next(x, "end") == "end":
                live.remove(x)
        rounds += 1
        yield




def mixer(g, phase):
    nc, a = g.nc, g.dram
    V, S = nc.vector, nc.scalar
    g.top = phase
    consts = g.place("mix_consts", [P, P + TILES * TOKENS])
    swap, mask = consts[:, 0:P], consts[:, P:]
    hT = g.pair("hT", [P, KD, TOKENS])
    branch = g.pair("branch", [P, 16, TOKENS])
    branch.marks = []
    memT_at = g.top - 2 * 16 * 4 * TOKENS
    memT = g.pair("memT", [P, KD, TOKENS], at=memT_at)
    qk = g.place("qk", [P, 8, TOKENS])
    v_a = g.place("v_a", [P, TILES, 256])
    xl_w = TOKENS + CONV_TAPS - 1
    xl = g.place("xl", [P, LRU_BLOCKS, xl_w])
    xc = g.place("xc", [P, LRU_BLOCKS, TOKENS])
    gl = g.place("gelu_gate", [P, LRU_BLOCKS, TOKENS])
    qm = g.place("qm", [P, MEM_HEADS, TOKENS])
    gates_at = g.top
    gates = g.place("gates", [P, 24, TOKENS])
    x_in = g.place("x_in", [P, TILES, D], at=gates_at)
    m_in = g.place("m_in", [P, TILES, D], at=gates_at + 8192)
    g.junk = g.place("squares", [P, TILES, D], at=gates_at + 16384)
    km = g.place("km", [P, MEM_HEADS, TOKENS])
    vm = g.place("vm", [P, TILES, MIX])
    lru_a = g.place("lru_a", [P, LRU_BATCH, 2, TOKENS])
    lru_b = g.place("lru_b", [P, LRU_BATCH, 2, TOKENS])
    lru_i = g.place("lru_i", [P, LRU_BATCH, 2, TOKENS])
    lru_w = g.place("lru_w", [P, 24, P])
    Sbuf = [g.place(f"S{i}", [P, 512]) for i in range(2)]
    PT = g.place("PT", [P, 512])
    t1 = g.place("t1", [P, 2, TOKENS])
    rope_c, rope_s = g.place("rope_c", [P, TOKENS]), g.place("rope_s", [P, TOKENS])
    pos_i = g.place("pos_i", [P, TOKENS], I32, at=g.addr(lru_b))
    ang, kk = (g.place(n, [P, TOKENS], at=g.addr(lru_i) + 1024 * i) for i, n in enumerate(("ang", "kk")))

    g.rope_tmp = g.place("rope_tmp", [P, TOKENS])[:, :]
    m_ready = g.dma("m_in", m_in[:, :, :], a["mem"])
    g.load_unit(0)
    g.load_unit(1)
    x_ready = g.dma("x_in", x_in[:, :, :], a["x"])
    g.load_unit(2)
    mix_consts = g.dma("mix_consts", consts[:, :], a["mix_consts"])
    pos_ready = g.dma("pos", pos_i[:, :], a["positions"])
    w_ready = g.dma("lru_w", lru_w[:, :, :], a["lru_w"].rearrange("p (a e) -> p a e", a=24))

    for q in (g.pe, g.act, g.dve, g.pool):
        q.wait(g.base_ready)
    halves = [(t, h) for t in range(TILES) for h in range(2)]
    memory_norm = g.norm_steps(m_in, [(th, m_ready) for th in halves], "g_mem", memT, "nm")
    next(memory_norm)
    for n in range(g.H - 1):
        g.split_unit(n)
        next(memory_norm, None)
    for _ in memory_norm:
        pass
    pads_zero = g.dve.did(V.memset(xl[:, :, 0:CONV_LEFT], 0.0))
    pads_zero = g.dve.did(V.memset(xl[:, :, CONV_LEFT + TOKENS:xl_w], 0.0))
    marks = {}
    two_pi = 2 * np.pi
    lam = g.col("lam", 0, 12)
    ya, yb, c8, hb = g.small("ya", 12), g.small("yb", 12), g.small("c8", 12), g.small("hb", 24)
    z, z2 = g.small("z", 12), g.small("z2", 12)
    hgb = g.small("hgb", 24)

    def token_norm():
        g.act.wait((g.act.sem, g.act.count))
        yield from g.norm_steps(x_in, [(th, x_ready) for th in halves], "g_mix", hT, "nx")
        marks["inputs_read"] = [(g.pe.sem, g.pe.count), (g.act.sem, g.act.count), (g.dve.sem, g.dve.count)]

    def tables():
        c1 = 6.28125
        c2 = float(np.float32(two_pi - c1).view(np.uint32) & 0xFFFFF000)
        c2 = float(np.array([int(c2)], np.uint32).view(np.float32)[0])
        c3 = two_pi - c1 - c2
        magic = 12582912.0
        g.dve.wait(pos_ready, g.base_ready)
        g.dve.then(V.tensor_copy(ang[:, :], pos_i[:, :]))
        g.dve.then(V.tensor_scalar(ang[:, :], ang[:, :], g.inv_freq, None, ALU.mult))
        g.dve.then(V.tensor_scalar(kk[:, :], ang[:, :], 1 / two_pi, magic, ALU.mult, ALU.add))
        g.dve.then(V.tensor_scalar(kk[:, :], kk[:, :], magic, None, ALU.subtract))
        yield
        for c in (c1, c2, c3):
            g.dve.then(V.scalar_tensor_tensor(ang[:, :], kk[:, :], -c, ang[:, :], ALU.mult, ALU.add))
        yield
        g.dve.then(V.tensor_scalar(ang[:, :], ang[:, :], 3.1415925, -3.1415925, ALU.min, ALU.max))
        m = g.dve.then(V.scalar_tensor_tensor(kk[:, :], ang[:, :], -1.0, ang[:, :], ALU.mult, ALU.max))
        m = g.dve.then(V.tensor_scalar(kk[:, :], kk[:, :], -1.0, float(np.pi / 2), ALU.mult, ALU.add))
        g.dve.did(V.memset(rope_s[:, :], 0.0))
        m = g.dve.did(V.memset(rope_c[:, :], 1.0))
        yield
        g.act.wait(m)
        g.act.did(S.activation(rope_s[0:ROPE_DIM, :], ang[0:ROPE_DIM, :], ACT.Sin))
        marks["rope_tables"] = g.act.did(S.activation(rope_c[0:ROPE_DIM, :], kk[0:ROPE_DIM, :], ACT.Sin))

        yield
        g.dve.then(V.scalar_tensor_tensor(ya, lam, -1.0, lam, ALU.mult, ALU.max))
        m = g.dve.then(V.tensor_scalar(yb, lam, -1.0, 0.0, ALU.mult, ALU.max))
        g.act.wait(m)
        m = g.act.did(S.activation(ya, ya, ACT.Exp, scale=-1.0))
        yield
        g.dve.wait(m)
        g.dve.then(V.tensor_scalar(z, ya, 2.0, None, ALU.add))
        g.dve.then(V.reciprocal(z, z))
        g.dve.then(V.tensor_tensor(z, ya, z, ALU.mult))
        g.dve.then(V.tensor_tensor(z2, z, z, ALU.mult))
        terms = 9
        g.dve.then(V.tensor_scalar(c8, z2, 1.0 / (2 * terms + 1), 1.0 / (2 * terms - 1), ALU.mult, ALU.add))
        for i in range(terms - 2, -1, -1):
            g.dve.then(V.tensor_tensor(c8, c8, z2, ALU.mult))
            g.dve.then(V.tensor_scalar(c8, c8, 1.0 / (2 * i + 1), None, ALU.add))
            if i % 3 == 0:
                yield
        g.dve.then(V.tensor_tensor(c8, c8, z, ALU.mult))
        g.dve.then(V.scalar_tensor_tensor(c8, c8, 2.0, yb, ALU.mult, ALU.add))
        g.dve.then(V.tensor_scalar(c8, c8, -LRU_C / 2, None, ALU.mult))
        yield
        g.dve.did(V.tensor_scalar(hb, g.cols[:, COLS["lru_br"][0]:COLS["lru_br"][0] + 24], 0.5, None, ALU.mult))
        marks["smalls"] = g.dve.did(V.tensor_scalar(hgb, g.col("gate_b", 0, 24), 0.5, None, ALU.mult))

    def to_sbuf(key, i, dst, chunks=KD, rhs=hT, func=ACT.Copy, **kw):
        b, out, m = g.fm_unit((key, i), rhs, chunks)
        g.act.wait(m, kw.pop("after", None))
        m = g.act.did(S.activation(dst, out, func, **kw))
        b.free = [m]
        marks[key, i] = m

    def tm_to_sbuf(key, dst, units, chunks, width, lhs):
        banks = [g.side_banks[0], g.side_banks[1]]
        for b in banks:
            g.pe.wait(b.free)
        for u in range(units):
            m = g.tm_unit((key, u), lhs, u * chunks, chunks, width, [[b.t] for b in banks], u == 0, u == units - 1)
            yield
        g.act.wait(m)
        for t, b in enumerate(banks):
            e = g.act.did(S.activation(dst[:, t, :], b.t[:, 0:width], ACT.Copy))
            b.free = [e]
        marks[key] = e

    def main():
        for i in range(MEM_HEADS):
            to_sbuf("km", i, km[:, i, :], rhs=memT)
            yield
        yield from tm_to_sbuf("vm", vm, 4, 2, 512, memT)
        marks["memT"] = (g.pe.sem, g.pe.count)
        while "inputs_read" not in marks:
            yield
        yield from tm_to_sbuf("va", v_a, 2, 4, 256, hT)
        for i in range(LRU_BLOCKS):
            to_sbuf("xl", i, xl[:, i, CONV_LEFT:CONV_LEFT + TOKENS], after=pads_zero)
            yield
        for i in range(MEM_HEADS):
            to_sbuf("qm", i, qm[:, i, :])
            yield
        for i in range(8):
            to_sbuf("qk", i, qk[:, i, :])
            yield
        for i in range(LRU_BLOCKS):
            to_sbuf("gl", i, gl[:, i, :])
            yield
        while "smalls" not in marks:
            yield
        g.act.wait(marks["inputs_read"])
        for i in range(24):
            to_sbuf("gate", i, gates[:, i, :], func=ACT.Tanh, scale=0.5, bias=hgb[:, i:i + 1],
                    after=[marks["smalls"]])
            yield

    def conv():
        for i in range(LRU_BLOCKS):
            while ("xl", i) not in marks:
                yield
            g.dve.wait(marks["xl", i], g.base_ready)
            w = lambda j: g.col("conv_w", j * LRU_BLOCKS + i)
            g.dve.then(V.tensor_scalar(xc[:, i, :], xl[:, i, 0:TOKENS], w(0), g.col("conv_b", i), ALU.mult, ALU.add))
            for j in range(1, CONV_TAPS):
                m = g.dve.then(V.scalar_tensor_tensor(xc[:, i, :], xl[:, i, j:j + TOKENS], w(j), xc[:, i, :],
                                                      ALU.mult, ALU.add))
            marks["xc", i] = m
            yield

    lru_free = [None, None]

    def lru_gates(i):
        bank = g.side_banks[4]
        j = i % LRU_BATCH
        for kind in range(2):
            g.pe.wait(bank.free, marks["xc", i], w_ready)
            for d in range(2):
                last = nc.tensor.matmul(bank.t[:, d * TOKENS:(d + 1) * TOKENS], lru_w[:, (kind * 2 + d) * 6 + i, :],
                                        xc[:, i, :], start=True, stop=True)
            m = g.pe.did(last)
            dst = lru_a if kind == 0 else lru_i
            g.act.wait(m, marks["smalls"], lru_free)
            for d in range(2):
                m = g.act.did(S.activation(dst[:, j, d, :], bank.t[:, d * TOKENS:(d + 1) * TOKENS], ACT.Tanh,
                                           scale=0.5, bias=hb[:, kind * 12 + d * 6 + i:kind * 12 + d * 6 + i + 1]))
            bank.free = [m]
            if kind == 0:
                g.act.wait(m)
                for d in range(2):
                    c = c8[:, d * 6 + i:d * 6 + i + 1]
                    m = g.act.did(S.activation(lru_b[:, j, d, :], lru_a[:, j, d, :], ACT.Tanh, scale=c, bias=c))
                g.act.wait(m)
                for d in range(2):
                    c = c8[:, d * 6 + i:d * 6 + i + 1]
                    m = g.act.did(S.activation(lru_a[:, j, d, :], lru_a[:, j, d, :], ACT.Exp, scale=c, bias=c))
                th = m
            yield
        g.dve.wait(m, th)
        g.dve.then(V.tensor_scalar(t1[:, :, :], lru_b[:, j, :, :], -1.0, 1.0, ALU.mult, ALU.add))
        g.dve.then(V.reciprocal(t1[:, :, :], t1[:, :, :]))
        m = g.dve.then(V.tensor_tensor(lru_b[:, j, :, :], lru_b[:, j, :, :], t1[:, :, :], ALU.mult))
        for d in range(2):
            m2 = g.dve.did(V.scalar_tensor_tensor(lru_i[:, j, d, :], lru_i[:, j, d, :], 1.0, xc[:, i, :],
                                                  ALU.add, ALU.mult))
        marks["lru_q", i] = [m, m2]
        yield

    def lru_scan(i):
        j = i % LRU_BATCH
        g.dve.wait(marks["lru_sqrt", i // LRU_BATCH])
        m = g.dve.then(V.tensor_tensor(lru_b[:, j, :, :], lru_b[:, j, :, :], lru_i[:, j, :, :], ALU.mult))
        g.dve.then(V.tensor_tensor_scan(t1[:, 0, :], lru_a[:, j, 0, :], lru_b[:, j, 0, :], 0.0, ALU.mult, ALU.add))
        g.dve.then(V.tensor_tensor_scan(t1[:, 1, ::-1], lru_a[:, j, 1, ::-1], lru_b[:, j, 1, ::-1], 0.0,
                                        ALU.mult, ALU.add))
        yield
        g.dve.then(V.tensor_tensor(t1[:, 0, :], t1[:, 0, :], t1[:, 1, :], ALU.add))
        g.dve.wait(marks["gelu"])
        m = g.dve.then(V.scalar_tensor_tensor(t1[:, 0, :], t1[:, 0, :], 0.5, gl[:, i, :], ALU.mult, ALU.mult))
        bp = branch.at(lambda t: t[:, 6 + i, :])
        branch.marks = g.split(bp, t1[:, 0, :], None, m, marks["memT"])
        g.dve.wait(branch.marks)
        yield

    def gelu_gate():
        while ("gl", LRU_BLOCKS - 1) not in marks:
            yield
        c = float(np.sqrt(2 / np.pi))
        for i in range(LRU_BLOCKS):
            u = t1[:, 0, :]
            m = g.dve.wait(marks["gl", i])
            g.dve.then(V.tensor_tensor(u, gl[:, i, :], gl[:, i, :], ALU.mult))
            g.dve.then(V.tensor_scalar(u, u, 0.044715, 1.0, ALU.mult, ALU.add))
            m = g.dve.then(V.tensor_tensor(u, u, gl[:, i, :], ALU.mult))
            g.act.wait(m)
            m = g.act.did(S.activation(u, u, ACT.Tanh, scale=c))
            g.dve.wait(m)
            m = g.dve.then(V.scalar_tensor_tensor(gl[:, i, :], u, 1.0, gl[:, i, :], ALU.add, ALU.mult))
            yield
        marks["gelu"] = m

    def lru():
        yield from tables()
        yield from conv()
        for half in range(LRU_BLOCKS // LRU_BATCH):
            blocks = range(LRU_BATCH * half, LRU_BATCH * (half + 1))
            for i in blocks:
                yield from lru_gates(i)
            m = sum((marks["lru_q", i] for i in blocks), [])
            g.act.wait(m)
            marks["lru_sqrt", half] = g.act.did(S.activation(lru_b[:, :, :, :], lru_b[:, :, :, :], ACT.Sqrt, scale=-0.5))
            if half == 0:
                yield from gelu_gate()
            for i in blocks:
                yield from lru_scan(i)
            lru_free[:] = [(g.dve.sem, g.dve.count)]
        marks["p_lru"] = [(g.act.sem, g.act.count), (g.dve.sem, g.dve.count)]

    S_free, PT_free = [[None], [None]], [None]
    n_head = [0]

    def rope():
        def add(c, cos_part):
            g.dve.wait(cos_part)
            marks["rope", c] = g.dve.then(V.tensor_tensor(qk[:, c, :], qk[:, c, :], g.rope_tmp, ALU.add))

        due = None
        for c in list(range(6, 8)) + list(range(6)):
            while ("qk", c) not in marks:
                yield
            if due:
                add(*due)
            bank = g.side_banks[3]
            g.pe.wait(bank.free, marks["qk", c], mix_consts)
            m = g.pe.did(nc.tensor.matmul(bank.t[:, 0:TOKENS], swap, qk[:, c, :], start=True, stop=True))
            g.pool.wait(marks["qk", c], marks["rope_tables"], m)
            m2 = g.pool.did(nc.gpsimd.tensor_tensor(qk[:, c, :], qk[:, c, :], rope_c[:, :], ALU.mult))
            g.dve.wait(m, marks["rope_tables"])
            u = g.rope_tmp
            m3 = g.dve.then(V.tensor_tensor(u, bank.t[:, 0:TOKENS], rope_s[:, :], ALU.mult))
            bank.free = [m3]
            due = (c, m2)
            yield
        add(*due)
        yield

    def head(kind, h):
        i = n_head[0]
        n_head[0] += 1
        st = dict(bank=i % 2, turn_bank=2, out_bank=3, queries=TOKENS, scale=HEAD ** -0.5,
                  segments=[(t, 0, TOKENS) for t in range(TILES)], S=Sbuf[i % 2], S_free=S_free[i % 2], PT=PT,
                  PT_free=PT_free, mx=g.small(f"mx{i}", 2), den=g.small(f"den{i}", 2), es=g.small(f"es{i}", 2))
        if kind == "attn":
            kv = h // 3
            st.update(marks=[marks["rope", h], marks["rope", 6 + kv]], q=lambda t: qk[:, h, t * P:(t + 1) * P],
                      k=lambda k0, kn: qk[:, 6 + kv, k0:k0 + kn], v=lambda kt: v_a[:, kt, kv * P:(kv + 1) * P],
                      v_marks=marks["va"], bias=lambda i: mask[:, i * TOKENS:(i + 1) * TOKENS],
                      bias_ready=mix_consts, sink=g.col("sink", h))
            chunk = h
        else:
            st.update(marks=[marks["qm", h], marks["km", h]], q=lambda t: qm[:, h, t * P:(t + 1) * P],
                      k=lambda k0, kn: km[:, h, k0:k0 + kn], v=lambda kt: vm[:, kt, h * P:(h + 1) * P],
                      v_marks=marks["vm"], bias=None, bias_ready=None, sink=None)
            chunk = 12 + h

        def done(bank, out, m):
            branch.marks = g.split(branch.at(lambda t: t[:, chunk, :]), out, bank, m, marks["memT"])

        st["done"] = done
        yield from softmax_head(g, st)

    def attention():
        while ("qm", MEM_HEADS - 1) not in marks or "va" not in marks or "rope_tables" not in marks:
            yield
        yield from pipeline([head("mem", h) for h in range(MEM_HEADS)])
        marks["p_mem"] = [(g.act.sem, g.act.count), (g.dve.sem, g.dve.count)]
        yield from rope()
        yield from pipeline([head("attn", h) for h in range(Q_HEADS)])
        marks["p_attn"] = [(g.act.sem, g.act.count), (g.dve.sem, g.dve.count)]
        marks["attn_pe"] = (g.pe.sem, g.pe.count)

    merged = Pair(hT.hi, hT.lo, [])
    merged.chunk_marks = []
    xr = g.place("x_res", [P, TILES, D], at=g.addr(qk))
    xr_ready = []

    def branches():
        hT_free = (g.pe.sem, g.pe.count)
        spans = (("p_mem", 2, 12, 4), ("p_attn", 0, 0, 6), ("p_lru", 1, 6, 6))
        for nth, (key, n, first, chunks) in enumerate(spans):
            while key not in marks:
                yield
            if key == "p_attn":
                xr_ready.append(g.dma("x_res", xr[:, :, :], a["x"], marks[key], marks["attn_pe"]))
            part = Pair(branch.hi[:, first:first + chunks, :], branch.lo[:, first:first + chunks, :], marks[key])
            outs = 2 if chunks == 4 else 1
            for i in range(0, KD, outs):
                b, out, mk = g.fm_unit((key, i // outs), part, chunks, outs=outs)
                gate = gates[:, n * KD + i:n * KD + i + outs, :]
                g.dve.wait(mk)
                m = g.dve.then(V.scalar_tensor_tensor(gate, gate, 1.0, out.rearrange("p (a t) -> p a t", a=outs),
                                                      ALU.add, ALU.mult))
                b.free = [m]
                if nth:
                    total = gates[:, 2 * KD + i, :]
                    m = g.dve.then(V.tensor_tensor(total, total, gate[:, 0, :], ALU.add))
                if nth == BRANCHES - 1:
                    g.act.wait(hT_free)
                    merged.chunk_marks.append(g.split(merged.at(lambda t: t[:, i, :]), total, None, m, scale=0.5))
                yield

    def main_and_branches():
        yield from main()
        yield from branches()

    g.run(main_and_branches(), [token_norm(), lru(), attention()])
    project_out(g, "w_out", merged, xr, xr_ready)


def project_out(g, key, lhs, res, res_marks):
    nc = g.nc
    marks = []
    for h in range(2):
        banks = [g.side_banks[2 * h + t] for t in range(TILES)]
        for b in banks:
            g.pe.wait(b.free)
        for u in range(4):
            g.tm_unit((key, h * 4 + u), lhs, 2 * u, 2, 512, [[b.t] for b in banks], u == 0, u == 3)
        for t, b in enumerate(banks):
            g.dve.wait(g.bank_marks[t, 0], *res_marks)
            mk = g.dve.did(nc.vector.tensor_tensor(g.X[:, t, h * 512:(h + 1) * 512], b.t[:, :],
                                                   res[:, t, h * 512:(h + 1) * 512], ALU.add))
            b.free = [mk]
            marks.append(mk)
    g.X_marks = marks
    g.X_pieces = [((t, h), marks[h * TILES + t]) for h in range(2) for t in range(TILES)]




def peer(g, phase):
    nc, a = g.nc, g.dram
    V, S = nc.vector, nc.scalar
    g.top = phase
    experts = g.place("experts", [P, KEYS, TOKENS])
    h2T = g.pair("h2T", [P, KD, TOKENS])
    slot_T = g.place("slot_T", [P, 3, TOKENS])
    G = 4
    hot_at = g.addr(h2T.hi)
    HOTS = 3
    first_hot = [g.place(f"first_hot{i}", [P, G, P], at=hot_at + 2048 * i) for i in range(HOTS)]
    second_hot = [g.place(f"second_hot{i}", [P, G, P], at=hot_at + 2048 * (HOTS + i)) for i in range(HOTS)]
    ex = g.addr(experts)
    g.junk = g.place("squares2", [P, TILES, D], at=ex)
    late_j = 70
    late = ex + 4 * late_j * TOKENS
    late_top = [late]

    def in_late(name, shape, dtype=F32):
        t = g.place(name, shape, dtype, at=late_top[0])
        late_top[0] += 4 * int(np.prod(shape[1:]))
        assert late_top[0] <= ex + 4 * KEYS * TOKENS
        return t

    HP = 2 * PEER_HEADS
    queries = in_late("queries", [P, HP, TOKENS])
    keys = in_late("sub_keys", [P, HP, KEYS])
    scores = in_late("key_scores", [P, HP, KEYS])
    top_v = in_late("top_v", [P, HP, TOPK])
    top_i = in_late("top_i", [P, HP, TOPK], U32)
    top_f = in_late("top_f", [P, HP, TOPK])
    pairs = in_late("pair_sums", [P, PEER_HEADS, TOPK, TOPK])
    hot = in_late("hot", [P, PEER_HEADS, TOPK, TOPK])
    best_v = in_late("best_v", [P, PEER_HEADS, TOPK])
    best_p = in_late("best_p", [P, PEER_HEADS, TOPK], U32)
    part_u = in_late("part_u", [P, PEER_HEADS, TOPK], U32)
    part_f = in_late("part_f", [P, PEER_HEADS, TOPK])
    picked = in_late("picked", [P, 3, PEER_HEADS, TOPK])
    sums = in_late("gate_sums", [P, PEER_HEADS])

    g.norm_to_fm(g.X, g.X_pieces, "g_ffn", h2T, "nf")
    norm_done = [(g.pe.sem, g.pe.count), (g.act.sem, g.act.count)]
    keys_ready = g.dma("keys", keys[:, :, :], a["sub_keys"].rearrange("p (a k) -> p a k", a=HP), norm_done)
    q_marks = []
    for i in range(HP):
        b, out, m = g.fm_unit(("peer_q", i), h2T, KD)
        g.act.wait(m)
        m = g.act.did(S.activation(queries[:, i, :], out, ACT.Copy))
        b.free = [m]
        q_marks = [m]
    topk_done = []

    def topk():
        for t in range(TILES):
            for b4 in range(4):
                b = g.side_banks[b4]
                g.pe.wait(b.free, q_marks, keys_ready)
                for j in range(4):
                    i = 4 * b4 + j
                    last = nc.tensor.matmul(b.t[:, j * P:(j + 1) * P], queries[:, i, t * P:(t + 1) * P],
                                            keys[:, i, :], start=True, stop=True)
                m = g.pe.did(last)
                g.act.wait(m, (g.dve.sem, g.dve.count) if t else None)
                m = g.act.did(S.activation(scores[:, 4 * b4:4 * b4 + 4, :],
                                           b.t[:, :].rearrange("p (a k) -> p a k", a=4), ACT.Copy))
                b.free = [m]
            g.dve.wait(m)
            yield
            for i in range(HP):
                top16(scores[:, i, :], top_v[:, i, :], top_i[:, i, :])
                yield
            g.dve.then(V.tensor_copy(top_f[:, :, :], top_i[:, :, :]))
            v4 = top_v[:, :, :].rearrange("p (h two) k -> p h two k", two=2)
            g.dve.then(V.tensor_tensor(pairs[:, :, :, :], v4[:, :, 0, :].unsqueeze(3).to_broadcast(list(pairs.shape)),
                                       v4[:, :, 1, :].unsqueeze(2).to_broadcast(list(pairs.shape)), ALU.add))
            for h in range(PEER_HEADS):
                top16(pairs[:, h, :, :].rearrange("p a b -> p (a b)"), best_v[:, h, :], best_p[:, h, :])
                yield
            f4 = top_f[:, :, :].rearrange("p (h two) k -> p h two k", two=2)
            for part in range(2):
                if part == 0:
                    g.dve.then(V.tensor_single_scalar(part_u[:, :, :], best_p[:, :, :], 4, ALU.logical_shift_right))
                else:
                    g.dve.then(V.tensor_single_scalar(part_u[:, :, :], best_p[:, :, :], 15, ALU.bitwise_and))
                g.dve.then(V.tensor_copy(part_f[:, :, :], part_u[:, :, :]))
                shape = list(hot.shape)
                g.dve.then(V.tensor_tensor(
                    hot[:, :, :, :], part_f[:, :, :].unsqueeze(3).to_broadcast(shape),
                    g.iota[:, 0:TOPK].unsqueeze(1).unsqueeze(1).to_broadcast(shape), ALU.is_equal))
                yield
                g.dve.then(V.tensor_tensor(hot[:, :, :, :], hot[:, :, :, :],
                                           f4[:, :, part, :].unsqueeze(2).to_broadcast(shape), ALU.mult))
                yield
                g.dve.then(V.tensor_reduce(picked[:, part, :, :], hot[:, :, :, :], AXIS_X, ALU.add))
                yield
            gate = picked[:, 2, :, :]
            m = g.dve.then(V.tensor_tensor(gate, best_v[:, :, :], best_v[:, :, 0:1].to_broadcast(list(best_v.shape)),
                                           ALU.subtract))
            yield
            g.act.wait(m)
            m = g.act.did(S.activation(gate, gate, ACT.Exp))
            yield
            g.dve.wait(m)
            g.dve.then(V.tensor_reduce(sums[:, :], gate, AXIS_X, ALU.add))
            g.dve.then(V.reciprocal(sums[:, :], sums[:, :]))
            m = g.dve.then(V.tensor_tensor(gate, gate, sums[:, :].unsqueeze(2).to_broadcast(list(best_v.shape)),
                                           ALU.mult))
            yield
            yield
            b = g.side_banks[4]
            g.pe.wait(b.free, m)
            for k in range(3):
                last = nc.tensor.transpose(b.t[:, k * P:(k + 1) * P], picked[:, k, :, :].rearrange("p a b -> p (a b)"),
                                           g.ident)
            m = g.pe.did(last)
            g.act.wait(m)
            m = g.act.did(S.activation(slot_T[:, :, t * P:(t + 1) * P],
                                       b.t[:, 0:3 * P].rearrange("p (a k) -> p a k", a=3), ACT.Copy))
            b.free = [m]
            g.dve.wait(m)
            yield
        topk_done.extend([m, (g.pe.sem, g.pe.count), (g.dve.sem, g.dve.count)])

    def top16(src, values, places):
        g.dve.then(V.max(values[:, 0:8], src))
        g.dve.then(V.max_index(places[:, 0:8], values[:, 0:8], src))
        g.dve.then(V.match_replace(src, values[:, 0:8], src, -3.0e38))
        g.dve.then(V.max(values[:, 8:16], src))
        g.dve.then(V.max_index(places[:, 8:16], values[:, 8:16], src))

    def activations():
        g.act.wait(norm_done)
        for j in range(KEYS):
            if j == late_j:
                while not topk_done:
                    yield
                g.dve_every = DVE_EVERY_ALONE
            b, out, m = g.fm_unit(("peer_u", j), h2T, KD)
            g.act.wait(m, list(topk_done) if j >= late_j else None)
            m = g.act.did(S.activation(experts[:, j, :], out, ACT.Gelu_apprx_tanh))
            b.free = [m]
            yield
        activations.mark = m

    g.run(activations(), [topk()])
    h2T_free = (g.pe.sem, g.pe.count)

    hot_free = [h2T_free] * HOTS
    g.dve.wait(activations.mark, topk_done)
    g.pool.wait(topk_done, g.base_ready)
    minus_key = g.place("minus_key", [P, TOKENS], at=hot_at + 4096 * HOTS)
    g.act.wait(topk_done, h2T_free)
    g.act.then(S.activation(minus_key[:, :], slot_T[:, 1, :], ACT.Copy, scale=-1.0))
    for n in range(TOKENS // G):
        fh, sh = first_hot[n % HOTS], second_hot[n % HOTS]
        g.pool.wait(hot_free[n % HOTS])
        t = n * G + G - 1
        g.pool.did(nc.gpsimd.tensor_scalar(fh[:, G - 1, :], g.iota, slot_T[:, 0, t:t + 1], slot_T[:, 2, t:t + 1],
                                           ALU.is_equal, ALU.mult))
        m2 = g.pool.did(nc.gpsimd.tensor_scalar(sh[:, G - 1, :], g.iota, slot_T[:, 1, t:t + 1], None, ALU.is_equal))
        g.act.wait(hot_free[n % HOTS])
        for k in range(G - 1):
            t = n * G + k
            m3 = g.act.did(S.activation(sh[:, k, :], g.iota, ACT.Abs, bias=minus_key[:, t:t + 1]))
        g.act.wait(m3)
        m3 = g.act.did(S.activation(sh[:, 0:G - 1, :], sh[:, 0:G - 1, :], ACT.Relu, scale=-1.0, bias=1.0))
        g.dve.wait(hot_free[n % HOTS])
        for k in range(G - 1):
            t = n * G + k
            m1 = g.dve.did(V.tensor_scalar(fh[:, k, :], g.iota, slot_T[:, 0, t:t + 1], slot_T[:, 2, t:t + 1],
                                           ALU.is_equal, ALU.mult))
        b = g.side_banks[n % 4]
        g.pe.wait(b.free, m1, m2, m3)
        for k in range(G):
            last = nc.tensor.matmul(b.t[:, k * P:(k + 1) * P], fh[:, k, :], sh[:, k, :], start=True, stop=True)
        m = g.pe.did(last)
        hot_free[n % HOTS] = m
        if n:
            apply_gates(g, experts, n - 1, G, gate_mark)
        gate_mark = m
    apply_gates(g, experts, TOKENS // G - 1, G, gate_mark)
    gated = (g.dve.sem, g.dve.count)

    gf = g.place("g_final", [P, D], at=g.addr(h2T.hi) + 8192)
    gf_ready = g.dma("g_final", gf[:, :], a["g_final"], gated, (g.pe.sem, g.pe.count))

    epair = [g.pair(f"expert_pair{i}", [P, TOKENS], at=g.addr(h2T.hi) + i * 2048).at(lambda t: t[:, :]) for i in range(3)]
    banks = [[g.side_banks[2 * t + h] for h in range(2)] for t in range(TILES)]
    free = [(g.pe.sem, g.pe.count)] * 3
    g.act.wait(gated)

    def split_expert(j):
        ep = epair[j % 3]
        ep.marks = g.split(ep, experts[:, j, :], None, free[j % 3], gated)

    split_expert(0)
    split_expert(1)
    for bb in banks:
        for b in bb:
            g.pe.wait(b.free)
    for j in range(KEYS):
        if j + 2 < KEYS:
            split_expert(j + 2)
        ep = epair[j % 3]
        n, w = g.take(("peer_v", j))
        g.pe.wait(ep.marks)
        for t in range(TILES):
            for h in range(2):
                last = g.mm3(banks[t][h].t[:, :], ep.at(lambda x: x[:, t * P:(t + 1) * P]),
                             w.at(lambda x: x[:, h * 512:(h + 1) * 512]), j == 0, j == KEYS - 1)
                if j == KEYS - 1:
                    g.bank_marks[t, h] = m = g.pe.did(last)
        if j < KEYS - 1:
            m = g.pe.did(last)
        g.used[n] = m
        free[j % 3] = m
    g.dve.wait(g.X_marks)
    marks = []
    for t in range(TILES):
        for h in range(2):
            g.dve.wait(g.bank_marks[t, h])
            mk = g.dve.did(V.tensor_tensor(g.X[:, t, h * 512:(h + 1) * 512], banks[t][h].t[:, :],
                                           g.X[:, t, h * 512:(h + 1) * 512], ALU.add))
            banks[t][h].free = [mk]
            marks.append(mk)
    g.X_marks = marks
    g.X_pieces = [((t, h), marks[t * 2 + h]) for t in range(TILES) for h in range(2)]

    g.junk = g.place("squares3", [P, TILES, D], at=ex)
    g.keep_warm()
    r = g.rstd_tm(g.X, g.X_pieces, "nl")
    g.dve.wait(gf_ready)
    marks = []
    g.X_pieces = []
    for t in range(TILES):
        for h in range(2):
            cols = slice(h * 512, (h + 1) * 512)
            marks.append(g.dve.did(V.scalar_tensor_tensor(g.X[:, t, cols], g.X[:, t, cols], r[:, t:t + 1],
                                                          gf[:, cols], ALU.mult, ALU.mult)))
            g.X_pieces.append(((t, h), marks[-1]))
    g.X_marks = marks


def apply_gates(g, experts, n, G, mark):
    b = g.side_banks[n % 4]
    view = experts[:, :, n * G:(n + 1) * G]
    g.dve.wait(mark)
    m = g.dve.did(g.nc.vector.tensor_tensor(view, view, b.t[:, :].rearrange("p (t j) -> p j t", t=G), ALU.mult))
    b.free = [m]




def bias_tables(g, bias, at, bias_marks):
    nc, a = g.nc, g.dram
    consts = g.place("bias_consts", [P, 2 * SKEW], at=at)
    rb = g.place("rel_bias", [P, SWA_HEADS], at=at + 8 * SKEW)
    rbw = g.place("rel_bias_wide", [P, SWA_HEADS, P], at=at + 8 * SKEW + 32)
    row = g.place("bias_rows", [P, SWA_HEADS, SKEW], at=at + 8 * SKEW + 32 + 4096)
    m1 = g.dma("bias_consts", consts[:, :], a["bias_consts"])
    m2 = g.dma("rel_bias", rb[0:BUCKETS, :], a["rel_bias"])
    for _ in range(4):
        yield
    g.dve.wait(m2)
    m = g.dve.did(nc.vector.tensor_copy(rbw[0:BUCKETS, :, :], wide(rb[0:BUCKETS, :], P)))
    yield
    for h in range(SWA_HEADS):
        b = g.side_banks[2 + h % 2]
        g.pe.wait(m, m1, b.free)
        mm = g.pe.did(nc.tensor.matmul(b.t[:, 0:SKEW], rbw[0:BUCKETS, h, :], consts[0:BUCKETS, 0:SKEW],
                                       start=True, stop=True))
        g.dve.wait(mm, m1)
        r = g.dve.did(nc.vector.tensor_tensor(row[:, h, :], b.t[:, 0:SKEW], consts[:, SKEW:], ALU.add))
        b.free = [r]
        yield
    scratch = nc.dram_tensor("bias_scratch", [SWA_HEADS * P * SKEW], F32, kind="Internal").ap()
    w = g.dma("bias_out", scratch.rearrange("(h p m) -> p h m", h=SWA_HEADS, p=P), row[:, :, :], r)
    for h in range(SWA_HEADS):
        start = h * P * SKEW + P - 1
        src = scratch[start:start + P * (SKEW - 1)].rearrange("(p m) -> p m", m=SKEW - 1)[:, 0:2 * P]
        ready = g.dma("bias_in", bias[:, h, :], src, w)
        yield
    g.act.wait(w)
    bias_marks.append(ready)


def layer(g, l, places, first_steps):
    nc, a = g.nc, g.dram
    V, S = nc.vector, nc.scalar
    (hT, ys, qk, v_r, ga, cu, cv, gu, gv, sq, sk, sv, gates, Sbuf, PT, t1, t2, y_tm, ws, lnb) = places["all"]
    cos, sin, swap, decay, tril, half_ones, bias = places["consts"]
    c_ready, bias_ready = places["ready"]
    name = lambda s: f"{s}.{l}"
    before = [(g.pe.sem, g.pe.count), (g.act.sem, g.act.count), (g.dve.sem, g.dve.count), (g.pool.sem, g.pool.count)]
    ws_ready = g.dma("ws", ws[:, :], a["gmlp_ws"][l], before)
    lnb_ready = g.dma("lnb", lnb[:, :], a["gmlp_ln"][l], before)
    bs_ready = g.dma("bs", places["bs"][0:1, :], a["gmlp_bs"][l:l + 1, :], before)
    bs = places["bs"]
    g.dve_every = DVE_EVERY_BESIDE_SIDE_WORK
    g.junk = places["junk"]
    g.norm_to_fm(g.X, g.X_pieces, name("norm1"), hT, name("n1"))
    g.pool.wait(ws_ready, c_ready, before)
    for i in range(4):
        ws_masked = g.pool.did(nc.gpsimd.tensor_tensor(ws[:, i * P:(i + 1) * P], ws[:, i * P:(i + 1) * P], tril, ALU.mult))
    g.dve.wait(before)
    pads = g.dve.did(V.memset(cu[:, :, 0:TAPS2 - 1], 0.0))
    marks = {}

    def to_sbuf(key, i, dst, rhs=hT, func=ACT.Copy, after=None, **kw):
        b, out, m = g.fm_unit((name(key), i), rhs, KD)
        g.act.wait(m, after)
        m = g.act.did(S.activation(dst, out, func, **kw))
        b.free = [m]
        marks[key, i] = m

    def tm_to_sbuf(key, dst, units, chunks, width):
        banks = [g.side_banks[0], g.side_banks[1]]
        for b in banks:
            g.pe.wait(b.free)
        for u in range(units):
            m = g.tm_unit((name(key), u), hT, u * chunks, chunks, width, [[b.t] for b in banks], u == 0, u == units - 1)
            if u < units - 1:
                yield
        g.act.wait(m)
        for t, b in enumerate(banks):
            e = g.act.did(S.activation(dst[:, t, :], b.t[:, 0:width], ACT.Copy))
            b.free = [e]
        marks[key] = e
        yield

    def main():
        for i in range(KM):
            to_sbuf("cg", i, cv[:, i, :], func=ACT.Tanh, scale=0.5)
            yield
        for i in range(KM):
            b, out, m = g.fm_unit((name("ca"), i), hT, KD)
            g.dve.wait(m, marks["cg", i], pads)
            m = g.dve.then(V.scalar_tensor_tensor(cu[:, i, TAPS2 - 1:], cv[:, i, :], 1.0, out, ALU.add, ALU.mult))
            b.free = [m]
            marks["cu", i] = g.dve.did(V.tensor_scalar(cu[:, i, TAPS2 - 1:], cu[:, i, TAPS2 - 1:], 0.5, None, ALU.mult))
            yield
        for i in range(8):
            to_sbuf("rqk", i, qk[:, i, :])
            yield
        yield from tm_to_sbuf("rv", v_r, 4, 2, 512)
        for i in range(4):
            to_sbuf("ga", i, ga[:, i, :])
            yield
        yield from tm_to_sbuf("gv", gv, 4, 2, 512)
        to_sbuf("sk", 0, sk[:, :])
        yield
        for i in range(4):
            to_sbuf("sq", i, sq[:, i, :])
            yield
        yield from tm_to_sbuf("sv", sv, 1, 8, 128)
        for i in range(4):
            to_sbuf("gu", i, gu[:, i, :])
            yield
        while not bias_ready:
            yield
        for i in range(32):
            to_sbuf("gate", i, gates[:, i, :], func=ACT.Tanh, scale=0.5)
            yield

    def take_bank(i):
        b = g.side_banks[i]
        g.pe.wait(b.free)
        return b

    def gelu2(key, dst, tmp, marks_):
        g.dve.wait(marks_)
        g.dve.then(V.tensor_tensor(tmp, dst, dst, ALU.mult))
        g.dve.then(V.tensor_scalar(tmp, tmp, 0.044715, 1.0, ALU.mult, ALU.add))
        m = g.dve.then(V.tensor_tensor(tmp, tmp, dst, ALU.mult))
        yield
        g.act.wait(m)
        m = g.act.did(S.activation(tmp, tmp, ACT.Tanh, scale=float(np.sqrt(2 / np.pi))))
        yield
        g.dve.wait(m)
        marks[key] = g.dve.then(V.scalar_tensor_tensor(dst, tmp, 1.0, dst, ALU.add, ALU.mult))

    def convolution():
        for i in range(KM):
            while ("cu", i) not in marks:
                yield
            g.dve.wait(marks["cu", i])
            w = lambda j: g.col(name("conv_w2"), j * KM + i)
            g.dve.then(V.tensor_scalar(cv[:, i, :], cu[:, i, 0:TOKENS], w(0), g.col(name("conv_b2"), i),
                                       ALU.mult, ALU.add))
            for j in range(1, TAPS2):
                m = g.dve.then(V.scalar_tensor_tensor(cv[:, i, :], cu[:, i, j:j + TOKENS], w(j), cv[:, i, :],
                                                      ALU.mult, ALU.add))
                if j % 4 == 0:
                    yield
            yield
        yield
        b = take_bank(4)
        g.pe.wait(m)
        for i in range(KM):
            last = nc.tensor.matmul(b.t[:, 0:TOKENS], g.ones, cv[:, i, :], start=(i == 0), stop=(i == KM - 1))
        mm = g.pe.did(last)
        yield
        g.dve.wait(mm)
        mean = t2[:, 0, :]
        g.dve.then(V.tensor_scalar(mean, b.t[:, 0:TOKENS], 1.0 / MIX, None, ALU.mult))
        for i in range(KM):
            m = g.dve.did(V.tensor_tensor(cv[:, i, :], cv[:, i, :], mean, ALU.subtract))
        yield
        g.act.wait(m)
        sqs = cu[:, :, 0:TOKENS]
        m = g.act.did(S.activation(sqs, cv[:, :, :], ACT.Square))
        yield
        g.pe.wait(m)
        for i in range(KM):
            last = nc.tensor.matmul(b.t[:, TOKENS:2 * TOKENS], g.ones, cu[:, i, 0:TOKENS], start=(i == 0),
                                    stop=(i == KM - 1))
        mm = g.pe.did(last)
        yield
        g.dve.wait(mm)
        var = t2[:, 1, :]
        m = g.dve.then(V.tensor_scalar(var, b.t[:, TOKENS:2 * TOKENS], 1.0 / MIX, EPS, ALU.mult, ALU.add))
        b.free = [m]
        marks["conv_stats"] = m
        yield
        g.act.wait(m)
        m = g.act.did(S.activation(var, var, ACT.Sqrt))
        yield
        g.dve.wait(m)
        g.dve.then(V.reciprocal(var, var))
        yield
        for i in range(KM):
            u, sg = cv[:, i, :], t2[:, 0, :]
            g.dve.then(V.tensor_tensor(u, u, var, ALU.mult))
            m = g.dve.then(V.tensor_scalar(u, u, g.col(name("cln_g"), i), g.col(name("cln_b"), i), ALU.mult, ALU.add))
            g.act.wait(m)
            m = g.act.did(S.activation(sg, u, ACT.Tanh, scale=0.5))
            g.dve.wait(m)
            m = g.dve.then(V.scalar_tensor_tensor(u, sg, 1.0, u, ALU.add, ALU.mult))
            ys.marks = g.split(ys.at(lambda t: t[:, 4 + i, :]), u, None, m, scale=0.5)
            yield

    def gating_norm():
        while "gv" not in marks:
            yield
        for t in range(TILES):
            v, tmp = gv[:, t, :], y_tm[:, 0, :]
            yield from gelu2(("gelu_v", t), v, tmp, marks["gv"])
            yield
            st, ag = g.small(name(f"gst{t}"), 6), g.small(name(f"gag{t}"), 2)
            g.dve.then(V.bn_stats(st, v))
            g.dve.then(V.bn_aggr(ag, st))
            m = g.dve.then(V.tensor_scalar(ag[:, 1:2], ag[:, 1:2], 0.25, EPS, ALU.mult, ALU.add))
            yield
            g.act.wait(m)
            m = g.act.did(S.activation(ag[:, 1:2], ag[:, 1:2], ACT.Sqrt, scale=4.0))
            yield
            g.dve.wait(m)
            g.dve.then(V.reciprocal(ag[:, 1:2], ag[:, 1:2]))
            m = g.dve.then(V.tensor_scalar(v, v, ag[:, 0:1], ag[:, 1:2], ALU.subtract, ALU.mult))
            yield
            g.pool.wait(m, lnb_ready)
            g.pool.then(nc.gpsimd.tensor_tensor(v, v, lnb[:, 0:MIX], ALU.mult))
            marks["gvn", t] = g.pool.did(nc.gpsimd.tensor_tensor(v, v, lnb[:, MIX:], ALU.add))
            yield

    def gating():
        while ("gu", KM - 1) not in marks or "conv_stats" not in marks:
            yield
        for i in range(KM):
            yield from gelu2(("gelu_u", i), gu[:, i, :], t1[:, 0, :], marks["gu", i])
            b = take_bank(4)
            g.pe.wait(marks["gvn", 0], marks["gvn", 1], ws_masked, bs_ready, g.base_ready)
            for t in range(TILES):
                out = b.t[:, t * P:(t + 1) * P]
                nc.tensor.matmul(out, gv[:, t, i * P:(i + 1) * P], ws[:, i * P:(i + 1) * P], start=True, stop=False)
                last = nc.tensor.matmul(out, g.ones[0:1, :], bs[0:1, i * P:(i + 1) * P], start=False, stop=True)
            mm = g.pe.did(last)
            u = gu[:, i, :]
            yield
            g.dve.wait(mm)
            m = g.dve.then(V.tensor_tensor(u, b.t[:, 0:TOKENS], u, ALU.mult))
            b.free = [m]
            ys.marks = g.split(ys.at(lambda t: t[:, 8 + i, :]), u, None, m, scale=0.5)
            yield

    def retention():
        due = None

        def add(c, m2):
            g.dve.wait(m2)
            marks["rot", c] = g.dve.then(V.tensor_tensor(qk[:, c, :], qk[:, c, :], g.rope_tmp, ALU.add))

        for c in range(8):
            while ("rqk", c) not in marks:
                yield
            if due:
                add(*due)
            b = take_bank(3)
            g.pe.wait(marks["rqk", c], c_ready)
            m = g.pe.did(nc.tensor.matmul(b.t[:, 0:TOKENS], swap, qk[:, c, :], start=True, stop=True))
            g.pool.wait(m, c_ready)
            m2 = g.pool.did(nc.gpsimd.tensor_tensor(qk[:, c, :], qk[:, c, :], cos, ALU.mult))
            g.dve.wait(m, c_ready)
            m3 = g.dve.then(V.tensor_tensor(g.rope_tmp, b.t[:, 0:TOKENS], sin, ALU.mult))
            b.free = [m3]
            due = (c, m2)
            yield
        add(*due)
        yield
        while "rv" not in marks:
            yield
        yield from pipeline([retention_head(h) for h in range(RET_HEADS)], 4)

    def retention_head(h):
        b = take_bank(2)
        g.pe.wait(marks["rot", h], marks["rot", 4 + h])
        nc.tensor.matmul(b.t[:, 0:TOKENS], qk[:, 4 + h, 0:P], qk[:, h, :], start=True, stop=True)
        last = nc.tensor.matmul(b.t[:, TOKENS:TOKENS + P], qk[:, 4 + h, P:], qk[:, h, P:], start=True, stop=True)
        mm = g.pe.did(last)
        scores = Sbuf[h % 2]
        g.dve.wait(mm, marks.get(("ret_y", h - 2)))
        g.dve.did(V.tensor_tensor(scores[:, 0:TOKENS], b.t[:, 0:TOKENS], decay[:, h, :], ALU.mult))
        m = g.dve.did(V.tensor_tensor(scores[:, TOKENS:TOKENS + P], b.t[:, TOKENS:TOKENS + P], decay[:, h, 0:P],
                                      ALU.mult))
        b.free = [m]
        yield
        yb = take_bank(3)
        g.pe.wait(m, marks["rv"])
        v = lambda t: v_r[:, t, h * P:(h + 1) * P]
        nc.tensor.matmul(yb.t[:, 0:P], scores[:, 0:P], v(0), start=True, stop=True)
        nc.tensor.matmul(yb.t[:, P:2 * P], scores[:, P:2 * P], v(0), start=True, stop=False)
        last = nc.tensor.matmul(yb.t[:, P:2 * P], scores[:, 2 * P:3 * P], v(1), start=False, stop=True)
        mm = marks["ret_y", h] = g.pe.did(last)
        yield
        g.dve.wait(mm)
        st, ag = g.small(name(f"rst{h}"), 6 * TILES), g.small(name(f"rag{h}"), 2 * TILES)
        for t in range(TILES):
            m = g.dve.did(V.bn_stats(st[:, 6 * t:6 * t + 6], yb.t[:, t * P:(t + 1) * P]))
        g.dve.wait(m)
        for t in range(TILES):
            m = g.dve.did(V.bn_aggr(ag[:, 2 * t:2 * t + 2], st[:, 6 * t:6 * t + 6]))
        g.dve.wait(m)
        var = ag.rearrange("p (t two) -> p t two", two=2)[:, :, 1]
        m = g.dve.then(V.tensor_scalar(var, var, EPS, None, ALU.add))
        yield
        g.act.wait(m)
        m = g.act.did(S.activation(var, var, ACT.Sqrt))
        yield
        g.dve.wait(m, marks.get(("yT", h - 1)))
        g.dve.then(V.reciprocal(var, var))
        for t in range(TILES):
            m = g.dve.did(V.tensor_scalar(g.ret_n[:, t, :], yb.t[:, t * P:(t + 1) * P], ag[:, 2 * t:2 * t + 1],
                                          ag[:, 2 * t + 1:2 * t + 2], ALU.subtract, ALU.mult))
        yb.free = [m]
        yield
        b = take_bank(2)
        g.pe.wait(m)
        for t in range(TILES):
            last = nc.tensor.transpose(b.t[:, t * P:(t + 1) * P], g.ret_n[:, t, :], g.ident)
        mm = marks["yT", h] = g.pe.did(last)
        while ("ga", h) not in marks:
            yield
        g.act.wait(marks["ga", h], marks.get("ret_out"))
        sg = g.ret_s
        m = g.act.did(S.activation(sg, ga[:, h, :], ACT.Tanh, scale=0.5))
        yield
        g.dve.wait(m, mm)
        g.dve.then(V.scalar_tensor_tensor(ga[:, h, :], sg, 1.0, ga[:, h, :], ALU.add, ALU.mult))
        m = g.dve.then(V.scalar_tensor_tensor(ga[:, h, :], b.t[:, 0:TOKENS], g.col(name("gn"), h), ga[:, h, :],
                                              ALU.mult, ALU.mult))
        marks["ret_out"] = m
        b.free = [m]
        ys.marks = g.split(ys.at(lambda t: t[:, h, :]), ga[:, h, :], None, m, scale=0.5)
        yield

    def swa_square_sum(i, x, mark):
        square = g.swa_t[:, i % 2, :]
        g.act.wait(mark, marks.get(("swa_sum", i - 2)))
        m = g.act.did(S.activation(square, x, ACT.Square))
        yield
        b = take_bank(i % 2)
        g.pe.wait(m, c_ready)
        m = marks["swa_sum", i] = g.pe.did(nc.tensor.matmul(b.t[:, 0:TOKENS], half_ones, square, start=True, stop=True))
        yield
        g.dve.wait(m)
        m = g.dve.did(V.tensor_scalar(g.swa_var[:, i, :], b.t[:, 0:TOKENS], 1.0 / SWA_DIM, EPS, ALU.mult, ALU.add))
        b.free = [m]
        marks["swa_var"] = m
        yield

    def swa_scale(i, key, x, gain):
        r = g.swa_var[:, i, :]
        g.dve.wait(marks["swa_root"])
        g.dve.then(V.reciprocal(r, r))
        marks[key] = g.dve.then(V.scalar_tensor_tensor(x, x, gain, r, ALU.mult, ALU.mult))

    S_free, PT_free = [[None], [None]], [None]

    def swa_head(i, c, half):
        h = c + 4 * half
        rows = slice(half * SWA_DIM, (half + 1) * SWA_DIM)
        segments = [(0, 0, P), (1, 0, TOKENS)]
        st = dict(bank=i % 2, turn_bank=2, out_bank=3, queries=TOKENS, scale=SWA_DIM ** -0.5, segments=segments,
                  S=Sbuf[i % 2], S_free=S_free[i % 2], PT=PT, PT_free=PT_free, mx=g.small(name(f"smx{i}"), 2),
                  den=g.small(name(f"sden{i}"), 2), es=g.small(name(f"ses{i}"), 2),
                  marks=[marks["sqn", c], marks["skn"]], q=lambda t: sq[rows, c, t * P:(t + 1) * P],
                  k=lambda k0, kn: sk[rows, k0:k0 + kn], v=lambda kt: sv[:, kt, :], v_marks=marks["sv"],
                  bias=lambda s: bias[:, h, P:2 * P] if s == 0 else bias[:, h, :], bias_ready=bias_ready,
                  sink=g.col(name("sinks2"), h))

        def done(bank, out, m):
            part = ys.at(lambda t: t[rows, 12 + c, :])
            ys.marks = g.split(part, out[rows, :], bank, m)

        st["done"] = done
        yield from softmax_head(g, st)

    def swa():
        while ("sk", 0) not in marks or ("sq", 3) not in marks:
            yield
        g.act.wait(marks["ret_out"], (g.pe.sem, g.pe.count))
        g.dve.wait((g.pe.sem, g.pe.count))
        yield from pipeline([swa_square_sum(0, sk[:, :], marks["sk", 0])] +
                            [swa_square_sum(1 + c, sq[:, c, :], marks["sq", c]) for c in range(4)])
        g.act.wait(marks["swa_var"])
        marks["swa_root"] = g.act.did(S.activation(g.swa_var[:, :, :], g.swa_var[:, :, :], ACT.Sqrt))
        yield
        swa_scale(0, "skn", sk[:, :], g.col(name("k_g")))
        yield

        def queries():
            for c in range(4):
                swa_scale(1 + c, ("sqn", c), sq[:, c, :], g.col(name("q_g")))
                yield

        while ("gvn", 1) not in marks:
            yield
        g.act.wait(marks["gvn", 0], marks["gvn", 1])
        yield from pipeline([queries()] + [swa_head(2 * c + half, c, half) for c in range(4) for half in range(2)])

    mix = Pair(hT.hi, hT.lo, [])
    mix.chunk_marks = []

    def branches():
        hT_free = (g.pe.sem, g.pe.count)
        for nth, n in enumerate(BRANCH_ORDER):
            while ("branch", n) not in marks:
                yield
            part = Pair(ys.hi[:, 4 * n:4 * n + 4, :], ys.lo[:, 4 * n:4 * n + 4, :], marks["branch", n])
            for i in range(0, KD, 2):
                b, out, mk = g.fm_unit((name("branch"), (n * KD + i) // 2), part, KM, outs=2)
                gate = gates[:, n * KD + i:n * KD + i + 2, :]
                g.dve.wait(mk)
                m = g.dve.then(V.scalar_tensor_tensor(gate, gate, 1.0, out.rearrange("p (a t) -> p a t", a=2),
                                                      ALU.add, ALU.mult))
                b.free = [m]
                if nth:
                    total = gates[:, BRANCH_ORDER[0] * KD + i:BRANCH_ORDER[0] * KD + i + 2, :]
                    m = g.dve.then(V.tensor_tensor(total, total, gate, ALU.add))
                if nth == BRANCHES2 - 1:
                    g.act.wait(hT_free)
                    ms = g.split(mix.at(lambda t: t[:, i:i + 2, :]), total, None, m, scale=0.5)
                    mix.chunk_marks += [ms, ms]
                yield

    def finished(n, steps):
        yield from steps
        marks["branch", n] = [(g.act.sem, g.act.count), (g.dve.sem, g.dve.count)]

    def sides():
        yield from finished(0, retention())
        yield from finished(3, swa())

    def own_channels():
        conv = finished(1, convolution())
        for _ in range(CONV_STEPS_FIRST):
            next(conv)
            yield
        yield from gating_norm()
        yield from conv
        yield from finished(2, gating())

    def main_and_branches():
        yield from main()
        yield from branches()

    g.run(main_and_branches(), [first_steps, own_channels(), sides()])
    g.dve_every = DVE_EVERY_ALONE
    project_out(g, name("w_out"), mix, g.X, [])

    tmp_free = [None, None]
    g.norm_to_fm(g.X, g.X_pieces, name("norm2"), hT, name("n2"))
    hidden = places["hidden"]
    hidden.chunk_marks = []
    g.act.wait(g.X_marks)
    g.stream_banks += g.side_banks[:4]
    for i in range(KF):
        b, out, m = g.fm_unit((name("gt"), i), hT, KD)
        g.act.wait(m, tmp_free[i % 2])
        sg = t1[:, i % 2, :]
        m = g.act.did(S.activation(sg, out, ACT.Tanh, scale=0.5))
        g.dve.wait(m)
        u = t2[:, i % 2, :]
        m = g.dve.then(V.scalar_tensor_tensor(u, sg, 1.0, out, ALU.add, ALU.mult))
        b.free = [m]
        b, out, m = g.fm_unit((name("up"), i), hT, KD)
        g.dve.wait(m)
        m = g.dve.then(V.tensor_tensor(u, u, out, ALU.mult))
        b.free = [m]
        ms = g.split(hidden.at(lambda t: t[:, i, :]), u, None, m, scale=0.5)
        hidden.chunk_marks.append(ms)
        tmp_free[i % 2] = ms[1]
    g.stream_banks = g.stream_banks[:3]
    banks = [[g.side_banks[2 * t + h] for h in range(2)] for t in range(TILES)]
    for bb in banks:
        for b in bb:
            g.pe.wait(b.free)
    for i in range(KF):
        m = g.tm_unit((name("ffn_out"), i), hidden, i, 1, 1024, [[b.t for b in bb] for bb in banks], i == 0, i == KF - 1)
    mk = []
    for t in range(TILES):
        for h in range(2):
            g.dve.wait(g.bank_marks[t, h])
            x = g.dve.did(V.tensor_tensor(g.X[:, t, h * 512:(h + 1) * 512], banks[t][h].t[:, :],
                                          g.X[:, t, h * 512:(h + 1) * 512], ALU.add))
            banks[t][h].free = [x]
            mk.append(x)
    g.X_marks = mk
    g.X_pieces = [((t, h), mk[t * 2 + h]) for t in range(TILES) for h in range(2)]


def layers(g, phase):
    a = g.dram
    g.top = phase
    n_consts = a["layer_consts"].shape[-1]
    lc = g.place("layer_consts", [P, n_consts])
    widths = {"ret_cos": TOKENS, "ret_sin": TOKENS, "swap2": P, "decay": RET_HEADS * TOKENS, "tril": P, "half_ones": P}
    at, c = 0, {}
    for n in LAYER_CONSTS:
        c[n] = lc[:, at:at + widths[n]]
        at += widths[n]
    bias = g.place("bias", [P, SWA_HEADS, 2 * P])
    hT = g.pair("hT2", [P, KD, TOKENS])
    t1, t2 = g.place("t1b", [P, 2, TOKENS]), g.place("t2b", [P, 2, TOKENS])
    overlay = g.top
    ys = g.pair("ys", [P, 16, TOKENS])
    qk = g.place("ret_qk", [P, 8, TOKENS])
    junk = g.place("squares4", [P, TILES, D], at=g.addr(qk))
    v_r = g.place("ret_v", [P, TILES, MIX])
    ga = g.place("ret_gate", [P, KM, TOKENS])
    cu = g.place("conv_in", [P, KM, TAPS2 - 1 + TOKENS])
    cv = g.place("conv_out", [P, KM, TOKENS])
    gu = g.place("gmlp_u", [P, KM, TOKENS])
    gv = g.place("gmlp_v", [P, TILES, MIX])
    sq = g.place("swa_q", [P, KM, TOKENS])
    sk = g.place("swa_k", [P, TOKENS])
    sv = g.place("swa_v", [P, TILES, P])
    gates = g.place("gates2", [P, 32, TOKENS])
    Sbuf = [g.place(f"S2{i}", [P, 384]) for i in range(2)]
    PT = g.place("PT2", [P, 512])
    g.rope_tmp = g.place("rope_tmp2", [P, TOKENS])[:, :]
    g.swa_t = g.place("swa_t", [P, 2, TOKENS])
    g.swa_var = g.place("swa_var", [P, 1 + KM, TOKENS], at=g.addr(qk))
    g.ret_n = g.place("ret_n", [P, TILES, P], at=g.addr(g.swa_t))
    g.ret_s = g.place("ret_s", [P, TOKENS], at=g.addr(g.swa_t) + 1024)[:, :]
    y_tm = g.place("gelu_tmp", [P, 1, MIX], at=g.addr(ys.lo) + 14 * 1024)
    lnb = g.place("gmlp_ln", [P, 2 * MIX], at=g.addr(ys.hi) + 12 * 1024)
    ws = g.place("gmlp_ws", [P, 4 * P])
    bs = g.place("gmlp_bs", [P, 4 * P])
    hidden = g.pair("hidden", [P, KF, TOKENS], at=overlay)
    assert overlay + 2 * 4 * KF * TOKENS <= g.addr(gates), "hidden must not reach"
    c_ready = g.dma("layer_consts", lc[:, :], a["layer_consts"])
    bias_ready = []
    bias_steps = bias_tables(g, bias, g.addr(gates), bias_ready)
    places = {"all": (hT, ys, qk, v_r, ga, cu, cv, gu, gv, sq, sk, sv, gates, Sbuf, PT, t1, t2, y_tm, ws, lnb),
              "consts": (c["ret_cos"], c["ret_sin"], c["swap2"],
                         c["decay"].rearrange("p (h t) -> p h t", h=RET_HEADS), c["tril"], c["half_ones"], bias),
              "ready": (c_ready, bias_ready), "bs": bs, "junk": junk, "hidden": hidden}
    small = g.small_at
    for l in range(LAYERS):
        layer(g, l, places, bias_steps if l == 0 else iter(()))
        g.small_at = small



SOURCES = (("km", "w_km"), ("vm", "w_vm"), ("va", "w_va"), ("xl", "w_xl"), ("qm", "w_qm"), ("qk", "w_qk"),
           ("gl", "w_gl"), ("gate", "w_gate"))


def stream_plan(a):
    plan = []

    def add(key, array):
        src = a[array]
        for i in range(src.shape[0]):
            plan.append(((key, i), src[i]))

    for key, array in SOURCES:
        add(key, array)
    for n in ("p_mem", "p_attn", "p_lru"):
        add(n, n)
    add("w_out", "w_out")
    add("peer_q", "peer_q")
    add("peer_u", "peer_u")
    add("peer_v", "peer_v")
    for l in range(LAYERS):
        for key in ("cg", "ca", "rqk", "rv", "ga", "gv", "sk", "sq", "sv", "gu", "gate"):
            add(f"{key}.{l}", f"{key}.{l}")
        for n in BRANCH_ORDER:
            for i in range(n * KD // 2, (n + 1) * KD // 2):
                plan.append(((f"branch.{l}", i), a[f"branch.{l}"][i]))
        add(f"w_out.{l}", f"w_out.{l}")
        for i in range(KF):
            plan.append(((f"gt.{l}", i), a[f"gt.{l}"][i]))
            plan.append(((f"up.{l}", i), a[f"up.{l}"][i]))
        add(f"ffn_out.{l}", f"ffn_out.{l}")
    return plan


def build(nc, a, out):
    g = Program(nc, a, out)
    cols = g.place("cols", [P, COLS_N])
    g.cols = cols
    base = g.place("base_consts", [P, 2 * P + 1])
    g.ident, g.iota, g.inv_freq = base[:, 0:P], base[:, P:2 * P], base[:, 2 * P:2 * P + 1]
    ones = g.place("ones", [P, P])
    g.warm = base[:, 0:2 * P]
    g.smalls = g.place("smalls", [P, 400])
    g.small_at = 0
    g.X = g.place("X", [P, TILES, D])
    g.diag, g.diag_free = g.place("diag_rms", [P, TILES, P]), None
    m = [g.dma("cols", cols[:, :], a["cols"]), g.dma("base_consts", base[:, :], a["base_consts"])]
    g.ones = ones[:, :]
    m.append(g.dve.did(nc.vector.memset(ones[:, :], 1.0)))
    g.base_ready = m
    g.start_stream(stream_plan(a))
    phase = (g.top + 31) // 32 * 32
    g.junk = None
    g.mix_phase = phase
    mixer(g, phase)
    g.barrier()
    peer(g, phase)
    g.barrier()
    layers(g, phase)
    for (t, h), m in g.X_pieces:
        cols = slice(h * 512, (h + 1) * 512)
        g.writes_out.append(g.dma("out", out[:, t, cols], g.X[:, t, cols], m))
    g.sp.wait(g.writes_out)




def lay_out(inp):
    n = {k: np.asarray(v) for k, v in inp.items()}
    d = {}
    c = shape_constants()
    d["base_consts"] = pack(c, BASE_CONSTS)
    d["mix_consts"] = pack(c, MIX_CONSTS)
    d["layer_consts"] = pack(c, LAYER_CONSTS)
    d["bias_consts"] = pack(c, BIAS_CONSTS)

    def tm(x):
        return np.ascontiguousarray(x[0].reshape(TILES, P, D).transpose(1, 0, 2))

    d["x"], d["mem"] = tm(n["x"]), tm(n["mem"])
    d["positions"] = np.ascontiguousarray(np.broadcast_to(n["positions"], (P, TOKENS)))
    w = n["w_in"][0]
    o = np.cumsum([0, 768, 256, 256, 768, 768, 512, 3072])
    cut = lambda i, j=None: w[:, o[i]:o[i + 1 if j is None else j]]
    d["w_qk"], d["w_va"], d["w_xl"], d["w_gl"] = fm_units(cut(0, 2)), tm_units(cut(2), 4, 256), fm_units(cut(3)), fm_units(cut(4))
    d["w_qm"], d["w_gate"] = fm_units(cut(5)), fm_units(cut(6))
    kv = n["w_mem_kv"][0]
    d["w_km"], d["w_vm"] = fm_units(kv[:, :512]), tm_units(kv[:, 512:], 2, 512)
    for k in ("p_attn", "p_lru"):
        d[k] = fm_units(n[k][0])
    d["p_mem"] = fm_unit_pairs(n["p_mem"][0])
    d["w_out"] = tm_units(n["w_out"][0], 2, 512)
    lw = np.stack([n["lru_wr"][0], n["lru_wi"][0]])
    d["lru_w"] = np.ascontiguousarray(lw.reshape(24, P, P).transpose(1, 0, 2).reshape(P, -1))
    d["peer_q"] = fm_units(n["w_peer_q"][0])
    d["sub_keys"] = np.ascontiguousarray(n["peer_sub_keys"][0].reshape(16, KEYS, P).transpose(2, 0, 1).reshape(P, -1))
    d["peer_u"] = np.ascontiguousarray(
        n["peer_u"][0].reshape(KEYS, KEYS, KD, P).transpose(1, 3, 2, 0).reshape(KEYS, P, KD * KEYS))
    d["peer_v"] = np.ascontiguousarray(n["peer_v"][0].reshape(KEYS, KEYS, D).transpose(1, 0, 2))
    d["g_final"] = np.ascontiguousarray(np.broadcast_to(n["g_final"], (P, D)))
    d["rel_bias"] = n["rel_bias_2"]

    def rows(x):
        return np.broadcast_to(x, (P,) + x.shape)

    parts = {"g_mix": columns(n["g_mix"]), "g_mem": columns(n["g_mem"]), "gate_b": columns(n["gate_b"]),
             "conv_w": columns(n["conv_w"]), "conv_b": columns(n["conv_b"]), "lru_br": columns(n["lru_br"]),
             "lru_bi": columns(n["lru_bi"]), "lam": columns(n["lru_lambda"]), "g_ffn": columns(n["g_ffn"]),
             "sink": rows(n["attn_sink"][0])}
    w_in, wb, wf = n["w_in_2"], n["w_branch_2"], n["w_ffn_in_2"]
    for l in range(LAYERS):
        o = np.cumsum([0, 1024, 512, 512, 512, 512, 512, 512, 512, 128, 128, 4096])
        w = w_in[l]
        cut = lambda i: w[:, o[i]:o[i + 1]]
        d[f"rqk.{l}"], d[f"rv.{l}"], d[f"ga.{l}"] = fm_units(cut(0)), tm_units(cut(1), 2, 512), fm_units(cut(2))
        d[f"ca.{l}"], d[f"cg.{l}"] = fm_units(cut(3)), fm_units(cut(4))
        d[f"gu.{l}"], d[f"gv.{l}"] = fm_units(cut(5)), tm_units(cut(6), 2, 512)
        d[f"sq.{l}"], d[f"sk.{l}"], d[f"sv.{l}"] = fm_units(swa_q_columns(cut(7))), fm_units(cut(8)), tm_units(cut(9), 8, 128)
        d[f"gate.{l}"] = fm_units(cut(10))
        b = wb[l].copy()
        b[3] = b[3].reshape(SWA_HEADS, SWA_DIM, D)[SWA_ORDER].reshape(MIX, D)
        d[f"branch.{l}"] = np.concatenate([fm_unit_pairs(b[i]) for i in range(BRANCHES2)])
        d[f"w_out.{l}"] = tm_units(n["w_out_2"][l], 2, 512)
        d[f"gt.{l}"], d[f"up.{l}"] = fm_units(wf[l][:, :D_FF]), fm_units(wf[l][:, D_FF:])
        d[f"ffn_out.{l}"] = np.ascontiguousarray(n["w_ffn_out_2"][l].reshape(KF, P, D))
        parts[f"norm1.{l}"], parts[f"norm2.{l}"] = columns(n["norm1_g_2"][l]), columns(n["norm2_g_2"][l])
        parts[f"gn.{l}"] = columns(n["ret_gn_g_2"][l])
        parts[f"conv_w2.{l}"] = columns(n["conv_w_2"][l, :, 0])
        parts[f"conv_b2.{l}"] = columns(n["conv_b_2"][l])
        parts[f"cln_g.{l}"], parts[f"cln_b.{l}"] = columns(n["conv_ln_g_2"][l]), columns(n["conv_ln_b_2"][l])
        parts[f"q_g.{l}"] = np.tile(n["swa_q_g_2"][l], 2)[:, None]
        parts[f"k_g.{l}"] = np.tile(n["swa_k_g_2"][l], 2)[:, None]
        parts[f"sinks2.{l}"] = rows(n["swa_sinks_2"][l])
    d["cols"] = np.ascontiguousarray(np.concatenate([parts[k] for k in COLS], axis=1))
    d["gmlp_ws"] = np.ascontiguousarray(n["gmlp_ws_2"].transpose(0, 3, 1, 2).reshape(LAYERS, P, -1))
    d["gmlp_bs"] = n["gmlp_bs_2"].reshape(LAYERS, -1)
    ln = np.concatenate([n["gmlp_ln_g_2"], n["gmlp_ln_b_2"]], axis=1)
    d["gmlp_ln"] = np.ascontiguousarray(np.broadcast_to(ln[:, None, :], (LAYERS, P, 2 * MIX)))
    return d


def kernel(**inputs):
    import concourse.bacc as _bacc
    from concourse.bass_utils import run_bass_kernel_spmd as _run

    nc = _bacc.Bacc("TRN2", target_bir_lowering=False, num_devices=1)
    arrays, args = {}, {}
    for name, x in lay_out(inputs).items():
        dram = "in_" + name.replace(".", "_") + "_dram"
        arrays[dram] = x
        args[name] = nc.dram_tensor(dram, x.shape, mybir.dt.from_np(x.dtype), kind="ExternalInput").ap()
    out = nc.dram_tensor("out_dram", (P, TILES, D), F32, kind="ExternalOutput").ap()
    build(nc, args, out)
    r = _run(nc, [arrays], core_ids=[0])
    got = r.results[0]["out_dram"]
    return np.ascontiguousarray(got.transpose(1, 0, 2)).reshape(1, TOKENS, D)
```
